# Optimizing a Trainium2 kernel written in Bass

```python
import jax, jax.numpy as jnp
from jax import lax
import numpy as np

D_MODEL = 1024
BATCH = 1
SEQ = 512
DEPTH = 1
DEC_BATCH = 8
DEC_SEQ = 16
PAST_LEN = 128

CHUNK = 64
Q_BLOCK = 128
N_MIXERS = 2
SB_HEADS = 16
SB_HEAD_DIM = D_MODEL // SB_HEADS
RW_HEAD_DIM = 64
RW_HEADS = D_MODEL // RW_HEAD_DIM
DECAY_LORA = 64
AAA_LORA = 64
GATE_LORA = 160
N_EXPERTS = 16
N_GROUPS = 4
EXPERTS_PER_GROUP = N_EXPERTS // N_GROUPS
TOP_K = 2
D_EXPERT = 512
NORM_EPS = 1e-6
LNX_EPS = 64e-5

kernel_name = 'hybrid_stickbreak_rwkv7_grouped_moe_stream_step'

def _rmsnorm(x, g):
    x32 = x.astype(jnp.float32)
    y = x32 * lax.rsqrt(jnp.mean(x32 * x32, axis=-1, keepdims=True) + NORM_EPS)
    return (y * g.astype(jnp.float32)).astype(x.dtype)

def _stick_breaking_attend(q, k, v, q_pos, k_pos):
    z = jnp.einsum('bqhd,bkhd->bhqk', q, k).astype(jnp.float32) * (SB_HEAD_DIM ** -0.5)
    visible = (k_pos[None, :] < q_pos[:, None])[None, None]
    log_beta = jax.nn.log_sigmoid(z)
    log_keep = jnp.where(visible, jax.nn.log_sigmoid(-z), 0.0)
    suffix = lax.cumsum(log_keep, axis=3, reverse=True)
    suffix = jnp.concatenate([suffix[..., 1:], jnp.zeros_like(suffix[..., :1])], axis=-1)
    weights = jnp.where(visible, jnp.exp(log_beta + suffix), 0.0)
    return jnp.einsum('bhqk,bkhd->bqhd', weights.astype(v.dtype), v)

def _stick_breaking_mixer(h, w_qkv, w_o, k_past, v_past):
    bsz, seq, _ = h.shape
    q, k, v = jnp.split(h @ w_qkv, 3, axis=-1)
    q = q.reshape(bsz, seq, SB_HEADS, SB_HEAD_DIM)
    k = k.reshape(bsz, seq, SB_HEADS, SB_HEAD_DIM)
    v = v.reshape(bsz, seq, SB_HEADS, SB_HEAD_DIM)
    if k_past is None:
        outs = []
        for b0 in range(0, seq, Q_BLOCK):
            b1 = min(b0 + Q_BLOCK, seq)
            outs.append(_stick_breaking_attend(q[:, b0:b1], k[:, :b1], v[:, :b1],
                                               jnp.arange(b0, b1), jnp.arange(b1)))
        o = jnp.concatenate(outs, axis=1)
    else:
        past = k_past.shape[1]
        keys = jnp.concatenate([k_past.astype(k.dtype), k], axis=1)
        vals = jnp.concatenate([v_past.astype(v.dtype), v], axis=1)
        o = _stick_breaking_attend(q, keys, vals, past + jnp.arange(seq), jnp.arange(past + seq))
    return o.reshape(bsz, seq, D_MODEL) @ w_o, k, v

def _rwkv7_scan(r, decay, k, v, a, b, s0):
    def step(state, inp):
        r_t, w_t, k_t, v_t, a_t, b_t = inp
        sa = jnp.einsum('bhij,bhj->bhi', state, a_t)
        state = (state * w_t[:, :, None, :] + sa[..., None] * b_t[:, :, None, :]
                 + v_t[..., None] * k_t[:, :, None, :])
        return state, jnp.einsum('bhij,bhj->bhi', state, r_t)
    xs = tuple(jnp.swapaxes(t, 0, 1) for t in (r, decay, k, v, a, b))
    state, ys = lax.scan(step, s0, xs)
    return jnp.swapaxes(ys, 0, 1), state

def _rwkv7_mixer(h, shift_prev, s0, p):
    bsz, seq, _ = h.shape
    f32 = jnp.float32
    heads = lambda t: t.astype(f32).reshape(bsz, seq, RW_HEADS, RW_HEAD_DIM)
    xx = jnp.concatenate([shift_prev.astype(h.dtype), h[:, :-1]], axis=1) - h
    xr, xw, xk, xv, xa, xg = [h + xx * p['rw_mu'][j] for j in range(6)]
    r = xr @ p['rw_w_r']
    k = xk @ p['rw_w_k']
    v = xv @ p['rw_w_v']
    w = -jax.nn.softplus(-(p['rw_w0'] + jnp.tanh(xw @ p['rw_w1']) @ p['rw_w2']).astype(f32)) - 0.5
    decay = jnp.exp(-jnp.exp(w))
    a = jax.nn.sigmoid((p['rw_a0'] + (xa @ p['rw_a1']) @ p['rw_a2']).astype(f32))
    g = jax.nn.sigmoid(xg @ p['rw_g1']) @ p['rw_g2']
    kk = heads(k * p['rw_k_k'])
    kk = kk / jnp.maximum(jnp.sqrt(jnp.sum(kk * kk, axis=-1, keepdims=True)), 1e-12)
    k = k.astype(f32) * (1.0 + (a - 1.0) * p['rw_k_a'].astype(f32))
    r_h, k_h, v_h, a_h = heads(r), heads(k), heads(v), heads(a)
    y, state = _rwkv7_scan(r_h, heads(decay), k_h, v_h, -kk, kk * a_h, s0.astype(f32))
    mu = jnp.mean(y, axis=-1, keepdims=True)
    var = jnp.mean(jnp.square(y - mu), axis=-1, keepdims=True)
    y = (y - mu) * lax.rsqrt(var + LNX_EPS)
    y = (y * p['rw_lnx_g'].astype(f32).reshape(RW_HEADS, RW_HEAD_DIM)
         + p['rw_lnx_b'].astype(f32).reshape(RW_HEADS, RW_HEAD_DIM))
    bonus = jnp.sum(r_h * k_h * p['rw_r_k'].astype(f32), axis=-1, keepdims=True) * v_h
    out = ((y + bonus).reshape(bsz, seq, D_MODEL).astype(h.dtype) * g) @ p['rw_w_o']
    return out, h[:, -1:], state

def _grouped_moe(h, router_w, router_bias, w_gate, w_up, w_down):
    bsz, seq, _ = h.shape
    t = h.reshape(-1, D_MODEL)
    s = jax.nn.sigmoid((t @ router_w).astype(jnp.float32))
    sel = (s + router_bias.astype(jnp.float32)).reshape(-1, N_GROUPS, EXPERTS_PER_GROUP)
    group_score = jnp.sum(lax.top_k(sel, TOP_K)[0], axis=-1)
    gidx = jnp.argmax(group_score, axis=-1)
    within = jnp.take_along_axis(sel, gidx[:, None, None], axis=1)[:, 0]
    _, loc = lax.top_k(within, TOP_K)
    eidx = gidx[:, None] * EXPERTS_PER_GROUP + loc
    wsel = jnp.take_along_axis(s, eidx, axis=-1)
    wsel = wsel / jnp.sum(wsel, axis=-1, keepdims=True)
    gates = jnp.sum(jax.nn.one_hot(eidx, N_EXPERTS, dtype=jnp.float32) * wsel[..., None], axis=1)
    gates = gates.astype(t.dtype)
    out = jnp.zeros_like(t)
    for e in range(N_EXPERTS):
        he = jax.nn.silu(t @ w_gate[e]) * (t @ w_up[e])
        out = out + gates[:, e:e + 1] * (he @ w_down[e])
    return out.reshape(bsz, seq, D_MODEL)

def _run_trunk(x, c, p, sb_k_past, sb_v_past, rw_shift0, rw_s0):
    sb_k = sb_v = rw_state = rw_shift = None
    for i in range(DEPTH):
        mod = (jax.nn.silu(c) @ p['ada_w'][i] + p['ada_b'][i])[:, None, :]
        sh1, sc1, g1, sh2, sc2, g2 = jnp.split(mod, 6, axis=-1)
        h = _rmsnorm(x, p['norm_mix_g'][i]) * (1 + sc1) + sh1
        if i % N_MIXERS == 0:
            mix, sb_k, sb_v = _stick_breaking_mixer(h, p['sb_w_qkv'], p['sb_w_o'], sb_k_past, sb_v_past)
        else:
            mix, rw_shift, rw_state = _rwkv7_mixer(h, rw_shift0, rw_s0, p)
        x = x + (g1 * mix).astype(x.dtype)
        h = _rmsnorm(x, p['norm_ffn_g'][i]) * (1 + sc2) + sh2
        ffn = _grouped_moe(h, p['router_w'], p['router_bias'],
                           p['exp_w_gate'][i], p['exp_w_up'][i], p['exp_w_down'][i])
        x = x + (g2 * ffn).astype(x.dtype)
    return _rmsnorm(x, p['final_norm_g']), sb_k, sb_v, rw_state, rw_shift

def setup_inputs(seed: int = 0) -> dict:
    key = jax.random.key(seed)
    ks = iter(jax.random.split(key, 48))
    f32 = jnp.float32
    nrm = lambda shape, scale: jax.random.normal(next(ks), shape, f32) * scale
    D = D_MODEL
    return {
        'x_prompt': nrm((BATCH, SEQ, D), 1.0),
        'x_sample': nrm((DEC_BATCH, DEC_SEQ, D), 1.0),
        'cache_sb_k': nrm((DEC_BATCH, PAST_LEN, SB_HEADS, SB_HEAD_DIM), 1.0),
        'cache_sb_v': nrm((DEC_BATCH, PAST_LEN, SB_HEADS, SB_HEAD_DIM), 1.0),
        'state_rw_wkv': nrm((DEC_BATCH, RW_HEADS, RW_HEAD_DIM, RW_HEAD_DIM), 0.5),
        'state_rw_shift': nrm((DEC_BATCH, 1, D), 1.0),
        'c_prompt': nrm((BATCH, D), 1.0),
        'c_sample': nrm((DEC_BATCH, D), 1.0),
        'ada_w': nrm((DEPTH, D, 6 * D), 0.5 * D ** -0.5),
        'ada_b': nrm((DEPTH, 6 * D), 0.02),
        'norm_mix_g': 1.0 + nrm((DEPTH, D), 0.02),
        'norm_ffn_g': 1.0 + nrm((DEPTH, D), 0.02),
        'final_norm_g': 1.0 + nrm((D,), 0.02),
        'sb_w_qkv': nrm((D, 3 * D), D ** -0.5),
        'sb_w_o': nrm((D, D), D ** -0.5),
        'rw_mu': jax.random.uniform(next(ks), (6, D), f32, 0.0, 1.0),
        'rw_w_r': nrm((D, D), D ** -0.5),
        'rw_w_k': nrm((D, D), D ** -0.5),
        'rw_w_v': nrm((D, D), D ** -0.5),
        'rw_w0': jax.random.uniform(next(ks), (D,), f32, -5.0, 0.0),
        'rw_w1': nrm((D, DECAY_LORA), D ** -0.5),
        'rw_w2': nrm((DECAY_LORA, D), 0.5 * DECAY_LORA ** -0.5),
        'rw_a0': nrm((D,), 0.3),
        'rw_a1': nrm((D, AAA_LORA), D ** -0.5),
        'rw_a2': nrm((AAA_LORA, D), 0.5 * AAA_LORA ** -0.5),
        'rw_g1': nrm((D, GATE_LORA), D ** -0.5),
        'rw_g2': nrm((GATE_LORA, D), GATE_LORA ** -0.5),
        'rw_k_k': 0.85 + nrm((D,), 0.02),
        'rw_k_a': 1.0 + nrm((D,), 0.02),
        'rw_r_k': nrm((RW_HEADS, RW_HEAD_DIM), 0.1),
        'rw_lnx_g': 1.0 + nrm((D,), 0.02),
        'rw_lnx_b': nrm((D,), 0.02),
        'rw_w_o': nrm((D, D), D ** -0.5),
        'router_w': nrm((D, N_EXPERTS), D ** -0.5),
        'router_bias': nrm((N_EXPERTS,), 0.01),
        'exp_w_gate': nrm((DEPTH, N_EXPERTS, D, D_EXPERT), D ** -0.5),
        'exp_w_up': nrm((DEPTH, N_EXPERTS, D, D_EXPERT), D ** -0.5),
        'exp_w_down': nrm((DEPTH, N_EXPERTS, D_EXPERT, D), D_EXPERT ** -0.5),
    }

def reference(x_prompt, x_sample, cache_sb_k, cache_sb_v, state_rw_wkv, state_rw_shift,
              c_prompt, c_sample, ada_w, ada_b, norm_mix_g, norm_ffn_g, final_norm_g,
              sb_w_qkv, sb_w_o, rw_mu, rw_w_r, rw_w_k, rw_w_v, rw_w0, rw_w1, rw_w2,
              rw_a0, rw_a1, rw_a2, rw_g1, rw_g2, rw_k_k, rw_k_a, rw_r_k, rw_lnx_g, rw_lnx_b,
              rw_w_o, router_w, router_bias, exp_w_gate, exp_w_up, exp_w_down):
    assert x_sample.shape[1] <= CHUNK
    p = {
        'ada_w': ada_w, 'ada_b': ada_b, 'norm_mix_g': norm_mix_g, 'norm_ffn_g': norm_ffn_g,
        'final_norm_g': final_norm_g, 'sb_w_qkv': sb_w_qkv, 'sb_w_o': sb_w_o,
        'rw_mu': rw_mu, 'rw_w_r': rw_w_r, 'rw_w_k': rw_w_k, 'rw_w_v': rw_w_v,
        'rw_w0': rw_w0, 'rw_w1': rw_w1, 'rw_w2': rw_w2, 'rw_a0': rw_a0, 'rw_a1': rw_a1,
        'rw_a2': rw_a2, 'rw_g1': rw_g1, 'rw_g2': rw_g2, 'rw_k_k': rw_k_k, 'rw_k_a': rw_k_a,
        'rw_r_k': rw_r_k, 'rw_lnx_g': rw_lnx_g, 'rw_lnx_b': rw_lnx_b, 'rw_w_o': rw_w_o,
        'router_w': router_w, 'router_bias': router_bias,
        'exp_w_gate': exp_w_gate, 'exp_w_up': exp_w_up, 'exp_w_down': exp_w_down,
    }
    bsz = x_prompt.shape[0]
    shift0 = jnp.zeros((bsz, 1, D_MODEL), x_prompt.dtype)
    s0 = jnp.zeros((bsz, RW_HEADS, RW_HEAD_DIM, RW_HEAD_DIM), jnp.float32)
    y_prompt, sb_k_prompt, sb_v_prompt, rw_wkv_prompt, rw_shift_prompt = _run_trunk(
        x_prompt, c_prompt, p, None, None, shift0, s0)
    y_sample, sb_k_sample, sb_v_sample, rw_wkv_sample, rw_shift_sample = _run_trunk(
        x_sample, c_sample, p, cache_sb_k, cache_sb_v, state_rw_shift, state_rw_wkv)
    return (y_prompt, y_sample, sb_k_prompt, sb_v_prompt, sb_k_sample, sb_v_sample,
            rw_wkv_prompt, rw_shift_prompt, rw_wkv_sample, rw_shift_sample)


_drawn_inputs = setup_inputs


def setup_inputs(seed=0):
    import zlib

    import numpy as np

    out = dict(_drawn_inputs(seed))
    spreads = {}
    factors = {'norm_mix_g': 3.01, 'final_norm_g': 2.883}
    for name, (base, spread) in spreads.items():
        noise = np.random.default_rng([zlib.crc32(name.encode()), seed]).standard_normal(out[name].shape)
        drawn = base * np.exp(spread * noise) if base else spread * noise
        out[name] = __import__('jax').numpy.asarray(drawn.astype(out[name].dtype))
    for name, factor in factors.items():
        out[name] = (out[name] * factor).astype(out[name].dtype)
    return out
```

```python
from contextlib import ExitStack

import concourse.bass as bass
from concourse import mybir

F32 = mybir.dt.float32
I32 = mybir.dt.int32
BF16 = mybir.dt.bfloat16
ALU = mybir.AluOpType
ACT = mybir.ActivationFunctionType
AX_X = mybir.AxisListType.X

P = 128
D = 1024
KD = D // P
SEQ = 512
NS = 8
SS = 16
NSAM = NS * SS
PAST = 128
TOK = SEQ + NSAM
NT = TOK // P
NTP = SEQ // P
NC = 1 + NS
H = 16
HD = 64
NPAIR = H // 2
CW = 32
NG4 = P // CW
ADW = 512
NE = 16
NGRP = 4
EPG = NE // NGRP
FE = 512
KF = FE // P
EPS = 1e-6
SCALE = HD ** -0.5


def stream_step(nc, io):
    with ExitStack() as ctx:
        build(nc, io, ctx)


def build(nc, io, ctx):
    def sb(name, shape, dt=F32, c=ctx):
        return c.enter_context(nc.sbuf_tensor(name, shape, dt))

    def sem(name):
        return ctx.enter_context(nc.semaphore(name))

    x_tok = sb("x_tok", [P, NT, D])
    h_T = sb("h_T", [P, KD, TOK])
    ident = sb("ident", [P, P])
    sum_sel = sb("sum_sel", [P, NC])
    sel_tok = sb("sel_tok", [P, 2, P])
    ones_row = sb("ones_row", [1, P])
    mod_T = sb("mod_T", [P, 2 * KD, NC])
    ada_bT = sb("ada_bT", [P, 6 * KD])
    norm_gT = sb("norm_gT", [P, 2 * KD])
    scale_T = sb("scale_T", [P, KD, NC])
    rstd = sb("rstd", [P, NT])
    eps1 = sb("eps1", [P, 1])
    zeros = sb("zeros", [P, 256])

    phase_a = ExitStack()
    o_T = sb("o_T", [P, NPAIR, TOK], c=phase_a)
    mod_rows = sb("mod_rows", [P, 8, ADW], c=phase_a)
    ada_w = sb("ada_w", [P, 3, KD, ADW], c=phase_a)
    w_pair = sb("w_pair", [P, 3, KD, P], c=phase_a)
    past_k = sb("past_k", [P, NS, P], c=phase_a)
    past_v = sb("past_v", [P, NS, P], c=phase_a)
    past_kT = sb("past_kT", [P, NS, P], c=phase_a)
    q_z = sb("q_z", [P, 2, TOK], c=phase_a)
    k_T = sb("k_T", [P, TOK], c=phase_a)
    v_T = sb("v_T", [P, TOK], c=phase_a)
    k_tok = sb("k_tok", [P, NT, P], c=phase_a)
    v_tok = sb("v_tok", [P, NT, P], c=phase_a)
    ntri = sb("ntri", [P, P], c=phase_a)
    nones = sb("nones", [P, P], c=phase_a)
    c_T = sb("c_T", [P, KD, CW], c=phase_a)
    ZC = 6 * 512
    ew_t = sb("ew_t", [P, ZC], c=phase_a)
    ew_sp = sb("ew_sp", [P, ZC], c=phase_a)
    ew_w = sb("ew_w", [P, ZC], c=phase_a)
    c_rows = mod_rows[:, 6:8, :].rearrange("p a n -> p (a n)")
    c_tmp = mod_rows[:, 4:6, :].rearrange("p a n -> p (a n)")
    in_rows = v_T[0:64, 0:P]
    xs = [ew_t[:, 0:1024], ew_t[:, 1024:2048], ew_t[:, 2048:3072], ew_sp[:, 0:1024], ew_sp[:, 1024:2048]]
    x_sq = ew_w[:, 0:1024]
    w_o = ada_w[:, 1:3, :, :].rearrange("p a k n -> p (a k n)").rearrange("p (k n) -> p k n", n=D)

    phase_a.close()

    MAX_SLOTS = NE + 2 * TOK // P - 1
    exp_w = sb("exp_w", [P, 2, 3 * 4096])
    gate2 = sb("gate2", [P, 2, D])
    std2 = sb("std2", [P, NT])
    ones_b = sb("ones_b", [P, P], BF16)
    before_b = sb("before_b", [P, P], BF16)
    chosen_b = sb("chosen_b", [P, NT, NE], BF16)
    router_w = sb("router_w", [P, KD, NE])
    router_b = sb("router_b", [P, NE])
    s_e = sb("s_e", [P, NT, NE])
    sel = sb("sel", [P, NT, NE])
    in_top = sb("in_top", [P, NT, NE])
    r_tmp = sb("r_tmp", [P, NT, NE])
    rows = sb("rows", [P, NT, NE])
    cmp4 = sb("cmp4", [P, NT * NGRP, EPG, EPG])
    g_score = sb("g_score", [P, NT, NGRP])
    g_rank = sb("g_rank", [P, NT, NGRP])
    tok1 = sb("tok1", [P, NT])
    row_f = sb("row_f", [P, NT, 2])
    row_i = sb("row_i", [P, NT, 2], I32)
    gates12 = sb("gates12", [P, NT, 2])
    slot_iota = sb("slot_iota", [P, MAX_SLOTS + 1], I32)
    iota_f = sb("iota_f", [P, MAX_SLOTS + 1])
    limits = sb("limits", [P, NT])
    count = sb("count", [P, NE])
    over = sb("over", [P, NE, NT])
    n_slots = sb("n_slots", [P, NE])
    ones_e = sb("ones_e", [P, NE])
    slot_end = sb("slot_end", [P, NE])
    base = sb("base", [P, NE])
    ended = sb("ended", [P, MAX_SLOTS + 1, NE])
    slot_f = sb("slot_f", [P, MAX_SLOTS + 2])
    slot_tab = sb("slot_tab", [P, MAX_SLOTS + 2], I32)
    sq_tmp = sb("sq_tmp", [P, D])
    tmp = sb("tmp", [P, D])
    phase_r = ExitStack()
    h2_tok = sb("h2_tok", [P, NT, D], c=phase_r)
    gate1 = sb("gate1", [P, 2, D], c=phase_r)
    shift2 = sb("shift2", [P, 2, D], c=phase_r)
    scale2 = sb("scale2", [P, 2, D], c=phase_r)
    phase_r.close()
    ada_b_row = h2_tok[0:1, 0:4, :].rearrange("p a n -> p (a n)")
    x_slot = sb("x_slot", [P, D])
    x_slotT = sb("x_slotT", [P, KD, P])
    sig = sb("sig", [P, FE])
    hid = sb("hid", [P, FE])
    hidT = sb("hidT", [P, KF, P])
    y_slot = sb("y_slot", [P, D])
    y_rows = exp_w[:, 0, 0:NT * 2 * D].rearrange("p (t r n) -> p t r n", r=2, n=D)
    g_fin = exp_w[:, 1, 0:D]
    g_ffn = tmp
    slots_in = nc.dram_tensor("slots_in", [(MAX_SLOTS + 1) * P, D], F32, kind="Internal").ap()
    slots_out = nc.dram_tensor("slots_out", [MAX_SLOTS * P, D], F32, kind="Internal").ap()

    z = ctx.enter_context(nc.psum_tensor("z", [P, ZC], F32))
    fill_ps = ctx.enter_context(nc.psum_tensor("fill_ps", [P, 2, 512], F32))

    def zb(b, a=0, e=512):
        return z[:, 512 * b + a:512 * b + e]

    def blocks_of(buf, first, step, n):
        lo = first - first % step
        return buf[:, lo:lo + step * n].rearrange("p (n c) -> p n c", c=step)[:, :, first % step:first % step + P]

    ada_v = io["ada_w"].rearrange("o (k p) n -> p (o k) n", p=P)
    qkv_v = io["sb_w_qkv"].rearrange("(k p) n -> p k n", p=P)
    ck_v = io["cache_sb_k"].rearrange("s k h d -> k s (h d)")
    cv_v = io["cache_sb_v"].rearrange("s k h d -> k s (h d)")
    wo_v = io["sb_w_o"].rearrange("(k p) n -> p k n", p=P)
    xp_v = io["x_prompt"].rearrange("b (t p) d -> p (b t) d", p=P)
    xs_v = io["x_sample"].rearrange("b s d -> (b s) d")
    kp_v = io["k_prompt"].rearrange("b (t p) h d -> p (b t) (h d)", p=P)
    vp_v = io["v_prompt"].rearrange("b (t p) h d -> p (b t) (h d)", p=P)
    ks_v = io["k_sample"].rearrange("b s h d -> (b s) (h d)")
    vs_v = io["v_sample"].rearrange("b s h d -> (b s) (h d)")
    yp_v = io["y_prompt"].rearrange("b (t p) d -> p (b t) d", p=P)
    ys_v = io["y_sample"].rearrange("b s d -> (b s) d")

    c_loaded = sem("c_loaded")
    x_loaded = sem("x_loaded")
    ada_loaded = [sem(f"ada_loaded{i}") for i in range(3)]
    wqkv_loaded = [sem(f"w{c}_loaded") for c in "qkv"]
    past_k_loaded = sem("past_k_loaded")
    past_v_loaded = sem("past_v_loaded")
    wo_loaded = sem("wo_loaded")
    kv_stored = sem("kv_stored")
    y_stored = sem("y_stored")
    consts_set = sem("consts_set")
    small_dve = sem("small_dve")
    small_act = sem("small_act")
    silu_exp = sem("silu_exp")
    silu_ready = sem("silu_ready")
    setup_T = sem("setup_T")
    setup_T_used = sem("setup_T_used")
    sq_ready = sem("sq_ready")
    std_ready = sem("std_ready")
    rstd_ready = sem("rstd_ready")
    xs_ready = sem("xs_ready")
    xsT_ready = sem("xsT_ready")
    hT_ready = sem("hT_ready")
    modT_ready = sem("modT_ready")
    mod_T_mm = sem("mod_T_mm")
    ada_mm = sem("ada_mm")
    ada_kept = sem("ada_kept")
    z_ready = sem("z_ready")
    fill_ready = sem("fill_ready")
    fill_kept = sem("fill_kept")
    abs_ready = sem("abs_ready")
    exp_ready = sem("exp_ready")
    ln_ready = sem("ln_ready")
    sp_ready = sem("sp_ready")
    sp_masked = sem("sp_masked")
    keep_sum = sem("keep_sum")
    logw_ready = sem("logw_ready")
    w_ready = sem("w_ready")
    w_masked = sem("w_masked")
    o_ready = sem("o_ready")
    o_kept = sem("o_kept")
    rows_loaded = sem("rows_loaded")
    exp_loaded = [sem(f"{c}_loaded") for c in ("gate", "up", "down")]
    x_slot_loaded = sem("x_slot_loaded")
    y_slot_stored = sem("y_slot_stored")
    zeros_stored = sem("zeros_stored")
    consts_b = sem("consts_b")
    scattered = sem("scattered")
    gathered = [sem(f"gathered{t}") for t in range(NT)]
    pair_fill = sem("pair_fill")
    pair_kept = sem("pair_kept")
    x1_ready = sem("x1_ready")
    std2_ready = sem("std2_ready")
    std3_ready = sem("std3_ready")
    h2_ready = sem("h2_ready")
    h2T_mm = sem("h2T_mm")
    h2T_kept = sem("h2T_kept")
    logits_ready = sem("logits_ready")
    sig_exp = sem("sig_exp")
    route_step = sem("route_step")
    chosen_ready = sem("chosen_ready")
    places_mm = sem("places_mm")
    rows_known = sem("rows_known")
    slots_known = sem("slots_known")
    x_slotT_mm = sem("x_slotT_mm")
    x_slotT_kept = sem("x_slotT_kept")
    gate_ready = sem("gate_ready")
    up_ready = sem("up_ready")
    gate_exp = sem("gate_exp")
    sig_step = sem("sig_step")
    hid_ready = sem("hid_ready")
    hidT_mm = sem("hidT_mm")
    hidT_kept = sem("hidT_kept")
    down_ready = sem("down_ready")
    y_slot_kept = sem("y_slot_kept")
    y1_ready = sem("y1_ready")
    x2_ready = sem("x2_ready")
    y_ready = sem("y_ready")

    def phase_b_sync(sp):
        sp.wait_ge(ada_mm, 4 + NPAIR)
        sp.wait_ge(kv_stored, 64 * NPAIR)
        sp.dma_start(g_ffn[:, :], io["norm_ffn_g"].to_broadcast([P, D])).then_inc(rows_loaded, 16)
        sp.dma_start(ada_b_row, io["ada_b"][0:1, 2 * D:6 * D]).then_inc(rows_loaded, 16)
        sp.dma_start(router_w[:, :, :], io["router_w"].rearrange("(k p) e -> p k e", p=P)).then_inc(rows_loaded, 16)
        sp.dma_start(router_b[:, :], io["router_bias"].unsqueeze(0).to_broadcast([P, NE])).then_inc(rows_loaded, 16)
        sp.wait_ge(pair_fill, 8 + NT)
        load_expert(sp, 0, 0, None)
        sp.wait_ge(scattered, 16 * 2 * NT)
        sp.dma_start(x_slot[:, :], slots_in[0:P, :]).then_inc(x_slot_loaded, 16)
        sp.wait_ge(slots_known, 1)
        n = sp.value_load(slot_tab[0:1, MAX_SLOTS + 1:MAX_SLOTS + 2], min_val=NE, max_val=MAX_SLOTS)
        with sp.Fori(0, n) as j:
            e_now = sp.value_load(slot_tab[0:1, bass.ds(j, 1)], min_val=0, max_val=NE - 1)
            e_next = sp.value_load(slot_tab[0:1, bass.ds(j + 1, 1)], min_val=0, max_val=NE - 1)
            sp.wait_ge(down_ready, j)
            sp.nop(nofuse=True)
            for i in range(3):
                sp.wait_ge(exp_loaded[i], 16 * (j + 1))
            sp.nop(nofuse=True)
            load_expert(sp, e_next, e_next % 2, e_next != e_now)
            sp.wait_ge(x_slotT_mm, j + 1)
            sp.dma_start(x_slot[:, :], slots_in[bass.ds((j + 1) * P, P), :]).then_inc(x_slot_loaded, 16)
            sp.wait_ge(y_slot_kept, j + 1)
            sp.dma_start(slots_out[bass.ds(j * P, P), :], y_slot[:, :]).then_inc(y_slot_stored, 16)
        sp.wait_ge(x_slot_loaded, 16 * (n + 1))
        for i in range(3):
            sp.wait_ge(exp_loaded[i], 16 * (n + 1))
        sp.nop(nofuse=True)
        sp.dma_start(g_fin, io["final_norm_g"].unsqueeze(0).to_broadcast([P, D])).then_inc(rows_loaded, 16)
        for t in range(NT):
            sp.wait_ge(y_ready, t + 1)
            dst = yp_v[:, t, :] if t < NTP else ys_v
            sp.dma_start(dst, y_rows[:, t, 0, :]).then_inc(y_stored, 16)
        sp.wait_ge(y_stored, 16 * NT)

    def load_expert(sp, e, b, cond):
        more = {} if cond is None else {"cond": cond}
        for i, (name, view) in enumerate((("exp_w_gate", expert_view), ("exp_w_up", expert_view), ("exp_w_down", expert_view))):
            dst = exp_w[:, bass.ds(b, 1), i * 4096:(i + 1) * 4096].rearrange("p b (k f) -> p b k f", f=(FE, FE, D)[i])
            sp.dma_start(dst, view(name, e), **more).then_inc(exp_loaded[i], 16)

    def expert_view(name, e):
        return io[name][0].rearrange("e (k p) f -> p e k f", p=P)[:, bass.ds(e, 1)]

    def phase_b_pool(pool):
        pool.wait_ge(ada_mm, 4 + NPAIR)
        pool.memset(ones_b[:, :], 1.0).then_inc(consts_b, 1)
        pool.memset(before_b[:, :], 1.0).then_inc(consts_b, 1)
        pool.memset(ones_e[:, :], 1.0).then_inc(consts_b, 1)
        pool.memset(cmp4[:, :, :, :], 0.0).then_inc(consts_b, 1)
        pool.iota(slot_iota[:, :], pattern=[[1, MAX_SLOTS + 1]], base=0, channel_multiplier=0).then_inc(consts_b, 1)
        pool.wait_ge(consts_b, 5)
        pool.affine_select(out=before_b[:, :], in_=before_b[:, :], compare_op=ALU.is_gt, fill=0.0, base=0,
                           pattern=[[1, P]], channel_multiplier=-1).then_inc(consts_b, 1)
        pool.wait_ge(zeros_stored, 32)
        pool.wait_ge(rows_known, 1)
        for t in range(NT):
            for r in range(2):
                pool.indirect_dma_start(out=slots_in[:, :], out_offset=bass.IndirectOffsetOnAxis(ap=row_i[:, t, r:r + 1], axis=0),
                                        in_=h2_tok[:, t, :], in_offset=None).then_inc(scattered, 16)
        pool.wait_ge(slots_known, 1)
        n = pool.value_load(slot_tab[0:1, MAX_SLOTS + 1:MAX_SLOTS + 2], min_val=NE, max_val=MAX_SLOTS)
        pool.wait_ge(y_slot_stored, n * 16)
        pool.nop(nofuse=True)
        for t in range(NT):
            for r in range(2):
                pool.indirect_dma_start(out=y_rows[:, t, r, :], out_offset=None, in_=slots_out[:, :],
                                        in_offset=bass.IndirectOffsetOnAxis(ap=row_i[:, t, r:r + 1], axis=0)).then_inc(gathered[t], 16)

    def rms(act, src, dst, done, count):
        act.activation(sq_tmp[:, :], src, ACT.Square, accum_out=dst).then_inc(sq_ready, 1)
        act.wait_ge(sq_ready, count)
        act.activation(dst, dst, ACT.Sqrt, scale=1.0 / D, bias=eps1[:, 0:1]).then_inc(done, 1)

    def phase_b_act(act):
        for t in range(NT):
            act.wait_ge(x1_ready, t + 1)
            rms(act, x_tok[:, t, :], std2[:, t:t + 1], std2_ready, NT + t + 1)
        act.wait_ge(logits_ready, NT)
        act.activation(s_e[:, :, :], fill_ps[:, 0, 0:NT * NE].rearrange("p (t e) -> p t e", e=NE), ACT.Exp,
                       scale=-1.0).then_inc(sig_exp, 1)
        act.wait_ge(slots_known, 1)
        n = act.value_load(slot_tab[0:1, MAX_SLOTS + 1:MAX_SLOTS + 2], min_val=NE, max_val=MAX_SLOTS)
        with act.Fori(0, n) as j:
            act.wait_ge(gate_ready, j + 1)
            act.activation(sig[:, :], zb(0), ACT.Exp, scale=-1.0).then_inc(gate_exp, 1)
            act.wait_ge(down_ready, j + 1)
            act.wait_ge(y_slot_stored, 16 * j)
            act.activation(y_slot[:, :], z[:, 1024:2048], ACT.Copy).then_inc(y_slot_kept, 1)
        for t in range(NT):
            act.wait_ge(gathered[t], 32)
            act.activation(y_rows[:, t, 0, :], y_rows[:, t, 0, :], ACT.Copy, scale=gates12[:, t, 0:1]).then_inc(y1_ready, 1)
            if t:
                act.wait_ge(x2_ready, t)
                rms(act, x_tok[:, t - 1, :], std2[:, t - 1:t], std3_ready, 2 * NT + t)
        act.wait_ge(x2_ready, NT)
        rms(act, x_tok[:, NT - 1, :], std2[:, NT - 1:NT], std3_ready, 3 * NT)

    def phase_b_dve(dve):
        n_step = [0]

        def step(ins):
            n_step[0] += 1
            ins.then_inc(route_step, 1)
            dve.wait_ge(route_step, n_step[0])

        dve.wait_ge(consts_b, 6)
        dve.wait_ge(rows_loaded, 64)
        for r in range(8):
            kind, part = r // 2, r % 2
            dve.wait_ge(pair_fill, r + 1)
            if kind == 2:
                dve.scalar_tensor_tensor(out=scale2[:, part, :], in0=pair_ps(r), scalar=1.0, in1=g_ffn[:, :],
                                         op0=ALU.add, op1=ALU.mult).then_inc(pair_kept, 1)
            else:
                dst = {0: gate1, 1: shift2, 3: gate2}[kind]
                dve.tensor_copy(dst[:, part, :], pair_ps(r)).then_inc(pair_kept, 1)
        for t in range(NT + 2):
            if t < NT:
                part = t // NTP
                dve.wait_ge(pair_fill, 8 + t + 1)
                if t == 0:
                    dve.wait_ge(pair_kept, 8)
                else:
                    dve.wait_ge(x1_ready, t)
                dve.tensor_tensor(tmp[:, :], proj_ps(t), gate1[:, part, :], ALU.mult).then_inc(pair_kept, 1)
                dve.wait_ge(pair_kept, 9 + t)
                dve.tensor_tensor(x_tok[:, t, :], x_tok[:, t, :], tmp[:, :], ALU.add).then_inc(x1_ready, 1)
            if 1 <= t <= NT:
                u = t - 1
                part = u // NTP
                dve.wait_ge(std2_ready, u + 1)
                step(dve.reciprocal(rstd[:, u:u + 1], std2[:, u:u + 1]))
                step(dve.scalar_tensor_tensor(out=h2_tok[:, u, :], in0=x_tok[:, u, :], scalar=rstd[:, u:u + 1],
                                              in1=scale2[:, part, :], op0=ALU.mult, op1=ALU.mult))
                dve.tensor_tensor(h2_tok[:, u, :], h2_tok[:, u, :], shift2[:, part, :], ALU.add).then_inc(h2_ready, 1)
            if t >= 2:
                u = t - 2
                dve.wait_ge(h2T_mm, u + 1)
                dve.tensor_copy(h_T[:, :, u * P:(u + 1) * P],
                                z[:, 2048:3072].rearrange("p (k c) -> p k c", c=P)).then_inc(h2T_kept, 1)
        dve.wait_ge(sig_exp, 1)
        step(dve.tensor_scalar_add(s_e[:, :, :], s_e[:, :, :], 1.0))
        step(dve.reciprocal(s_e[:, :, :], s_e[:, :, :]))
        step(dve.tensor_tensor(sel[:, :, :], s_e[:, :, :], router_b[:, :].unsqueeze(1).to_broadcast([P, NT, NE]), ALU.add))

        def ranks(v, n, out):
            for j in range(EPG):
                for lo, hi, op in ((0, j, ALU.is_gt), (j + 1, EPG, ALU.is_ge)):
                    if hi > lo:
                        ins = dve.tensor_tensor(cmp4[:, 0:n, lo:hi, j], v[:, :, j:j + 1].to_broadcast([P, n, hi - lo]),
                                                v[:, :, lo:hi], op)
            step(ins)
            step(dve.tensor_reduce(out, cmp4[:, 0:n], AX_X, ALU.add))

        sel4 = sel[:, :, :].rearrange("p t (g i) -> p (t g) i", i=EPG)
        in_top4 = in_top[:, :, :].rearrange("p t (g i) -> p (t g) i", i=EPG)
        tmp4 = r_tmp[:, :, :].rearrange("p t (g i) -> p (t g) i", i=EPG)
        ranks(sel4, NT * NGRP, in_top4)
        step(dve.tensor_scalar(in_top[:, :, :], in_top[:, :, :], 2.0, None, ALU.is_lt))
        step(dve.tensor_tensor(r_tmp[:, :, :], sel[:, :, :], in_top[:, :, :], ALU.mult))
        step(dve.tensor_reduce(g_score[:, :, :].rearrange("p t g -> p (t g)"), tmp4, AX_X, ALU.add))
        ranks(g_score[:, :, :], NT, g_rank[:, :, :])
        step(dve.tensor_scalar(g_rank[:, :, :], g_rank[:, :, :], 1.0, None, ALU.is_lt))
        step(dve.tensor_tensor(in_top4, in_top4,
                               g_rank[:, :, :].rearrange("p t g -> p (t g)").unsqueeze(2).to_broadcast([P, NT * NGRP, EPG]),
                               ALU.mult))
        dve.tensor_copy(chosen_b[:, :, :], in_top[:, :, :]).then_inc(chosen_ready, 1)
        step(dve.tensor_tensor(s_e[:, :, :], s_e[:, :, :], in_top[:, :, :], ALU.mult))
        step(dve.tensor_reduce(tok1[:, :], s_e[:, :, :], AX_X, ALU.add))
        step(dve.reciprocal(tok1[:, :], tok1[:, :]))
        step(dve.tensor_tensor(s_e[:, :, :], s_e[:, :, :], tok1[:, :].unsqueeze(2).to_broadcast([P, NT, NE]), ALU.mult))
        step(dve.tensor_copy(iota_f[:, :], slot_iota[:, :]))
        step(dve.tensor_scalar(limits[:, :], iota_f[:, 0:NT], float(P), None, ALU.mult))
        dve.wait_ge(places_mm, 1)
        step(dve.tensor_copy(count[:, :], fill_ps[:, 1, NT * NE:(NT + 1) * NE]))
        step(dve.tensor_tensor(over[:, :, :], count[:, :].unsqueeze(2).to_broadcast([P, NE, NT]),
                               limits[:, :].unsqueeze(1).to_broadcast([P, NE, NT]), ALU.is_gt))
        step(dve.tensor_reduce(n_slots[:, :], over[:, :, :], AX_X, ALU.add))
        step(dve.tensor_scalar(n_slots[:, :], n_slots[:, :], 1.0, None, ALU.max))
        step(dve.tensor_tensor_scan(slot_end[:, :], ones_e[:, :], n_slots[:, :], 0.0, ALU.mult, ALU.add))
        step(dve.tensor_tensor(base[:, :], slot_end[:, :], n_slots[:, :], ALU.subtract))
        step(dve.tensor_scalar(base[:, :], base[:, :], float(P), None, ALU.mult))
        step(dve.tensor_tensor(rows[:, :, :], fill_ps[:, 1, 0:NT * NE].rearrange("p (t e) -> p t e", e=NE),
                               base[:, :].unsqueeze(1).to_broadcast([P, NT, NE]), ALU.add))
        step(dve.tensor_tensor(rows[:, :, :], rows[:, :, :], in_top[:, :, :], ALU.mult))
        step(dve.tensor_reduce(row_f[:, :, 1], rows[:, :, :], AX_X, ALU.max))
        step(dve.tensor_scalar(r_tmp[:, :, :], in_top[:, :, :], -8192.0, 8192.0, ALU.mult, ALU.add))
        step(dve.tensor_tensor(sel[:, :, :], rows[:, :, :], r_tmp[:, :, :], ALU.add))
        step(dve.tensor_reduce(row_f[:, :, 0], sel[:, :, :], AX_X, ALU.min))
        dve.tensor_copy(row_i[:, :, :], row_f[:, :, :]).then_inc(rows_known, 1)
        step(dve.tensor_tensor(ended[:, :, :], iota_f[:, :].unsqueeze(2).to_broadcast([P, MAX_SLOTS + 1, NE]),
                               slot_end[:, :].unsqueeze(1).to_broadcast([P, MAX_SLOTS + 1, NE]), ALU.is_ge))
        step(dve.tensor_reduce(slot_f[:, 0:MAX_SLOTS + 1], ended[:, :, :], AX_X, ALU.add))
        step(dve.tensor_scalar(slot_f[:, 0:MAX_SLOTS + 1], slot_f[:, 0:MAX_SLOTS + 1], float(NE - 1), None, ALU.min))
        step(dve.tensor_copy(slot_f[:, MAX_SLOTS + 1:MAX_SLOTS + 2], slot_end[:, NE - 1:NE]))
        dve.tensor_copy(slot_tab[:, :], slot_f[:, :]).then_inc(slots_known, 1)
        for r, src in ((0, sel), (1, rows)):
            step(dve.tensor_tensor(r_tmp[:, :, :], src[:, :, :], row_f[:, :, r:r + 1].to_broadcast([P, NT, NE]), ALU.is_equal))
            step(dve.tensor_tensor(r_tmp[:, :, :], r_tmp[:, :, :], s_e[:, :, :], ALU.mult))
            step(dve.tensor_reduce(gates12[:, :, r], r_tmp[:, :, :], AX_X, ALU.add))

        dve.wait_ge(slots_known, 1)
        n = dve.value_load(slot_tab[0:1, MAX_SLOTS + 1:MAX_SLOTS + 2], min_val=NE, max_val=MAX_SLOTS)

        def keep_slotT(j):
            dve.wait_ge(x_slotT_mm, j + 1)
            dve.tensor_copy(x_slotT[:, :, :], z[:, 2048:3072].rearrange("p (k c) -> p k c", c=P)).then_inc(x_slotT_kept, 1)

        dve.wait_ge(scattered, 16 * 2 * NT)
        keep_slotT(0)
        with dve.Fori(0, n) as j:
            dve.wait_ge(gate_exp, j + 1)
            dve.tensor_scalar_add(sig[:, :], sig[:, :], 1.0).then_inc(sig_step, 1)
            dve.wait_ge(sig_step, 3 * j + 1)
            dve.reciprocal(sig[:, :], sig[:, :]).then_inc(sig_step, 1)
            dve.wait_ge(sig_step, 3 * j + 2)
            dve.tensor_tensor(sig[:, :], sig[:, :], zb(0), ALU.mult).then_inc(sig_step, 1)
            dve.wait_ge(sig_step, 3 * j + 3)
            dve.wait_ge(up_ready, j + 1)
            dve.tensor_tensor(hid[:, :], sig[:, :], zb(1), ALU.mult).then_inc(hid_ready, 1)
            keep_slotT(j + 1)
            dve.wait_ge(hidT_mm, j + 1)
            dve.tensor_copy(hidT[:, :, :], fill_ps[:, 0, :].rearrange("p (k c) -> p k c", c=P)).then_inc(hidT_kept, 1)

        dve.wait_ge(rows_loaded, 80)
        for t in range(NT + 1):
            if t < NT:
                part = t // NTP
                dve.wait_ge(y1_ready, t + 1)
                step(dve.scalar_tensor_tensor(out=y_rows[:, t, 0, :], in0=y_rows[:, t, 1, :], scalar=gates12[:, t, 1:2],
                                              in1=y_rows[:, t, 0, :], op0=ALU.mult, op1=ALU.add))
                step(dve.tensor_tensor(y_rows[:, t, 0, :], y_rows[:, t, 0, :], gate2[:, part, :], ALU.mult))
                dve.tensor_tensor(x_tok[:, t, :], x_tok[:, t, :], y_rows[:, t, 0, :], ALU.add).then_inc(x2_ready, 1)
            if t:
                u = t - 1
                dve.wait_ge(std3_ready, u + 1)
                step(dve.reciprocal(rstd[:, u:u + 1], std2[:, u:u + 1]))
                dve.scalar_tensor_tensor(out=y_rows[:, u, 0, :], in0=x_tok[:, u, :], scalar=rstd[:, u:u + 1],
                                         in1=g_fin, op0=ALU.mult, op1=ALU.mult).then_inc(y_ready, 1)

    def pair_ps(r):
        return z[:, 1024 * (r % 3):1024 * (r % 3) + 1024]

    def proj_ps(t):
        return z[:, 1024 * (t % 2):1024 * (t % 2) + 1024]

    def phase_b_pe(pe):
        def acc(out, lhsT, rhs, start=False, stop=False):
            return pe.matmul(out, lhsT, rhs, start=start, stop=stop, skip_group_check=True)

        pe.wait_ge(rows_loaded, 64)
        pe.wait_ge(ada_kept, 4 + NPAIR)
        pe.wait_ge(o_kept, NPAIR)
        for r in range(8):
            kind, part = r // 2, r % 2
            if r >= 3:
                pe.wait_ge(pair_kept, r - 2)
            for c in range(2):
                out = pair_ps(r)[:, 512 * c:512 * c + 512]
                acc(out, sel_tok[:, part, :], mod_rows[:, 2 * kind + c, :], start=True)
                mm = acc(out, ones_row[:, :], ada_b_row[:, (2 * kind + c) * ADW:(2 * kind + c + 1) * ADW], stop=True)
            mm.then_inc(pair_fill, 1)
        pe.wait_ge(wo_loaded, 16)
        def project_out(t):
            pe.wait_ge(pair_kept, 8 + max(t - 1, 0))
            for c in range(2):
                out = proj_ps(t)[:, 512 * c:512 * c + 512]
                for k in range(NPAIR):
                    mm = acc(out, o_T[:, k, t * P:(t + 1) * P], w_o[:, k, 512 * c:512 * c + 512],
                             start=(k == 0), stop=(k == NPAIR - 1))
            mm.then_inc(pair_fill, 1)

        def turn_h2(u):
            pe.wait_ge(h2_ready, u + 1)
            pe.wait_ge(h2T_kept, u)
            for k in range(KD):
                mm = pe.transpose(z[:, 2048 + k * P:2048 + (k + 1) * P], h2_tok[:, u, k * P:(k + 1) * P], ident[:, :])
            mm.then_inc(h2T_mm, 1)

        def route(u):
            pe.wait_ge(h2T_kept, u + 1)
            for k in range(KD):
                mm = acc(fill_ps[:, 0, NE * u:NE * (u + 1)], h_T[:, k, u * P:(u + 1) * P], router_w[:, k, :],
                         start=(u == 0 and k == 0), stop=(k == KD - 1))
            mm.then_inc(logits_ready, 1)

        for t in range(NT + 3):
            if t < NT:
                project_out(t)
            if 2 <= t < NT + 2:
                turn_h2(t - 2)
            if t >= 3:
                route(t - 3)
        pe.wait_ge(chosen_ready, 1)
        for t in range(NT + 1):
            for u in range(min(t, NT - 1) + 1):
                mm = acc(fill_ps[:, 1, NE * t:NE * (t + 1)], before_b[:, :] if u == t else ones_b[:, :],
                         chosen_b[:, u, :], start=(t == 0), stop=(u == min(t, NT - 1)))
        mm.then_inc(places_mm, 1)

        def turn_slot(j):
            pe.wait_ge(x_slot_loaded, 16 * (j + 1))
            for k in range(KD):
                mm = pe.transpose(z[:, 2048 + k * P:2048 + (k + 1) * P], x_slot[:, k * P:(k + 1) * P], ident[:, :])
            mm.then_inc(x_slotT_mm, 1)

        turn_slot(0)
        pe.wait_ge(slots_known, 1)
        n = pe.value_load(slot_tab[0:1, MAX_SLOTS + 1:MAX_SLOTS + 2], min_val=NE, max_val=MAX_SLOTS)
        with pe.Fori(0, n) as j:
            b = pe.value_load(slot_tab[0:1, bass.ds(j, 1)], min_val=0, max_val=NE - 1) % 2
            pe.wait_ge(x_slotT_kept, j + 1)
            pe.wait_ge(hid_ready, j)
            for i, done in ((0, gate_ready), (1, up_ready)):
                pe.wait_ge(exp_loaded[i], 16 * (j + 1))
                for k in range(KD):
                    mm = acc(zb(i), x_slotT[:, k, :], exp_w[:, bass.ds(b, 1), i * 4096 + k * FE:i * 4096 + (k + 1) * FE],
                             start=(k == 0), stop=(k == KD - 1))
                mm.then_inc(done, 1)
            turn_slot(j + 1)
            pe.wait_ge(hid_ready, j + 1)
            for k in range(KF):
                mm = pe.transpose(fill_ps[:, 0, k * P:(k + 1) * P], hid[:, k * P:(k + 1) * P], ident[:, :])
            mm.then_inc(hidT_mm, 1)
            pe.wait_ge(hidT_kept, j + 1)
            pe.wait_ge(exp_loaded[2], 16 * (j + 1))
            pe.wait_ge(y_slot_kept, j)
            for c in range(2):
                for k in range(KF):
                    mm = acc(zb(2 + c), hidT[:, k, :],
                             exp_w[:, bass.ds(b, 1), 8192 + k * D + c * 512:8192 + k * D + (c + 1) * 512],
                             start=(k == 0), stop=(k == KF - 1))
            mm.then_inc(down_ready, 1)

    FILLS = 11

    block = ctx.enter_context(nc.Block())

    @block.sync
    def _(sp):
        sp.dma_start(c_rows[0:1, :], io["c_prompt"]).then_inc(c_loaded, 16)
        sp.dma_start(c_rows[1:NC, :], io["c_sample"]).then_inc(c_loaded, 16)
        sp.dma_start(in_rows[0:6 * KD, :], io["ada_b"].rearrange("o (k p) -> (o k) p", p=P)).then_inc(c_loaded, 16)
        sp.dma_start(in_rows[6 * KD:7 * KD, :], io["norm_mix_g"].rearrange("o (k p) -> (o k) p", p=P)).then_inc(c_loaded, 16)
        sp.dma_start(in_rows[7 * KD:8 * KD, :], io["norm_ffn_g"].rearrange("o (k p) -> (o k) p", p=P)).then_inc(c_loaded, 16)
        sp.dma_start(x_tok[:, 0:NTP, :], xp_v).then_inc(x_loaded, 16)
        sp.dma_start(x_tok[:, NTP, :], xs_v).then_inc(x_loaded, 16)
        for j in range(3):
            sp.dma_start(ada_w[:, j], ada_v[:, :, j * ADW:(j + 1) * ADW]).then_inc(ada_loaded[j], 16)
        sp.wait_ge(ada_mm, 1)
        sp.dma_start(ada_w[:, 0], ada_v[:, :, 3 * ADW:4 * ADW]).then_inc(ada_loaded[0], 16)

        def load_pair(p, first):
            for c in range(3):
                if not first:
                    sp.wait_ge(fill_ready, (p - 1) * FILLS + 2 * c + 2)
                sp.dma_start(w_pair[:, c], qkv_v[:, :, bass.ds(p * P + c * D, P)]).then_inc(wqkv_loaded[c], 16)
            if not first:
                sp.wait_ge(fill_ready, (p - 1) * FILLS + 8)
            sp.dma_start(past_k[:, :, :], ck_v[:, :, bass.ds(p * P, P)]).then_inc(past_k_loaded, 16)

        def store_pair(p):
            sp.wait_ge(fill_kept, (p + 1) * FILLS)
            c = bass.ds(p * P, P)
            sp.dma_start(kp_v[:, :, c], k_tok[:, 0:NTP, :]).then_inc(kv_stored, 16)
            sp.dma_start(vp_v[:, :, c], v_tok[:, 0:NTP, :]).then_inc(kv_stored, 16)
            sp.dma_start(ks_v[:, c], k_tok[:, NTP, :]).then_inc(kv_stored, 16)
            sp.dma_start(vs_v[:, c], v_tok[:, NTP, :]).then_inc(kv_stored, 16)

        load_pair(0, True)
        sp.dma_start(past_v[:, :, :], cv_v[:, :, 0:P]).then_inc(past_v_loaded, 16)
        sp.wait_ge(consts_set, 10)
        sp.dma_start(slots_in.rearrange("(p n) (a c) -> p (n a) c", p=P, c=256),
                     zeros[:, :].unsqueeze(1).to_broadcast([P, (MAX_SLOTS + 1) * D // 256, 256])).then_inc(zeros_stored, 16)
        sp.dma_start(slots_out[NE * P:, :].rearrange("(p n) (a c) -> p (n a) c", p=P, c=256),
                     zeros[:, :].unsqueeze(1).to_broadcast([P, (MAX_SLOTS - NE) * D // 256, 256])).then_inc(zeros_stored, 16)
        sp.wait_ge(ada_mm, 4)
        sp.dma_start(ada_w[:, 0], ada_v[:, :, 4 * ADW:5 * ADW]).then_inc(ada_loaded[0], 16)
        sp.dma_start(w_o, wo_v).then_inc(wo_loaded, 16)
        with sp.Fori(0, NPAIR - 1) as p:
            load_pair(p + 1, False)
            store_pair(p)
            sp.wait_ge(o_ready, p + 1)
            sp.dma_start(past_v[:, :, :], cv_v[:, :, bass.ds((p + 1) * P, P)]).then_inc(past_v_loaded, 16)
            sp.wait_ge(ada_mm, p + 5)
            sp.dma_start(ada_w[:, 0], ada_v[:, :, bass.ds((p + 5) * ADW, ADW)]).then_inc(ada_loaded[0], 16)
        store_pair(NPAIR - 1)
        phase_b_sync(sp)

    @block.gpsimd
    def _(pool):
        pool.memset(ident[:, :], 0.0).then_inc(consts_set, 1)
        pool.memset(sum_sel[:, :], 0.0).then_inc(consts_set, 1)
        pool.memset(sel_tok[:, :, :], 0.0).then_inc(consts_set, 1)
        pool.memset(ntri[:, :], -1.0).then_inc(consts_set, 1)
        pool.memset(nones[:, :], -1.0).then_inc(consts_set, 1)
        pool.memset(ones_row[:, :], 1.0).then_inc(consts_set, 1)
        pool.memset(eps1[:, :], EPS).then_inc(consts_set, 1)
        pool.memset(zeros[:, :], 0.0).then_inc(consts_set, 1)
        pool.memset(q_z[:, :, :], 0.0).then_inc(consts_set, 1)
        pool.memset(c_T[:, :, :], 0.0).then_inc(consts_set, 1)
        pool.wait_ge(consts_set, 10)
        pool.affine_select(out=ident[:, :], in_=ident[:, :], compare_op=ALU.not_equal, fill=1.0, base=0,
                           pattern=[[-1, P]], channel_multiplier=1).then_inc(consts_set, 1)
        pool.affine_select(out=ntri[:, :], in_=ntri[:, :], compare_op=ALU.is_ge, fill=0.0, base=0,
                           pattern=[[-1, P]], channel_multiplier=1).then_inc(consts_set, 1)
        for g in range(NG4):
            pool.wait_ge(consts_set, 12 + 3 * g)
            pool.affine_select(out=sum_sel[:, :], in_=sum_sel[:, :], compare_op=ALU.not_equal, fill=1.0,
                               base=-CW * g, pattern=[[-1, NC]], channel_multiplier=1).then_inc(consts_set, 1)
            pool.affine_select(out=sel_tok[:, 0, :], in_=sel_tok[:, 0, :], compare_op=ALU.not_equal, fill=1.0,
                               base=-CW * g, pattern=[[0, P]], channel_multiplier=1).then_inc(consts_set, 1)
            pool.affine_select(out=sel_tok[:, 1, :], in_=sel_tok[:, 1, :], compare_op=ALU.not_equal, fill=1.0,
                               base=-CW * g - 1, pattern=[[-1, NS], [0, SS]],
                               channel_multiplier=1).then_inc(consts_set, 1)

        def causal(buf):
            for first, step, n in ((0, 512, 4), (1408, 512, 2), (2048, 256, 3), (2688, 128, 1)):
                v = buf[:, first:first + P] if n == 1 else blocks_of(buf, first, step, n)
                yield pool.affine_select(out=v, in_=v, compare_op=ALU.is_gt, fill=0.0, base=0,
                                         pattern=[[0, n], [1, P]] if n > 1 else [[1, P]],
                                         channel_multiplier=-1)

        def mask(buf, done, count):
            for ins in causal(buf):
                last = ins
            last.then_inc(done, 1)
            pool.wait_ge(done, count)
            pool.nop(nofuse=True)
            v = buf[:, 2560:2816].rearrange("p (a s q) -> p a s q", a=2, s=NS)
            pool.affine_select(out=v, in_=v, compare_op=ALU.is_ge, fill=0.0, base=0,
                               pattern=[[0, 2], [-SS, NS], [0, SS]], channel_multiplier=1).then_inc(done, 1)

        with pool.Fori(0, NPAIR) as p:
            pool.wait_ge(sp_ready, p + 1)
            pool.nop(nofuse=True)
            mask(ew_sp, sp_masked, 2 * p + 1)
            pool.wait_ge(w_ready, p + 1)
            pool.nop(nofuse=True)
            mask(ew_w, w_masked, 2 * p + 1)
        phase_b_pool(pool)

    @block.scalar
    def _(act):
        act.wait_ge(c_loaded, 80)
        act.activation(c_tmp[0:NC, :], c_rows[0:NC, :], ACT.Exp, scale=-1.0).then_inc(silu_exp, 1)
        act.wait_ge(x_loaded, 32)
        for t in range(NT):
            act.activation(x_sq, x_tok[:, t, :], ACT.Square, accum_out=rstd[:, t:t + 1]).then_inc(sq_ready, 1)
            act.wait_ge(sq_ready, t + 1)
        act.wait_ge(consts_set, 10)
        act.activation(rstd[:, :], rstd[:, :], ACT.Sqrt, scale=1.0 / D, bias=eps1[:, 0:1]).then_inc(std_ready, 1)
        for t in range(NT):
            act.wait_ge(rstd_ready, 1)
            act.activation(xs[t], x_tok[:, t, :], ACT.Copy, scale=rstd[:, t:t + 1]).then_inc(xs_ready, 1)
        with act.Fori(0, NPAIR) as p:
            act.wait_ge(abs_ready, p + 1)
            act.activation(ew_t[:, :], ew_t[:, :], ACT.Exp, scale=-1.0).then_inc(exp_ready, 1)
            act.wait_ge(exp_ready, p + 1)
            act.activation(ew_t[:, :], ew_t[:, :], ACT.Ln, bias=1.0).then_inc(ln_ready, 1)
            act.wait_ge(logw_ready, p + 1)
            act.activation(ew_w[:, :], z[:, :], ACT.Exp).then_inc(w_ready, 1)
        phase_b_act(act)

    @block.vector
    def _(dve):
        dve.wait_ge(silu_exp, 1)
        dve.tensor_scalar_add(c_tmp[0:NC, :], c_tmp[0:NC, :], 1.0).then_inc(small_dve, 1)
        dve.wait_ge(small_dve, 1)
        dve.reciprocal(c_tmp[0:NC, :], c_tmp[0:NC, :]).then_inc(small_dve, 1)
        dve.wait_ge(small_dve, 2)
        dve.tensor_tensor(c_rows[0:NC, :], c_rows[0:NC, :], c_tmp[0:NC, :], ALU.mult).then_inc(silu_ready, 1)
        dve.wait_ge(std_ready, 1)
        dve.reciprocal(rstd[:, :], rstd[:, :]).then_inc(rstd_ready, 1)
        dve.wait_ge(setup_T, 1)
        dve.wait_ge(consts_set, 10)
        dve.tensor_copy(c_T[:, :, 0:NC], fill_ps[:, 0, 0:KD * NC].rearrange("p (k c) -> p k c", c=NC)).then_inc(setup_T_used, 1)
        dve.tensor_copy(ada_bT[:, :], fill_ps[:, 0, 128:128 + 6 * KD]).then_inc(setup_T_used, 1)
        dve.tensor_copy(norm_gT[:, :], fill_ps[:, 0, 128 + 6 * KD:128 + 8 * KD]).then_inc(setup_T_used, 1)
        for j in range(4):
            dve.wait_ge(ada_mm, j + 1)
            dve.tensor_copy(mod_rows[:, j, :], fill_ps[:, j % 2, :]).then_inc(ada_kept, 1)
        dve.wait_ge(mod_T_mm, 1)
        dve.tensor_tensor(mod_T[:, :, :], fill_ps[:, 0, 0:2 * KD * NC].rearrange("p (k c) -> p k c", c=NC),
                          ada_bT[:, 0:2 * KD].unsqueeze(2).to_broadcast([P, 2 * KD, NC]), ALU.add).then_inc(small_dve, 1)
        dve.wait_ge(small_dve, 3)
        dve.scalar_tensor_tensor(out=scale_T[:, :, :], in0=mod_T[:, KD:2 * KD, :], scalar=1.0,
                                 in1=norm_gT[:, 0:KD].unsqueeze(2).to_broadcast([P, KD, NC]),
                                 op0=ALU.add, op1=ALU.mult).then_inc(modT_ready, 1)
        dve.wait_ge(modT_ready, 1)
        for k in range(KD):
            dve.wait_ge(xsT_ready, k + 1)
            dve.tensor_scalar(h_T[:, k, 0:SEQ], zb(k % 6), scale_T[:, k, 0:1], mod_T[:, k, 0:1],
                              ALU.mult, ALU.add).then_inc(hT_ready, 1)
        for a in range(2):
            ks = slice(4 * a, 4 * a + 4)
            hs = h_T[:, ks, SEQ:TOK]
            dve.wait_ge(xsT_ready, KD + 1 + a)
            for k in range(4 * a, 4 * a + 4):
                hv = h_T[:, k, SEQ:TOK].rearrange("p (s q) -> p s q", q=SS)
                src = zb(2 + a, 128 * (k % 4), 128 * (k % 4) + 128).rearrange("p (s q) -> p s q", q=SS)
                dve.tensor_tensor(hv, src, scale_T[:, k, 1:NC].unsqueeze(2).to_broadcast([P, NS, SS]),
                                  ALU.mult).then_inc(hT_ready, 1)
        for k in range(KD):
            hv = h_T[:, k, SEQ:TOK].rearrange("p (s q) -> p s q", q=SS)
            dve.wait_ge(hT_ready, KD + k + 1)
            dve.tensor_tensor(hv, hv, mod_T[:, k, 1:NC].unsqueeze(2).to_broadcast([P, NS, SS]),
                              ALU.add).then_inc(hT_ready, 1)

        def keep(p, f):
            dve.wait_ge(fill_ready, p * FILLS + f + 1)
            src = fill_ps[:, f % 2, :]
            n, a = (512, 0) if f % 2 == 0 else (P, SEQ)
            if f < 2:
                dve.tensor_scalar(q_z[0:HD, 0, a:a + n], src[0:HD, 0:n], SCALE, None, ALU.mult)
                ins = dve.tensor_scalar(q_z[HD:P, 1, a:a + n], src[HD:P, 0:n], SCALE, None, ALU.mult)
            elif f < 4:
                ins = dve.tensor_copy(k_T[:, a:a + n], src[:, 0:n])
            elif f < 6:
                ins = dve.tensor_copy(v_T[:, a:a + n], src[:, 0:n])
            elif f < 8:
                ins = dve.tensor_copy(past_kT[:, 4 * (f - 6):4 * (f - 6) + 4, :], src.rearrange("p (s k) -> p s k", k=P))
            elif f == 8:
                ins = dve.tensor_copy(k_tok[:, 0:NTP, :], src.rearrange("p (s k) -> p s k", k=P))
            elif f == 9:
                ins = dve.tensor_copy(v_tok[:, 0:NTP, :], src.rearrange("p (s k) -> p s k", k=P))
            elif f == 10:
                dve.tensor_copy(k_tok[:, NTP, :], src[:, 0:P])
                ins = dve.tensor_copy(v_tok[:, NTP, :], src[:, P:2 * P])
            ins.then_inc(fill_kept, 1)

        def attend(p, more):
            dve.wait_ge(z_ready, p + 1)
            dve.tensor_scalar(ew_t[:, :].bitcast(I32), z[:, :].bitcast(I32), 0x7FFFFFFF, None,
                              ALU.bitwise_and).then_inc(abs_ready, 1)
            if more:
                keep(p + 1, 0)
                keep(p + 1, 1)
            dve.wait_ge(ln_ready, p + 1)
            dve.scalar_tensor_tensor(out=ew_sp[:, :], in0=z[:, :], scalar=0.0, in1=ew_t[:, :],
                                     op0=ALU.max, op1=ALU.add).then_inc(sp_ready, 1)
            if more:
                for f in range(2, 8):
                    keep(p + 1, f)
            dve.wait_ge(o_ready, p + 1)
            dve.tensor_copy(o_T[:, bass.ds(p, 1), 0:SEQ], zb(0).unsqueeze(1))
            dve.tensor_copy(o_T[:, bass.ds(p, 1), SEQ:TOK], zb(1, 0, P).unsqueeze(1)).then_inc(o_kept, 1)
            if more:
                dve.wait_ge(kv_stored, 64 * (p + 1))
                for f in range(8, 11):
                    keep(p + 1, f)
            dve.wait_ge(ada_mm, p + 5)
            dve.tensor_copy(mod_rows[:, bass.ds(p, 1), :], fill_ps[:, 1, :].unsqueeze(1)).then_inc(ada_kept, 1)

        for f in range(11):
            keep(0, f)
        with dve.Fori(0, NPAIR - 1) as p:
            attend(p, True)
        attend(NPAIR - 1, False)
        phase_b_dve(dve)

    @block.tensor
    def _(pe):
        def ada_slice(src, out):
            for k in range(KD):
                g = k % NG4
                mm = pe.matmul(out[CW * g:CW * g + CW, :], c_T[:, k, :], src[:, k, :],
                               start=(k < NG4), stop=(k >= NG4), skip_group_check=True)
            return mm

        def transposes(srcs, out):
            for i, s in enumerate(srcs):
                mm = pe.transpose(out[:, i * P:(i + 1) * P], s, ident[:, :])
            return mm

        pe.wait_ge(consts_set, 12 + 3 * NG4)
        pe.wait_ge(c_loaded, 80)
        pe.wait_ge(silu_ready, 1)
        for k in range(KD):
            pe.transpose(fill_ps[:, 0, k * NC:(k + 1) * NC], c_rows[0:NC, k * P:(k + 1) * P], ident[0:NC, 0:NC])
        pe.transpose(fill_ps[:, 0, 128:128 + 64], in_rows, ident[0:64, 0:64]).then_inc(setup_T, 1)
        pe.wait_ge(xs_ready, NT)
        for k in range(6):
            transposes([xs[t][:, k * P:(k + 1) * P] for t in range(NTP)], zb(k)).then_inc(xsT_ready, 1)
        pe.wait_ge(setup_T_used, 3)
        for j in range(4):
            pe.wait_ge(ada_loaded[j % 3], 16 * (1 + j // 3))
            if j >= 2:
                pe.wait_ge(ada_kept, j - 1)
            ada_slice(ada_w[:, j % 3], fill_ps[:, j % 2, :]).then_inc(ada_mm, 1)
        pe.wait_ge(ada_kept, 4)
        for k in range(2 * KD):
            mm = pe.matmul(fill_ps[:, 0, k * NC:(k + 1) * NC],
                           mod_rows[:, k // 4, (k % 4) * P:(k % 4 + 1) * P], sum_sel[:, :],
                           start=(k == 0), stop=True, skip_group_check=True)
        mm.then_inc(mod_T_mm, 1)
        for k in (6, 7):
            pe.wait_ge(hT_ready, k - 5)
            transposes([xs[t][:, k * P:(k + 1) * P] for t in range(NTP)], zb(k % 6)).then_inc(xsT_ready, 1)
        for a in range(2):
            pe.wait_ge(hT_ready, 3 + a)
            transposes([xs[NTP][:, k * P:(k + 1) * P] for k in range(4 * a, 4 * a + 4)],
                       zb(2 + a)).then_inc(xsT_ready, 1)

        def project(p, f, first=False):
            out = fill_ps[:, f % 2, :]
            if f == 0 and not first:
                pe.wait_ge(fill_kept, p * FILLS)
            elif f == 1 and not first:
                pe.wait_ge(ada_kept, p + 3)
            elif f >= 2:
                pe.wait_ge(fill_kept, p * FILLS + f - 1)
            if f < 6:
                c, a, n = f // 2, (f % 2) * SEQ, (SEQ, P)[f % 2]
                if f % 2 == 0:
                    pe.wait_ge(wqkv_loaded[c], 16 * (p + 1))
                for k in range(KD):
                    mm = pe.matmul(out[:, 0:n], w_pair[:, c, k, :], h_T[:, k, a:a + n],
                                   start=(k == 0), stop=(k == KD - 1))
            elif f < 8:
                pe.wait_ge(past_k_loaded, 16 * (p + 1))
                mm = transposes([past_k[:, s, :] for s in range(4 * (f - 6), 4 * (f - 6) + 4)], out)
            elif f < 10:
                pe.wait_ge(fill_kept, p * FILLS + 6)
                src = (k_T, v_T)[f - 8]
                mm = transposes([src[:, t * P:(t + 1) * P] for t in range(NTP)], out)
            else:
                mm = transposes([k_T[:, SEQ:TOK], v_T[:, SEQ:TOK]], out)
            mm.then_inc(fill_ready, 1)

        def acc(out, lhsT, rhs, start=False, stop=False):
            return pe.matmul(out, lhsT, rhs, start=start, stop=stop, skip_group_check=True)

        def scores(p):
            pe.wait_ge(fill_kept, p * FILLS + 8)
            pe.wait_ge(o_kept, p)
            for h in range(2):
                acc(zb(h), k_T[:, 0:P], q_z[:, h, 0:SEQ], start=True)
                acc(zb(2 + h, 0, 384), k_T[:, P:2 * P], q_z[:, h, P:SEQ], start=True)
                acc(zb(2 + h, 384, 512), k_T[:, 3 * P:4 * P], q_z[:, h, 3 * P:SEQ])
            acc(zb(4), k_T[:, 2 * P:3 * P], q_z[:, :, 2 * P:SEQ], start=True)
            acc(zb(5, 0, 256), k_T[:, SEQ:TOK], q_z[:, :, SEQ:TOK], start=True)
            past = zb(5, 256, 512).rearrange("p (h s q) -> p h s q", h=2, s=NS)
            for s in range(NS):
                mm = acc(past[:, :, s, :], past_kT[:, s, :], q_z[:, :, SEQ + SS * s:SEQ + SS * (s + 1)])
            mm.then_inc(z_ready, 1)

        def keep_sums(p):
            pe.wait_ge(sp_masked, 2 * p + 2)
            for b in range(6):
                acc(zb(b), ntri[:, :], ew_sp[:, 512 * b:512 * b + 512])
            for h in range(2):
                k1, k2, k3 = 1024 + 512 * h, 2048 + 256 * h, 1408 + 512 * h
                for dst, src, n in ((512 * h + 128, k1, 384), (512 * h + 256, k2, 256), (512 * h + 384, k3, 128),
                                    (k1 + 128, k2, 256), (k1 + 256, k3, 128), (k2 + 128, k3, 128)):
                    acc(z[:, dst:dst + n], nones[:, :], ew_sp[:, src:src + n])
            acc(zb(5, 256, 512), nones[:, :], ew_sp[:, 2560:2816], stop=True).then_inc(logw_ready, 1)

        def values(p):
            pe.wait_ge(w_masked, 2 * p + 2)
            pe.wait_ge(past_v_loaded, 16 * (p + 1))
            pe.wait_ge(fill_kept, (p + 1) * FILLS)
            for kb in range(NTP):
                for h in range(2):
                    src = (512 * h, 1024 + 512 * h, 2048 + 256 * h, 1408 + 512 * h)[kb]
                    n = SEQ - kb * P
                    acc(z[HD * h:HD * h + HD, kb * P:SEQ], v_tok[:, kb, HD * h:HD * h + HD],
                        ew_w[:, src:src + n], start=(kb == 0))
            for h in range(2):
                acc(z[HD * h:HD * h + HD, 512:640], v_tok[:, NTP, HD * h:HD * h + HD],
                    ew_w[:, 2560 + P * h:2688 + P * h], start=True)
            for s in range(NS):
                for h in range(2):
                    c = 2816 + P * h + SS * s
                    mm = acc(z[HD * h:HD * h + HD, 512 + SS * s:512 + SS * (s + 1)],
                             past_v[:, s, HD * h:HD * h + HD], ew_w[:, c:c + SS])
            mm.then_inc(o_ready, 1)

        def attend(p, more):
            scores(p)
            if more:
                for f in range(4):
                    project(p + 1, f)
            keep_sums(p)
            if more:
                for f in range(4, 8):
                    project(p + 1, f)
            values(p)
            if more:
                for f in range(8, 11):
                    project(p + 1, f)
            pe.wait_ge(ada_loaded[0], 16 * (p + 3))
            if more:
                pe.wait_ge(fill_kept, (p + 1) * FILLS + 10)
            else:
                pe.wait_ge(ada_kept, p + 4)
            ada_slice(ada_w[:, 0], fill_ps[:, 1, :]).then_inc(ada_mm, 1)

        pe.wait_ge(hT_ready, KD + 2 * KD)
        for f in range(11):
            project(0, f, first=True)
        with pe.Fori(0, NPAIR - 1) as p:
            attend(p, True)
        attend(NPAIR - 1, False)
        phase_b_pe(pe)


_INS = ["x_prompt", "x_sample", "cache_sb_k", "cache_sb_v", "c_prompt", "c_sample", "ada_w", "ada_b",
        "norm_mix_g", "norm_ffn_g", "final_norm_g", "sb_w_qkv", "sb_w_o", "router_w", "router_bias",
        "exp_w_gate", "exp_w_up", "exp_w_down"]
_OUTS = {"y_prompt": (1, SEQ, D), "y_sample": (NS, SS, D), "k_prompt": (1, SEQ, H, HD), "v_prompt": (1, SEQ, H, HD),
         "k_sample": (NS, SS, H, HD), "v_sample": (NS, SS, H, HD)}


def kernel(**inputs):
    import numpy as _np
    import concourse.bacc as _bacc
    from concourse.bass_utils import run_bass_kernel_spmd as _run

    nc = _bacc.Bacc("TRN2", target_bir_lowering=False, num_devices=1)
    arrays, io = {}, {}
    for name in _INS:
        a = _np.ascontiguousarray(inputs[name])
        arrays[f"in_{name}"] = a
        io[name] = nc.dram_tensor(f"in_{name}", a.shape, mybir.dt.from_np(a.dtype), kind="ExternalInput").ap()
    for name, shape in _OUTS.items():
        io[name] = nc.dram_tensor(f"out_{name}", shape, F32, kind="ExternalOutput").ap()
    stream_step(nc, io)
    r = _run(nc, [arrays], core_ids=[0])
    got = tuple(r.results[0][f"out_{name}"] for name in _OUTS)
    return got + (None, None, None, None)
```

```python
from contextlib import ExitStack

import concourse.bass as bass
from concourse import mybir

F32 = mybir.dt.float32
I32 = mybir.dt.int32
BF16 = mybir.dt.bfloat16
F32R = mybir.dt.float32r
ALU = mybir.AluOpType
ACT = mybir.ActivationFunctionType
AX_X = mybir.AxisListType.X

P = 128
D = 1024
KD = D // P
SEQ = 512
NS = 8
SS = 16
NSAM = NS * SS
PAST = 128
TOK = SEQ + NSAM
NT = TOK // P
NTP = SEQ // P
NC = 1 + NS
H = 16
HD = 64
NPAIR = H // 2
CW = 32
NG4 = P // CW
ADW = 512
NE = 16
NGRP = 4
EPG = NE // NGRP
FE = 512
KF = FE // P
EPS = 1e-6
SCALE = HD ** -0.5


def stream_step(nc, io):
    with ExitStack() as ctx:
        build(nc, io, ctx)


def build(nc, io, ctx):
    def sb(name, shape, dt=F32, c=ctx):
        return c.enter_context(nc.sbuf_tensor(name, shape, dt))

    def sem(name):
        return ctx.enter_context(nc.semaphore(name))

    x_tok = sb("x_tok", [P, NT, D])
    h_T_at = nc.sbuf_base
    h_T = sb("h_T", [P, KD, TOK])
    ident = sb("ident", [P, P])
    sum_sel = sb("sum_sel", [P, NC])
    sel_tok = sb("sel_tok", [P, 2, P])
    ones_row = sb("ones_row", [1, P])
    mod_T = sb("mod_T", [P, 2 * KD, NC])
    ada_bT = sb("ada_bT", [P, 6 * KD])
    norm_gT = sb("norm_gT", [P, 2 * KD])
    scale_T = sb("scale_T", [P, KD, NC])
    rstd = sb("rstd", [P, NT])
    eps1 = sb("eps1", [P, 1])
    zero_f = sb("zero_f", [P, 1])
    zero_a = sb("zero_a", [P, 1])

    phase_a = ExitStack()
    o_T = sb("o_T", [P, NPAIR, TOK], c=phase_a)
    mod_rows = sb("mod_rows", [P, 8, ADW], c=phase_a)
    ada_w = sb("ada_w", [P, 3, KD, ADW], c=phase_a)
    w_pair = sb("w_pair", [P, 3, KD, P], c=phase_a)
    past_k = sb("past_k", [P, NS, P], c=phase_a)
    past_v = sb("past_v", [P, NS, P], c=phase_a)
    past_kT = sb("past_kT", [P, NS, P], c=phase_a)
    q_z = sb("q_z", [P, 2, TOK], c=phase_a)
    k_T = sb("k_T", [P, TOK], c=phase_a)
    v_T = sb("v_T", [P, TOK], c=phase_a)
    k_tok = sb("k_tok", [P, NT, P], c=phase_a)
    v_tok = sb("v_tok", [P, NT, P], c=phase_a)
    ntri = sb("ntri", [P, P], c=phase_a)
    nones = sb("nones", [P, P], c=phase_a)
    zeros = sb("zeros", [P, D // 2], c=phase_a)
    c_T = sb("c_T", [P, KD, CW], c=phase_a)
    ZC = 6 * 512
    ew_t = sb("ew_t", [P, ZC], c=phase_a)
    ew_sp = sb("ew_sp", [P, ZC], c=phase_a)
    ew_w = sb("ew_w", [P, ZC], c=phase_a)
    c_rows = mod_rows[:, 6:8, :].rearrange("p a n -> p (a n)")
    c_tmp = mod_rows[:, 4:6, :].rearrange("p a n -> p (a n)")
    in_rows = v_T[0:64, 0:P]
    xs = [ew_t[:, 0:1024], ew_t[:, 1024:2048], ew_t[:, 2048:3072], ew_sp[:, 0:1024], ew_sp[:, 1024:2048]]
    x_sq = ew_w[:, 0:1024]
    w_o = ada_w[:, 1:3, :, :].rearrange("p a k n -> p (a k n)").rearrange("p (k n) -> p k n", n=D)

    phase_a.close()

    MAX_SLOTS = NE + 2 * TOK // P - 1
    exp_w = sb("exp_w", [P, 2, 3 * 4096])
    gate2 = sb("gate2", [P, 2, D])
    std2 = sb("std2", [P, NT])
    ones_b = sb("ones_b", [P, P], BF16)
    before_b = sb("before_b", [P, P], BF16)
    chosen_b = sb("chosen_b", [P, NT, NE], BF16)
    router_w = sb("router_w", [P, KD, NE])
    router_b = sb("router_b", [P, NE])
    s_e = sb("s_e", [P, NT, NE])
    sel = sb("sel", [P, NT, NE])
    in_top = sb("in_top", [P, NT, NE])
    r_tmp = sb("r_tmp", [P, NT, NE])
    rows = sb("rows", [P, NT, NE])
    cmp4 = sb("cmp4", [P, NT * NGRP, EPG, EPG])
    g_score = sb("g_score", [P, NT, NGRP])
    g_rank = sb("g_rank", [P, NT, NGRP])
    tok1 = sb("tok1", [P, NT])
    row_f = sb("row_f", [P, NT, 2])
    row_i = sb("row_i", [P, NT, 2], I32)
    gates12 = sb("gates12", [P, NT, 2])
    slot_iota = sb("slot_iota", [P, MAX_SLOTS + 1], I32)
    iota_f = sb("iota_f", [P, MAX_SLOTS + 1])
    limits = sb("limits", [P, NT])
    count = sb("count", [P, NE])
    over = sb("over", [P, NE, NT])
    n_slots = sb("n_slots", [P, NE])
    ones_e = sb("ones_e", [P, NE])
    slot_end = sb("slot_end", [P, NE])
    base = sb("base", [P, NE])
    ended = sb("ended", [P, MAX_SLOTS + 1, NE])
    TAB_E, TAB_N = 0, MAX_SLOTS + 1
    TAB_NX = TAB_N + 1
    TAB_W = TAB_NX + MAX_SLOTS + 2
    TAB = TAB_W + MAX_SLOTS + 1
    slot_f = sb("slot_f", [P, TAB])
    slot_tab = sb("slot_tab", [P, TAB], I32)
    fetch_w = sb("fetch_w", [P, NE - 1])
    sq_tmp = sb("sq_tmp", [P, D])
    tmp = sb("tmp", [P, D])
    phase_r = ExitStack()
    h2_tok = sb("h2_tok", [P, NT, D], c=phase_r)
    gate1 = sb("gate1", [P, 2, D], c=phase_r)
    shift2 = sb("shift2", [P, 2, D], c=phase_r)
    scale2 = sb("scale2", [P, 2, D], c=phase_r)
    phase_r.close()
    ada_b_row = h2_tok[0:1, 0:4, :].rearrange("p a n -> p (a n)")
    x_slot = sb("x_slot", [P, D])
    x_slotT_hi = sb("x_slotT_hi", [P, KD, P], F32R)
    x_slotT_lo = sb("x_slotT_lo", [P, KD, P], F32R)
    sig = sb("sig", [P, FE])
    hid = sb("hid", [P, FE])
    hidT = sb("hidT", [P, KF, P])
    y_slot = sb("y_slot", [P, D])
    RING = 4
    UK = KD // RING
    w_lo = sb("w_lo", [P, RING, UK * FE], F32R)
    w_hi = nc.alloc_sbuf_tensor_at("w_hi", [P, RING, UK * FE], F32R, offset=h_T_at, align_bytes=32)
    y_rows = exp_w[:, 0, 0:NT * 2 * D].rearrange("p (t r n) -> p t r n", r=2, n=D)
    g_fin = exp_w[:, 1, 4096:4096 + D]
    g_ffn = tmp
    ZIN = -(-(MAX_SLOTS + 1) // (NPAIR - 1))
    ZOUT = -(-(MAX_SLOTS - NE - 1) // (NPAIR - 1))
    slots_in = nc.dram_tensor("slots_in", [ZIN * (NPAIR - 1) * P, D], F32, kind="Internal").ap()
    slots_out = nc.dram_tensor("slots_out", [(NE + 1 + ZOUT * (NPAIR - 1)) * P, D], F32, kind="Internal").ap()
    slots_in_z = slots_in.rearrange("(p n) (a c) -> p (n a) c", p=P, a=2)
    slots_out_z = slots_out[NE * P:, :].rearrange("(p n) (a c) -> p (n a) c", p=P, a=2)

    def zero_rows(n):
        return zeros[:, :].unsqueeze(1).to_broadcast([P, 2 * n, D // 2])

    z = ctx.enter_context(nc.psum_tensor("z", [P, ZC], F32))
    fill_ps = ctx.enter_context(nc.psum_tensor("fill_ps", [P, 2, 512], F32))

    def zb(b, a=0, e=512):
        return z[:, 512 * b + a:512 * b + e]

    def blocks_of(buf, first, step, n):
        lo = first - first % step
        return buf[:, lo:lo + step * n].rearrange("p (n c) -> p n c", c=step)[:, :, first % step:first % step + P]

    ada_v = io["ada_w"].rearrange("o (k p) n -> p (o k) n", p=P)
    qkv_v = io["sb_w_qkv"].rearrange("(k p) n -> p k n", p=P)
    ck_v = io["cache_sb_k"].rearrange("s k h d -> k s (h d)")
    cv_v = io["cache_sb_v"].rearrange("s k h d -> k s (h d)")
    wo_v = io["sb_w_o"].rearrange("(k p) n -> p k n", p=P)
    xp_v = io["x_prompt"].rearrange("b (t p) d -> p (b t) d", p=P)
    xs_v = io["x_sample"].rearrange("b s d -> (b s) d")
    kp_v = io["k_prompt"].rearrange("b (t p) h d -> p (b t) (h d)", p=P)
    vp_v = io["v_prompt"].rearrange("b (t p) h d -> p (b t) (h d)", p=P)
    ks_v = io["k_sample"].rearrange("b s h d -> (b s) (h d)")
    vs_v = io["v_sample"].rearrange("b s h d -> (b s) (h d)")
    yp_v = io["y_prompt"].rearrange("b (t p) d -> p (b t) d", p=P)
    ys_v = io["y_sample"].rearrange("b s d -> (b s) d")

    c_loaded = sem("c_loaded")
    x_loaded = sem("x_loaded")
    ada_loaded = [sem(f"ada_loaded{i}") for i in range(3)]
    wqkv_loaded = [sem(f"w{c}_loaded") for c in "qkv"]
    past_k_loaded = sem("past_k_loaded")
    past_v_loaded = sem("past_v_loaded")
    wo_loaded = sem("wo_loaded")
    kv_stored = sem("kv_stored")
    y_stored = sem("y_stored")
    consts_set = sem("consts_set")
    small_dve = sem("small_dve")
    small_act = sem("small_act")
    silu_exp = sem("silu_exp")
    silu_ready = sem("silu_ready")
    setup_T = sem("setup_T")
    setup_T_used = sem("setup_T_used")
    sq_ready = sem("sq_ready")
    std_ready = sem("std_ready")
    rstd_ready = sem("rstd_ready")
    xs_ready = sem("xs_ready")
    xsT_ready = sem("xsT_ready")
    hT_ready = sem("hT_ready")
    modT_ready = sem("modT_ready")
    mod_T_mm = sem("mod_T_mm")
    ada_mm = sem("ada_mm")
    ada_kept = sem("ada_kept")
    z_ready = sem("z_ready")
    fill_ready = sem("fill_ready")
    fill_kept = sem("fill_kept")
    abs_ready = sem("abs_ready")
    exp_ready = sem("exp_ready")
    ln_ready = sem("ln_ready")
    sp_ready = sem("sp_ready")
    sp_masked = sem("sp_masked")
    keep_sum = sem("keep_sum")
    logw_ready = sem("logw_ready")
    w_ready = sem("w_ready")
    w_masked = sem("w_masked")
    o_ready = sem("o_ready")
    o_kept = sem("o_kept")
    rows_loaded = sem("rows_loaded")
    exp_loaded = [sem(f"{c}_loaded") for c in ("gate", "up", "down")]
    x_slot_loaded = sem("x_slot_loaded")
    y_slot_stored = sem("y_slot_stored")
    zeros_stored = sem("zeros_stored")
    consts_b = sem("consts_b")
    scattered = sem("scattered")
    gathered = [sem(f"gathered{t}") for t in range(NT)]
    pair_fill = sem("pair_fill")
    pair_kept = sem("pair_kept")
    x1_ready = sem("x1_ready")
    std2_ready = sem("std2_ready")
    std3_ready = sem("std3_ready")
    h2_ready = sem("h2_ready")
    h2T_mm = sem("h2T_mm")
    h2T_kept = sem("h2T_kept")
    logits_ready = sem("logits_ready")
    sig_exp = sem("sig_exp")
    route_step = sem("route_step")
    chosen_ready = sem("chosen_ready")
    places_mm = sem("places_mm")
    rows_known = sem("rows_known")
    slots_known = sem("slots_known")
    hi_ready = sem("hi_ready")
    table_set = sem("table_set")
    lo_ready = sem("lo_ready")
    unit_used = sem("unit_used")
    x_hi_ready = sem("x_hi_ready")
    x_slotT_mm = sem("x_slotT_mm")
    x_slotT_kept = sem("x_slotT_kept")
    gate_sig = sem("gate_sig")
    sig_step = sem("sig_step")
    hid_ready = sem("hid_ready")
    hidT_mm = sem("hidT_mm")
    hidT_kept = sem("hidT_kept")
    down_ready = sem("down_ready")
    y_slot_kept = sem("y_slot_kept")
    y1_ready = sem("y1_ready")
    x2_ready = sem("x2_ready")
    y_ready = sem("y_ready")

    def phase_b_sync(sp):
        sp.wait_ge(ada_mm, 4 + NPAIR)
        sp.wait_ge(kv_stored, 64 * NPAIR)
        sp.dma_start(g_ffn[:, :], io["norm_ffn_g"].to_broadcast([P, D])).then_inc(rows_loaded, 16)
        sp.dma_start(ada_b_row, io["ada_b"][0:1, 2 * D:6 * D]).then_inc(rows_loaded, 16)
        sp.dma_start(router_w[:, :, :], io["router_w"].rearrange("(k p) e -> p k e", p=P)).then_inc(rows_loaded, 16)
        sp.dma_start(router_b[:, :], io["router_bias"].unsqueeze(0).to_broadcast([P, NE])).then_inc(rows_loaded, 16)
        sp.wait_ge(pair_fill, 8 + NT)
        for i in range(3):
            load_expert(sp, i, 0, 0, None)
        sp.wait_ge(scattered, 16 * 2 * NT)
        sp.dma_start(x_slot[:, :], slots_in[0:P, :]).then_inc(x_slot_loaded, 16)
        sp.wait_ge(slots_known, 1)
        n = sp.value_load(slot_tab[0:1, TAB_N:TAB_N + 1], min_val=NE, max_val=MAX_SLOTS)
        with sp.Fori(0, n) as j:
            before = sp.value_load(slot_tab[0:1, bass.ds(j + TAB_NX, 1)], min_val=0, max_val=NE - 1)
            fetch = sp.value_load(slot_tab[0:1, bass.ds(j + TAB_NX + 1, 1)], min_val=1, max_val=NE - 1)
            sp.wait_ge(x_slotT_mm, j + 1)
            sp.dma_start(x_slot[:, :], slots_in[bass.ds((j + 1) * P, P), :]).then_inc(x_slot_loaded, 16)
            sp.wait_ge(down_ready, j + 1)
            sp.nop(nofuse=True)
            for i in range(3):
                sp.wait_ge(exp_loaded[i], 16 * (j + 1))
                sp.nop(nofuse=True)
                load_expert(sp, i, fetch, fetch % 2, fetch != before)
            sp.wait_ge(y_slot_kept, j + 2)
            sp.dma_start(slots_out[bass.ds(j * P, P), :], y_slot[:, :]).then_inc(y_slot_stored, 16)
        sp.wait_ge(x_slot_loaded, 16 * (n + 1))
        for i in range(3):
            sp.wait_ge(exp_loaded[i], 16 * (n + 1))
        sp.nop(nofuse=True)
        sp.dma_start(g_fin, io["final_norm_g"].unsqueeze(0).to_broadcast([P, D])).then_inc(rows_loaded, 16)
        for t in range(NT):
            sp.wait_ge(y_ready, t + 1)
            dst = yp_v[:, t, :] if t < NTP else ys_v
            sp.dma_start(dst, y_rows[:, t, 0, :]).then_inc(y_stored, 16)
        sp.wait_ge(y_stored, 16 * NT)

    def load_expert(sp, i, e, b, cond):
        more = {} if cond is None else {"cond": cond}
        dst = exp_w[:, bass.ds(b, 1), i * 4096:(i + 1) * 4096].rearrange("p b (k f) -> p b k f", f=(FE, FE, D)[i])
        src = io[("exp_w_gate", "exp_w_up", "exp_w_down")[i]][0].rearrange("e (k p) f -> p e k f", p=P)
        sp.dma_start(dst, src[:, bass.ds(e, 1)], **more).then_inc(exp_loaded[i], 16)

    def raw_unit(b, u):
        return exp_w[:, bass.ds(b, 1), u * UK * FE:(u + 1) * UK * FE]

    def hi_unit(act, b, u):
        act.activation(w_hi[:, u % RING, :].unsqueeze(1), raw_unit(b, u), ACT.Copy).then_inc(hi_ready, 1)

    def lo_unit(dve, b, u):
        dve.tensor_tensor(w_lo[:, u % RING, :].unsqueeze(1), raw_unit(b, u), w_hi[:, u % RING, :].bitcast(F32).unsqueeze(1),
                          ALU.subtract).then_inc(lo_ready, 1)

    def slot_expert(eng, j):
        return eng.value_load(slot_tab[0:1, bass.ds(j, 1)], min_val=0, max_val=NE - 1)

    def slot_fetched(eng, j):
        return eng.value_load(slot_tab[0:1, bass.ds(j + TAB_W, 1)], min_val=16, max_val=16 * (MAX_SLOTS + 1))

    def phase_b_pool(pool):
        pool.wait_ge(ada_mm, 4 + NPAIR)
        pool.memset(ones_b[:, :], 1.0).then_inc(consts_b, 1)
        pool.memset(before_b[:, :], 1.0).then_inc(consts_b, 1)
        pool.memset(ones_e[:, :], 1.0).then_inc(consts_b, 1)
        pool.memset(cmp4[:, :, :, :], 0.0).then_inc(consts_b, 1)
        pool.iota(slot_iota[:, :], pattern=[[1, MAX_SLOTS + 1]], base=0, channel_multiplier=0).then_inc(consts_b, 1)
        pool.wait_ge(consts_b, 5)
        pool.affine_select(out=before_b[:, :], in_=before_b[:, :], compare_op=ALU.is_gt, fill=0.0, base=0,
                           pattern=[[1, P]], channel_multiplier=-1).then_inc(consts_b, 1)
        pool.wait_ge(zeros_stored, 32 * (NPAIR - 1))
        pool.wait_ge(rows_known, 1)
        for t in range(NT):
            for r in range(2):
                pool.indirect_dma_start(out=slots_in[:, :], out_offset=bass.IndirectOffsetOnAxis(ap=row_i[:, t, r:r + 1], axis=0),
                                        in_=h2_tok[:, t, :], in_offset=None).then_inc(scattered, 16)
        pool.wait_ge(slots_known, 1)
        n = pool.value_load(slot_tab[0:1, TAB_N:TAB_N + 1], min_val=NE, max_val=MAX_SLOTS)
        pool.wait_ge(y_slot_stored, n * 16 + 16)
        pool.wait_ge(lo_ready, n * (2 * RING) + RING)
        pool.nop(nofuse=True)
        for t in range(NT):
            for r in range(2):
                pool.indirect_dma_start(out=y_rows[:, t, r, :], out_offset=None, in_=slots_out[:, :],
                                        in_offset=bass.IndirectOffsetOnAxis(ap=row_i[:, t, r:r + 1], axis=0)).then_inc(gathered[t], 16)

    def rms(act, src, dst, done, count):
        act.activation(sq_tmp[:, :], src, ACT.Square, accum_out=dst).then_inc(sq_ready, 1)
        act.wait_ge(sq_ready, count)
        act.activation(dst, dst, ACT.Sqrt, scale=1.0 / D, bias=eps1[:, 0:1]).then_inc(done, 1)

    def phase_b_act(act):
        for t in range(NT):
            act.wait_ge(x1_ready, t + 1)
            rms(act, x_tok[:, t, :], std2[:, t:t + 1], std2_ready, NT + t + 1)
        act.wait_ge(logits_ready, NT)
        act.activation(s_e[:, :, :], fill_ps[:, 0, 0:NT * NE].rearrange("p (t e) -> p t e", e=NE), ACT.Exp,
                       scale=-1.0).then_inc(sig_exp, 1)
        act.wait_ge(exp_loaded[0], 16)
        for u in range(RING):
            hi_unit(act, 0, u)
        act.wait_ge(slots_known, 1)
        n = act.value_load(slot_tab[0:1, TAB_N:TAB_N + 1], min_val=NE, max_val=MAX_SLOTS)
        act.activation(zero_a[:, :], eps1[:, :], ACT.Sigmoid).then_inc(table_set, 1)
        act.wait_ge(table_set, 1)
        act.activation(zero_a[:, :], eps1[:, :], ACT.Copy).then_inc(y_slot_kept, 1)
        act.wait_ge(y_slot_kept, 1)
        with act.Fori(0, n) as j:
            act.wait_ge(table_set, j + 1)
            act.activation(zero_a[:, :], eps1[:, :], ACT.Sigmoid).then_inc(table_set, 1)
            b = slot_expert(act, j) % 2
            act.wait_ge(exp_loaded[1], slot_fetched(act, j))
            for u in range(RING):
                act.wait_ge(unit_used, (2 * RING) * j + u + 1)
                hi_unit(act, b, RING + u)
            act.wait_ge(unit_used, (2 * RING) * j + RING)
            act.activation(sig[:, :], zb(0), ACT.Sigmoid).then_inc(gate_sig, 1)
            b = slot_expert(act, j + 1) % 2
            act.wait_ge(exp_loaded[0], slot_fetched(act, j + 1))
            for u in range(RING):
                act.wait_ge(unit_used, (2 * RING) * j + RING + u + 1)
                hi_unit(act, b, u)
            act.wait_ge(down_ready, j + 2)
            act.wait_ge(y_slot_stored, 16 * (j + 1))
            act.activation(y_slot[:, :], z[:, 1024:2048], ACT.Copy).then_inc(y_slot_kept, 1)
        for t in range(NT):
            act.wait_ge(gathered[t], 32)
            act.activation(y_rows[:, t, 0, :], y_rows[:, t, 0, :], ACT.Copy, scale=gates12[:, t, 0:1]).then_inc(y1_ready, 1)
            if t:
                act.wait_ge(x2_ready, t)
                rms(act, x_tok[:, t - 1, :], std2[:, t - 1:t], std3_ready, 2 * NT + t)
        act.wait_ge(x2_ready, NT)
        rms(act, x_tok[:, NT - 1, :], std2[:, NT - 1:NT], std3_ready, 3 * NT)

    def phase_b_dve(dve):
        n_step = [0]

        def step(ins):
            n_step[0] += 1
            ins.then_inc(route_step, 1)
            dve.wait_ge(route_step, n_step[0])

        dve.wait_ge(consts_b, 6)
        dve.wait_ge(rows_loaded, 64)
        for r in range(8):
            kind, part = r // 2, r % 2
            dve.wait_ge(pair_fill, r + 1)
            if kind == 2:
                dve.scalar_tensor_tensor(out=scale2[:, part, :], in0=pair_ps(r), scalar=1.0, in1=g_ffn[:, :],
                                         op0=ALU.add, op1=ALU.mult).then_inc(pair_kept, 1)
            else:
                dst = {0: gate1, 1: shift2, 3: gate2}[kind]
                dve.tensor_copy(dst[:, part, :], pair_ps(r)).then_inc(pair_kept, 1)
        for t in range(NT + 2):
            if t < NT:
                part = t // NTP
                dve.wait_ge(pair_fill, 8 + t + 1)
                if t == 0:
                    dve.wait_ge(pair_kept, 8)
                else:
                    dve.wait_ge(x1_ready, t)
                dve.tensor_tensor(tmp[:, :], proj_ps(t), gate1[:, part, :], ALU.mult).then_inc(pair_kept, 1)
                dve.wait_ge(pair_kept, 9 + t)
                dve.tensor_tensor(x_tok[:, t, :], x_tok[:, t, :], tmp[:, :], ALU.add).then_inc(x1_ready, 1)
            if 1 <= t <= NT:
                u = t - 1
                part = u // NTP
                dve.wait_ge(std2_ready, u + 1)
                step(dve.reciprocal(rstd[:, u:u + 1], std2[:, u:u + 1]))
                step(dve.scalar_tensor_tensor(out=h2_tok[:, u, :], in0=x_tok[:, u, :], scalar=rstd[:, u:u + 1],
                                              in1=scale2[:, part, :], op0=ALU.mult, op1=ALU.mult))
                dve.tensor_tensor(h2_tok[:, u, :], h2_tok[:, u, :], shift2[:, part, :], ALU.add).then_inc(h2_ready, 1)
            if t >= 2:
                u = t - 2
                dve.wait_ge(h2T_mm, u + 1)
                dve.tensor_copy(h_T[:, :, u * P:(u + 1) * P],
                                z[:, 2048:3072].rearrange("p (k c) -> p k c", c=P)).then_inc(h2T_kept, 1)
        dve.wait_ge(sig_exp, 1)
        step(dve.tensor_scalar_add(s_e[:, :, :], s_e[:, :, :], 1.0))
        step(dve.reciprocal(s_e[:, :, :], s_e[:, :, :]))
        step(dve.tensor_tensor(sel[:, :, :], s_e[:, :, :], router_b[:, :].unsqueeze(1).to_broadcast([P, NT, NE]), ALU.add))

        def ranks(v, n, out):
            for j in range(EPG):
                for lo, hi, op in ((0, j, ALU.is_gt), (j + 1, EPG, ALU.is_ge)):
                    if hi > lo:
                        ins = dve.tensor_tensor(cmp4[:, 0:n, lo:hi, j], v[:, :, j:j + 1].to_broadcast([P, n, hi - lo]),
                                                v[:, :, lo:hi], op)
            step(ins)
            step(dve.tensor_reduce(out, cmp4[:, 0:n], AX_X, ALU.add))

        sel4 = sel[:, :, :].rearrange("p t (g i) -> p (t g) i", i=EPG)
        in_top4 = in_top[:, :, :].rearrange("p t (g i) -> p (t g) i", i=EPG)
        tmp4 = r_tmp[:, :, :].rearrange("p t (g i) -> p (t g) i", i=EPG)
        ranks(sel4, NT * NGRP, in_top4)
        step(dve.tensor_scalar(in_top[:, :, :], in_top[:, :, :], 2.0, None, ALU.is_lt))
        step(dve.tensor_tensor(r_tmp[:, :, :], sel[:, :, :], in_top[:, :, :], ALU.mult))
        step(dve.tensor_reduce(g_score[:, :, :].rearrange("p t g -> p (t g)"), tmp4, AX_X, ALU.add))
        ranks(g_score[:, :, :], NT, g_rank[:, :, :])
        step(dve.tensor_scalar(g_rank[:, :, :], g_rank[:, :, :], 1.0, None, ALU.is_lt))
        step(dve.tensor_tensor(in_top4, in_top4,
                               g_rank[:, :, :].rearrange("p t g -> p (t g)").unsqueeze(2).to_broadcast([P, NT * NGRP, EPG]),
                               ALU.mult))
        dve.tensor_copy(chosen_b[:, :, :], in_top[:, :, :]).then_inc(chosen_ready, 1)
        step(dve.tensor_tensor(s_e[:, :, :], s_e[:, :, :], in_top[:, :, :], ALU.mult))
        step(dve.tensor_reduce(tok1[:, :], s_e[:, :, :], AX_X, ALU.add))
        step(dve.reciprocal(tok1[:, :], tok1[:, :]))
        step(dve.tensor_tensor(s_e[:, :, :], s_e[:, :, :], tok1[:, :].unsqueeze(2).to_broadcast([P, NT, NE]), ALU.mult))
        step(dve.tensor_copy(iota_f[:, :], slot_iota[:, :]))
        step(dve.tensor_scalar(limits[:, :], iota_f[:, 0:NT], float(P), None, ALU.mult))
        dve.wait_ge(places_mm, 1)
        step(dve.tensor_copy(count[:, :], fill_ps[:, 1, NT * NE:(NT + 1) * NE]))
        step(dve.tensor_tensor(over[:, :, :], count[:, :].unsqueeze(2).to_broadcast([P, NE, NT]),
                               limits[:, :].unsqueeze(1).to_broadcast([P, NE, NT]), ALU.is_gt))
        step(dve.tensor_reduce(n_slots[:, :], over[:, :, :], AX_X, ALU.add))
        step(dve.tensor_scalar(n_slots[:, :], n_slots[:, :], 1.0, None, ALU.max))
        step(dve.tensor_tensor_scan(slot_end[:, :], ones_e[:, :], n_slots[:, :], 0.0, ALU.mult, ALU.add))
        step(dve.tensor_tensor(base[:, :], slot_end[:, :], n_slots[:, :], ALU.subtract))
        step(dve.tensor_scalar(base[:, :], base[:, :], float(P), None, ALU.mult))
        step(dve.tensor_tensor(rows[:, :, :], fill_ps[:, 1, 0:NT * NE].rearrange("p (t e) -> p t e", e=NE),
                               base[:, :].unsqueeze(1).to_broadcast([P, NT, NE]), ALU.add))
        step(dve.tensor_tensor(rows[:, :, :], rows[:, :, :], in_top[:, :, :], ALU.mult))
        step(dve.tensor_reduce(row_f[:, :, 1], rows[:, :, :], AX_X, ALU.max))
        step(dve.tensor_scalar(r_tmp[:, :, :], in_top[:, :, :], -8192.0, 8192.0, ALU.mult, ALU.add))
        step(dve.tensor_tensor(sel[:, :, :], rows[:, :, :], r_tmp[:, :, :], ALU.add))
        step(dve.tensor_reduce(row_f[:, :, 0], sel[:, :, :], AX_X, ALU.min))
        dve.tensor_copy(row_i[:, :, :], row_f[:, :, :]).then_inc(rows_known, 1)
        step(dve.memset(slot_f[:, TAB_NX:TAB_NX + 1], 0.0))
        step(dve.memset(fetch_w[:, 0:1], 16.0))
        step(dve.tensor_tensor(ended[:, :, :], iota_f[:, :].unsqueeze(2).to_broadcast([P, MAX_SLOTS + 1, NE]),
                               slot_end[:, :].unsqueeze(1).to_broadcast([P, MAX_SLOTS + 1, NE]), ALU.is_ge))
        step(dve.tensor_reduce(slot_f[:, 0:MAX_SLOTS + 1], ended[:, :, :], AX_X, ALU.add))
        step(dve.tensor_scalar(slot_f[:, TAB_NX + 1:TAB_NX + MAX_SLOTS + 2], slot_f[:, 0:MAX_SLOTS + 1], 1.0, float(NE - 1),
                               ALU.add, ALU.min))
        step(dve.tensor_scalar(slot_f[:, 0:MAX_SLOTS + 1], slot_f[:, 0:MAX_SLOTS + 1], float(NE - 1), None, ALU.min))
        step(dve.tensor_copy(slot_f[:, TAB_N:TAB_N + 1], slot_end[:, NE - 1:NE]))
        step(dve.tensor_scalar(fetch_w[:, 1:NE - 1], n_slots[:, 0:NE - 2], 16.0, None, ALU.mult))
        step(dve.tensor_tensor(ended[:, :, 0:NE - 1], ended[:, :, 0:NE - 1],
                               fetch_w[:, :].unsqueeze(1).to_broadcast([P, MAX_SLOTS + 1, NE - 1]), ALU.mult))
        step(dve.tensor_reduce(slot_f[:, TAB_W:TAB], ended[:, :, 0:NE - 1], AX_X, ALU.add))
        step(dve.tensor_scalar(slot_f[:, TAB_W:TAB], slot_f[:, TAB_W:TAB], 16.0, None, ALU.add))
        dve.tensor_copy(slot_tab[:, :], slot_f[:, :]).then_inc(slots_known, 1)
        for r, src in ((0, sel), (1, rows)):
            step(dve.tensor_tensor(r_tmp[:, :, :], src[:, :, :], row_f[:, :, r:r + 1].to_broadcast([P, NT, NE]), ALU.is_equal))
            step(dve.tensor_tensor(r_tmp[:, :, :], r_tmp[:, :, :], s_e[:, :, :], ALU.mult))
            step(dve.tensor_reduce(gates12[:, :, r], r_tmp[:, :, :], AX_X, ALU.add))

        dve.wait_ge(slots_known, 1)
        n = dve.value_load(slot_tab[0:1, TAB_N:TAB_N + 1], min_val=NE, max_val=MAX_SLOTS)

        def keep_slotT(j):
            dve.wait_ge(x_slotT_mm, j + 1)
            rows_T = z[:, 2048:3072].rearrange("p (k c) -> p k c", c=P)
            dve.tensor_copy(x_slotT_hi[:, :, :], rows_T).then_inc(x_hi_ready, 1)
            dve.wait_ge(x_hi_ready, j + 1)
            dve.tensor_tensor(x_slotT_lo[:, :, :], rows_T, x_slotT_hi[:, :, :].bitcast(F32),
                              ALU.subtract).then_inc(x_slotT_kept, 1)

        for u in range(RING):
            dve.wait_ge(hi_ready, u + 1)
            lo_unit(dve, 0, u)
        dve.wait_ge(scattered, 16 * 2 * NT)
        dve.tensor_copy(zero_f[:, :], eps1[:, :]).then_inc(hid_ready, 1)
        keep_slotT(0)
        with dve.Fori(0, n) as j:
            b = slot_expert(dve, j) % 2
            for u in range(RING):
                dve.wait_ge(hi_ready, (2 * RING) * j + RING + u + 1)
                lo_unit(dve, b, RING + u)
            dve.wait_ge(gate_sig, j + 1)
            dve.tensor_tensor(sig[:, :], sig[:, :], zb(0), ALU.mult).then_inc(sig_step, 1)
            dve.wait_ge(sig_step, j + 1)
            dve.wait_ge(unit_used, (2 * RING) * (j + 1))
            dve.tensor_tensor(hid[:, :], sig[:, :], zb(1), ALU.mult).then_inc(hid_ready, 1)
            dve.wait_ge(hidT_mm, j + 1)
            dve.tensor_copy(hidT[:, :, :], fill_ps[:, 0, :].rearrange("p (k c) -> p k c", c=P)).then_inc(hidT_kept, 1)
            keep_slotT(j + 1)
            b = slot_expert(dve, j + 1) % 2
            for u in range(RING):
                dve.wait_ge(hi_ready, (2 * RING) * (j + 1) + u + 1)
                lo_unit(dve, b, u)

        dve.wait_ge(rows_loaded, 80)
        for t in range(NT + 1):
            if t < NT:
                part = t // NTP
                dve.wait_ge(y1_ready, t + 1)
                step(dve.scalar_tensor_tensor(out=y_rows[:, t, 0, :], in0=y_rows[:, t, 1, :], scalar=gates12[:, t, 1:2],
                                              in1=y_rows[:, t, 0, :], op0=ALU.mult, op1=ALU.add))
                step(dve.tensor_tensor(y_rows[:, t, 0, :], y_rows[:, t, 0, :], gate2[:, part, :], ALU.mult))
                dve.tensor_tensor(x_tok[:, t, :], x_tok[:, t, :], y_rows[:, t, 0, :], ALU.add).then_inc(x2_ready, 1)
            if t:
                u = t - 1
                dve.wait_ge(std3_ready, u + 1)
                step(dve.reciprocal(rstd[:, u:u + 1], std2[:, u:u + 1]))
                dve.scalar_tensor_tensor(out=y_rows[:, u, 0, :], in0=x_tok[:, u, :], scalar=rstd[:, u:u + 1],
                                         in1=g_fin, op0=ALU.mult, op1=ALU.mult).then_inc(y_ready, 1)

    def pair_ps(r):
        return z[:, 1024 * (r % 3):1024 * (r % 3) + 1024]

    def proj_ps(t):
        return z[:, 1024 * (t % 2):1024 * (t % 2) + 1024]

    def phase_b_pe(pe):
        def acc(out, lhsT, rhs, start=False, stop=False):
            return pe.matmul(out, lhsT, rhs, start=start, stop=stop, skip_group_check=True)

        pe.wait_ge(rows_loaded, 64)
        pe.wait_ge(ada_kept, 4 + NPAIR)
        pe.wait_ge(o_kept, 1 + NPAIR)
        for r in range(8):
            kind, part = r // 2, r % 2
            if r >= 3:
                pe.wait_ge(pair_kept, r - 2)
            for c in range(2):
                out = pair_ps(r)[:, 512 * c:512 * c + 512]
                acc(out, sel_tok[:, part, :], mod_rows[:, 2 * kind + c, :], start=True)
                mm = acc(out, ones_row[:, :], ada_b_row[:, (2 * kind + c) * ADW:(2 * kind + c + 1) * ADW], stop=True)
            mm.then_inc(pair_fill, 1)
        pe.wait_ge(wo_loaded, 16)
        def project_out(t):
            pe.wait_ge(pair_kept, 8 + max(t - 1, 0))
            for c in range(2):
                out = proj_ps(t)[:, 512 * c:512 * c + 512]
                for k in range(NPAIR):
                    mm = acc(out, o_T[:, k, t * P:(t + 1) * P], w_o[:, k, 512 * c:512 * c + 512],
                             start=(k == 0), stop=(k == NPAIR - 1))
            mm.then_inc(pair_fill, 1)

        def turn_h2(u):
            pe.wait_ge(h2_ready, u + 1)
            pe.wait_ge(h2T_kept, u)
            for k in range(KD):
                mm = pe.transpose(z[:, 2048 + k * P:2048 + (k + 1) * P], h2_tok[:, u, k * P:(k + 1) * P], ident[:, :])
            mm.then_inc(h2T_mm, 1)

        def route(u):
            pe.wait_ge(h2T_kept, u + 1)
            for k in range(KD):
                mm = acc(fill_ps[:, 0, NE * u:NE * (u + 1)], h_T[:, k, u * P:(u + 1) * P], router_w[:, k, :],
                         start=(u == 0 and k == 0), stop=(k == KD - 1))
            mm.then_inc(logits_ready, 1)

        for t in range(NT + 3):
            if t < NT:
                project_out(t)
            if 2 <= t < NT + 2:
                turn_h2(t - 2)
            if t >= 3:
                route(t - 3)
        pe.wait_ge(chosen_ready, 1)
        for t in range(NT + 1):
            for u in range(min(t, NT - 1) + 1):
                mm = acc(fill_ps[:, 1, NE * t:NE * (t + 1)], before_b[:, :] if u == t else ones_b[:, :],
                         chosen_b[:, u, :], start=(t == 0), stop=(u == min(t, NT - 1)))
        mm.then_inc(places_mm, 1)

        def turn_slot(j):
            pe.wait_ge(x_slot_loaded, 16 * (j + 1))
            for k in range(KD):
                mm = pe.transpose(z[:, 2048 + k * P:2048 + (k + 1) * P], x_slot[:, k * P:(k + 1) * P], ident[:, :])
            mm.then_inc(x_slotT_mm, 1)

        turn_slot(0)
        pe.transpose(fill_ps[:, 0, 0:P], ident[:, :], ident[:, :]).then_inc(down_ready, 1)
        pe.wait_ge(slots_known, 1)
        n = pe.value_load(slot_tab[0:1, TAB_N:TAB_N + 1], min_val=NE, max_val=MAX_SLOTS)
        with pe.Fori(0, n) as j:
            b = slot_expert(pe, j) % 2
            fetched = slot_fetched(pe, j)
            pe.wait_ge(x_slotT_kept, j + 1)
            pe.wait_ge(hid_ready, j + 1)
            for i in range(2):
                for u in range(RING):
                    pe.wait_ge(lo_ready, (2 * RING) * j + i * RING + u + 1)
                    for k in range(UK * u, UK * (u + 1)):
                        cols = slice((k - UK * u) * FE, (k - UK * u + 1) * FE)
                        acc(zb(i), x_slotT_hi[:, k, :], w_hi[:, u, cols], start=(k == 0))
                        acc(zb(i), x_slotT_hi[:, k, :], w_lo[:, u, cols])
                        mm = acc(zb(i), x_slotT_lo[:, k, :], w_hi[:, u, cols], stop=(k == KD - 1))
                    mm.then_inc(unit_used, 1)
            turn_slot(j + 1)
            pe.wait_ge(hid_ready, j + 2)
            for k in range(KF):
                mm = pe.transpose(fill_ps[:, 0, k * P:(k + 1) * P], hid[:, k * P:(k + 1) * P], ident[:, :])
            mm.then_inc(hidT_mm, 1)
            pe.wait_ge(hidT_kept, j + 1)
            pe.wait_ge(exp_loaded[2], fetched)
            pe.wait_ge(y_slot_kept, j + 1)
            for c in range(2):
                for k in range(KF):
                    mm = acc(zb(2 + c), hidT[:, k, :],
                             exp_w[:, bass.ds(b, 1), 8192 + k * D + c * 512:8192 + k * D + (c + 1) * 512],
                             start=(k == 0), stop=(k == KF - 1))
            mm.then_inc(down_ready, 1)

    FILLS = 11

    block = ctx.enter_context(nc.Block())

    @block.sync
    def _(sp):
        sp.dma_start(c_rows[0:1, :], io["c_prompt"]).then_inc(c_loaded, 16)
        sp.dma_start(c_rows[1:NC, :], io["c_sample"]).then_inc(c_loaded, 16)
        sp.dma_start(in_rows[0:6 * KD, :], io["ada_b"].rearrange("o (k p) -> (o k) p", p=P)).then_inc(c_loaded, 16)
        sp.dma_start(in_rows[6 * KD:7 * KD, :], io["norm_mix_g"].rearrange("o (k p) -> (o k) p", p=P)).then_inc(c_loaded, 16)
        sp.dma_start(in_rows[7 * KD:8 * KD, :], io["norm_ffn_g"].rearrange("o (k p) -> (o k) p", p=P)).then_inc(c_loaded, 16)
        sp.dma_start(x_tok[:, 0:NTP, :], xp_v).then_inc(x_loaded, 16)
        sp.dma_start(x_tok[:, NTP, :], xs_v).then_inc(x_loaded, 16)
        for j in range(3):
            sp.dma_start(ada_w[:, j], ada_v[:, :, j * ADW:(j + 1) * ADW]).then_inc(ada_loaded[j], 16)
        sp.wait_ge(ada_mm, 1)
        sp.dma_start(ada_w[:, 0], ada_v[:, :, 3 * ADW:4 * ADW]).then_inc(ada_loaded[0], 16)

        def load_pair(p, first):
            for c in range(3):
                if not first:
                    sp.wait_ge(fill_ready, (p - 1) * FILLS + 2 * c + 2)
                sp.dma_start(w_pair[:, c], qkv_v[:, :, bass.ds(p * P + c * D, P)]).then_inc(wqkv_loaded[c], 16)
            if not first:
                sp.wait_ge(fill_ready, (p - 1) * FILLS + 8)
            sp.dma_start(past_k[:, :, :], ck_v[:, :, bass.ds(p * P, P)]).then_inc(past_k_loaded, 16)

        def store_pair(p):
            sp.wait_ge(fill_kept, (p + 1) * FILLS)
            c = bass.ds(p * P, P)
            sp.dma_start(kp_v[:, :, c], k_tok[:, 0:NTP, :]).then_inc(kv_stored, 16)
            sp.dma_start(vp_v[:, :, c], v_tok[:, 0:NTP, :]).then_inc(kv_stored, 16)
            sp.dma_start(ks_v[:, c], k_tok[:, NTP, :]).then_inc(kv_stored, 16)
            sp.dma_start(vs_v[:, c], v_tok[:, NTP, :]).then_inc(kv_stored, 16)

        load_pair(0, True)
        sp.dma_start(past_v[:, :, :], cv_v[:, :, 0:P]).then_inc(past_v_loaded, 16)
        sp.wait_ge(ada_mm, 4)
        sp.dma_start(ada_w[:, 0], ada_v[:, :, 4 * ADW:5 * ADW]).then_inc(ada_loaded[0], 16)
        sp.dma_start(w_o, wo_v).then_inc(wo_loaded, 16)
        sp.dma_start(slots_out_z[:, 0:2, :], zero_rows(1)).then_inc(y_slot_stored, 16)
        with sp.Fori(0, NPAIR - 1) as p:
            load_pair(p + 1, False)
            sp.dma_start(slots_in_z[:, bass.ds(p * 2 * ZIN, 2 * ZIN), :], zero_rows(ZIN)).then_inc(zeros_stored, 16)
            sp.dma_start(slots_out_z[:, bass.ds(p * 2 * ZOUT + 2, 2 * ZOUT), :], zero_rows(ZOUT)).then_inc(zeros_stored, 16)
            store_pair(p)
            sp.wait_ge(o_ready, p + 1)
            sp.dma_start(past_v[:, :, :], cv_v[:, :, bass.ds((p + 1) * P, P)]).then_inc(past_v_loaded, 16)
            sp.wait_ge(ada_mm, p + 5)
            sp.dma_start(ada_w[:, 0], ada_v[:, :, bass.ds((p + 5) * ADW, ADW)]).then_inc(ada_loaded[0], 16)
        store_pair(NPAIR - 1)
        phase_b_sync(sp)

    @block.gpsimd
    def _(pool):
        pool.memset(ident[:, :], 0.0).then_inc(consts_set, 1)
        pool.memset(sum_sel[:, :], 0.0).then_inc(consts_set, 1)
        pool.memset(sel_tok[:, :, :], 0.0).then_inc(consts_set, 1)
        pool.memset(ntri[:, :], -1.0).then_inc(consts_set, 1)
        pool.memset(nones[:, :], -1.0).then_inc(consts_set, 1)
        pool.memset(ones_row[:, :], 1.0).then_inc(consts_set, 1)
        pool.memset(eps1[:, :], EPS).then_inc(consts_set, 1)
        pool.memset(zeros[:, :], 0.0).then_inc(consts_set, 1)
        pool.memset(q_z[:, :, :], 0.0).then_inc(consts_set, 1)
        pool.memset(c_T[:, :, :], 0.0).then_inc(consts_set, 1)
        pool.wait_ge(consts_set, 10)
        pool.affine_select(out=ident[:, :], in_=ident[:, :], compare_op=ALU.not_equal, fill=1.0, base=0,
                           pattern=[[-1, P]], channel_multiplier=1).then_inc(consts_set, 1)
        pool.affine_select(out=ntri[:, :], in_=ntri[:, :], compare_op=ALU.is_ge, fill=0.0, base=0,
                           pattern=[[-1, P]], channel_multiplier=1).then_inc(consts_set, 1)
        for g in range(NG4):
            pool.wait_ge(consts_set, 12 + 3 * g)
            pool.affine_select(out=sum_sel[:, :], in_=sum_sel[:, :], compare_op=ALU.not_equal, fill=1.0,
                               base=-CW * g, pattern=[[-1, NC]], channel_multiplier=1).then_inc(consts_set, 1)
            pool.affine_select(out=sel_tok[:, 0, :], in_=sel_tok[:, 0, :], compare_op=ALU.not_equal, fill=1.0,
                               base=-CW * g, pattern=[[0, P]], channel_multiplier=1).then_inc(consts_set, 1)
            pool.affine_select(out=sel_tok[:, 1, :], in_=sel_tok[:, 1, :], compare_op=ALU.not_equal, fill=1.0,
                               base=-CW * g - 1, pattern=[[-1, NS], [0, SS]],
                               channel_multiplier=1).then_inc(consts_set, 1)

        def causal(buf):
            for first, step, n in ((0, 512, 4), (1408, 512, 2), (2048, 256, 3), (2688, 128, 1)):
                v = buf[:, first:first + P] if n == 1 else blocks_of(buf, first, step, n)
                yield pool.affine_select(out=v, in_=v, compare_op=ALU.is_gt, fill=0.0, base=0,
                                         pattern=[[0, n], [1, P]] if n > 1 else [[1, P]],
                                         channel_multiplier=-1)

        def mask(buf, done, count):
            for ins in causal(buf):
                last = ins
            last.then_inc(done, 1)
            pool.wait_ge(done, count)
            pool.nop(nofuse=True)
            v = buf[:, 2560:2816].rearrange("p (a s q) -> p a s q", a=2, s=NS)
            pool.affine_select(out=v, in_=v, compare_op=ALU.is_ge, fill=0.0, base=0,
                               pattern=[[0, 2], [-SS, NS], [0, SS]], channel_multiplier=1).then_inc(done, 1)

        with pool.Fori(0, NPAIR) as p:
            pool.wait_ge(sp_ready, p + 1)
            pool.nop(nofuse=True)
            mask(ew_sp, sp_masked, 2 * p + 1)
            pool.wait_ge(w_ready, p + 1)
            pool.nop(nofuse=True)
            mask(ew_w, w_masked, 2 * p + 1)
        phase_b_pool(pool)

    @block.scalar
    def _(act):
        act.wait_ge(c_loaded, 80)
        act.activation(c_tmp[0:NC, :], c_rows[0:NC, :], ACT.Exp, scale=-1.0).then_inc(silu_exp, 1)
        act.wait_ge(x_loaded, 32)
        for t in range(NT):
            act.activation(x_sq, x_tok[:, t, :], ACT.Square, accum_out=rstd[:, t:t + 1]).then_inc(sq_ready, 1)
            act.wait_ge(sq_ready, t + 1)
        act.wait_ge(consts_set, 10)
        act.activation(rstd[:, :], rstd[:, :], ACT.Sqrt, scale=1.0 / D, bias=eps1[:, 0:1]).then_inc(std_ready, 1)
        for t in range(NT):
            act.wait_ge(rstd_ready, 1)
            act.activation(xs[t], x_tok[:, t, :], ACT.Copy, scale=rstd[:, t:t + 1]).then_inc(xs_ready, 1)
        with act.Fori(0, NPAIR) as p:
            act.wait_ge(abs_ready, p + 1)
            act.activation(ew_t[:, :], ew_t[:, :], ACT.Exp, scale=-1.0).then_inc(exp_ready, 1)
            act.wait_ge(exp_ready, p + 1)
            act.activation(ew_t[:, :], ew_t[:, :], ACT.Ln, bias=1.0).then_inc(ln_ready, 1)
            act.wait_ge(logw_ready, p + 1)
            act.activation(ew_w[:, :], z[:, :], ACT.Exp).then_inc(w_ready, 1)
        phase_b_act(act)

    @block.vector
    def _(dve):
        dve.wait_ge(silu_exp, 1)
        dve.tensor_scalar_add(c_tmp[0:NC, :], c_tmp[0:NC, :], 1.0).then_inc(small_dve, 1)
        dve.wait_ge(small_dve, 1)
        dve.reciprocal(c_tmp[0:NC, :], c_tmp[0:NC, :]).then_inc(small_dve, 1)
        dve.wait_ge(small_dve, 2)
        dve.tensor_tensor(c_rows[0:NC, :], c_rows[0:NC, :], c_tmp[0:NC, :], ALU.mult).then_inc(silu_ready, 1)
        dve.wait_ge(std_ready, 1)
        dve.reciprocal(rstd[:, :], rstd[:, :]).then_inc(rstd_ready, 1)
        dve.wait_ge(setup_T, 1)
        dve.wait_ge(consts_set, 10)
        dve.tensor_copy(c_T[:, :, 0:NC], fill_ps[:, 0, 0:KD * NC].rearrange("p (k c) -> p k c", c=NC)).then_inc(setup_T_used, 1)
        dve.tensor_copy(ada_bT[:, :], fill_ps[:, 0, 128:128 + 6 * KD]).then_inc(setup_T_used, 1)
        dve.tensor_copy(norm_gT[:, :], fill_ps[:, 0, 128 + 6 * KD:128 + 8 * KD]).then_inc(setup_T_used, 1)
        for j in range(4):
            dve.wait_ge(ada_mm, j + 1)
            dve.tensor_copy(mod_rows[:, j, :], fill_ps[:, j % 2, :]).then_inc(ada_kept, 1)
        dve.wait_ge(mod_T_mm, 1)
        dve.tensor_tensor(mod_T[:, :, :], fill_ps[:, 0, 0:2 * KD * NC].rearrange("p (k c) -> p k c", c=NC),
                          ada_bT[:, 0:2 * KD].unsqueeze(2).to_broadcast([P, 2 * KD, NC]), ALU.add).then_inc(small_dve, 1)
        dve.wait_ge(small_dve, 3)
        dve.scalar_tensor_tensor(out=scale_T[:, :, :], in0=mod_T[:, KD:2 * KD, :], scalar=1.0,
                                 in1=norm_gT[:, 0:KD].unsqueeze(2).to_broadcast([P, KD, NC]),
                                 op0=ALU.add, op1=ALU.mult).then_inc(modT_ready, 1)
        dve.wait_ge(modT_ready, 1)
        for k in range(KD):
            dve.wait_ge(xsT_ready, k + 1)
            dve.tensor_scalar(h_T[:, k, 0:SEQ], zb(k % 6), scale_T[:, k, 0:1], mod_T[:, k, 0:1],
                              ALU.mult, ALU.add).then_inc(hT_ready, 1)
        for a in range(2):
            ks = slice(4 * a, 4 * a + 4)
            hs = h_T[:, ks, SEQ:TOK]
            dve.wait_ge(xsT_ready, KD + 1 + a)
            for k in range(4 * a, 4 * a + 4):
                hv = h_T[:, k, SEQ:TOK].rearrange("p (s q) -> p s q", q=SS)
                src = zb(2 + a, 128 * (k % 4), 128 * (k % 4) + 128).rearrange("p (s q) -> p s q", q=SS)
                dve.tensor_tensor(hv, src, scale_T[:, k, 1:NC].unsqueeze(2).to_broadcast([P, NS, SS]),
                                  ALU.mult).then_inc(hT_ready, 1)
        for k in range(KD):
            hv = h_T[:, k, SEQ:TOK].rearrange("p (s q) -> p s q", q=SS)
            dve.wait_ge(hT_ready, KD + k + 1)
            dve.tensor_tensor(hv, hv, mod_T[:, k, 1:NC].unsqueeze(2).to_broadcast([P, NS, SS]),
                              ALU.add).then_inc(hT_ready, 1)

        def keep(p, f):
            dve.wait_ge(fill_ready, p * FILLS + f + 1)
            src = fill_ps[:, f % 2, :]
            n, a = (512, 0) if f % 2 == 0 else (P, SEQ)
            if f < 2:
                dve.tensor_scalar(q_z[0:HD, 0, a:a + n], src[0:HD, 0:n], SCALE, None, ALU.mult)
                ins = dve.tensor_scalar(q_z[HD:P, 1, a:a + n], src[HD:P, 0:n], SCALE, None, ALU.mult)
            elif f < 4:
                ins = dve.tensor_copy(k_T[:, a:a + n], src[:, 0:n])
            elif f < 6:
                ins = dve.tensor_copy(v_T[:, a:a + n], src[:, 0:n])
            elif f < 8:
                ins = dve.tensor_copy(past_kT[:, 4 * (f - 6):4 * (f - 6) + 4, :], src.rearrange("p (s k) -> p s k", k=P))
            elif f == 8:
                ins = dve.tensor_copy(k_tok[:, 0:NTP, :], src.rearrange("p (s k) -> p s k", k=P))
            elif f == 9:
                ins = dve.tensor_copy(v_tok[:, 0:NTP, :], src.rearrange("p (s k) -> p s k", k=P))
            elif f == 10:
                dve.tensor_copy(k_tok[:, NTP, :], src[:, 0:P])
                ins = dve.tensor_copy(v_tok[:, NTP, :], src[:, P:2 * P])
            ins.then_inc(fill_kept, 1)

        def attend(p, more):
            dve.wait_ge(z_ready, p + 1)
            dve.tensor_scalar(ew_t[:, :].bitcast(I32), z[:, :].bitcast(I32), 0x7FFFFFFF, None,
                              ALU.bitwise_and).then_inc(abs_ready, 1)
            if more:
                keep(p + 1, 0)
                keep(p + 1, 1)
            dve.wait_ge(ln_ready, p + 1)
            dve.scalar_tensor_tensor(out=ew_sp[:, :], in0=z[:, :], scalar=0.0, in1=ew_t[:, :],
                                     op0=ALU.max, op1=ALU.add).then_inc(sp_ready, 1)
            if more:
                for f in range(2, 8):
                    keep(p + 1, f)
            dve.wait_ge(o_ready, p + 1)
            dve.tensor_copy(o_T[:, bass.ds(p, 1), 0:SEQ], zb(0).unsqueeze(1))
            dve.tensor_copy(o_T[:, bass.ds(p, 1), SEQ:TOK], zb(1, 0, P).unsqueeze(1)).then_inc(o_kept, 1)
            if more:
                dve.wait_ge(kv_stored, 64 * (p + 1))
                for f in range(8, 11):
                    keep(p + 1, f)
            dve.wait_ge(ada_mm, p + 5)
            dve.tensor_copy(mod_rows[:, bass.ds(p, 1), :], fill_ps[:, 1, :].unsqueeze(1)).then_inc(ada_kept, 1)

        for f in range(11):
            keep(0, f)
        dve.tensor_copy(zero_f[:, :], eps1[:, :]).then_inc(o_kept, 1)
        with dve.Fori(0, NPAIR - 1) as p:
            attend(p, True)
        attend(NPAIR - 1, False)
        phase_b_dve(dve)

    @block.tensor
    def _(pe):
        def ada_slice(src, out):
            for k in range(KD):
                g = k % NG4
                mm = pe.matmul(out[CW * g:CW * g + CW, :], c_T[:, k, :], src[:, k, :],
                               start=(k < NG4), stop=(k >= NG4), skip_group_check=True)
            return mm

        def transposes(srcs, out):
            for i, s in enumerate(srcs):
                mm = pe.transpose(out[:, i * P:(i + 1) * P], s, ident[:, :])
            return mm

        pe.wait_ge(consts_set, 12 + 3 * NG4)
        pe.wait_ge(c_loaded, 80)
        pe.wait_ge(silu_ready, 1)
        for k in range(KD):
            pe.transpose(fill_ps[:, 0, k * NC:(k + 1) * NC], c_rows[0:NC, k * P:(k + 1) * P], ident[0:NC, 0:NC])
        pe.transpose(fill_ps[:, 0, 128:128 + 64], in_rows, ident[0:64, 0:64]).then_inc(setup_T, 1)
        pe.wait_ge(xs_ready, NT)
        for k in range(6):
            transposes([xs[t][:, k * P:(k + 1) * P] for t in range(NTP)], zb(k)).then_inc(xsT_ready, 1)
        pe.wait_ge(setup_T_used, 3)
        for j in range(4):
            pe.wait_ge(ada_loaded[j % 3], 16 * (1 + j // 3))
            if j >= 2:
                pe.wait_ge(ada_kept, j - 1)
            ada_slice(ada_w[:, j % 3], fill_ps[:, j % 2, :]).then_inc(ada_mm, 1)
        pe.wait_ge(ada_kept, 4)
        for k in range(2 * KD):
            mm = pe.matmul(fill_ps[:, 0, k * NC:(k + 1) * NC],
                           mod_rows[:, k // 4, (k % 4) * P:(k % 4 + 1) * P], sum_sel[:, :],
                           start=(k == 0), stop=True, skip_group_check=True)
        mm.then_inc(mod_T_mm, 1)
        for k in (6, 7):
            pe.wait_ge(hT_ready, k - 5)
            transposes([xs[t][:, k * P:(k + 1) * P] for t in range(NTP)], zb(k % 6)).then_inc(xsT_ready, 1)
        for a in range(2):
            pe.wait_ge(hT_ready, 3 + a)
            transposes([xs[NTP][:, k * P:(k + 1) * P] for k in range(4 * a, 4 * a + 4)],
                       zb(2 + a)).then_inc(xsT_ready, 1)

        def project(p, f, first=False):
            out = fill_ps[:, f % 2, :]
            if f == 0 and not first:
                pe.wait_ge(fill_kept, p * FILLS)
            elif f == 1 and not first:
                pe.wait_ge(ada_kept, p + 3)
            elif f >= 2:
                pe.wait_ge(fill_kept, p * FILLS + f - 1)
            if f < 6:
                c, a, n = f // 2, (f % 2) * SEQ, (SEQ, P)[f % 2]
                if f % 2 == 0:
                    pe.wait_ge(wqkv_loaded[c], 16 * (p + 1))
                for k in range(KD):
                    mm = pe.matmul(out[:, 0:n], w_pair[:, c, k, :], h_T[:, k, a:a + n],
                                   start=(k == 0), stop=(k == KD - 1))
            elif f < 8:
                pe.wait_ge(past_k_loaded, 16 * (p + 1))
                mm = transposes([past_k[:, s, :] for s in range(4 * (f - 6), 4 * (f - 6) + 4)], out)
            elif f < 10:
                pe.wait_ge(fill_kept, p * FILLS + 6)
                src = (k_T, v_T)[f - 8]
                mm = transposes([src[:, t * P:(t + 1) * P] for t in range(NTP)], out)
            else:
                mm = transposes([k_T[:, SEQ:TOK], v_T[:, SEQ:TOK]], out)
            mm.then_inc(fill_ready, 1)

        def acc(out, lhsT, rhs, start=False, stop=False):
            return pe.matmul(out, lhsT, rhs, start=start, stop=stop, skip_group_check=True)

        def scores(p):
            pe.wait_ge(fill_kept, p * FILLS + 8)
            pe.wait_ge(o_kept, p + 1)
            for h in range(2):
                acc(zb(h), k_T[:, 0:P], q_z[:, h, 0:SEQ], start=True)
                acc(zb(2 + h, 0, 384), k_T[:, P:2 * P], q_z[:, h, P:SEQ], start=True)
                acc(zb(2 + h, 384, 512), k_T[:, 3 * P:4 * P], q_z[:, h, 3 * P:SEQ])
            acc(zb(4), k_T[:, 2 * P:3 * P], q_z[:, :, 2 * P:SEQ], start=True)
            acc(zb(5, 0, 256), k_T[:, SEQ:TOK], q_z[:, :, SEQ:TOK], start=True)
            past = zb(5, 256, 512).rearrange("p (h s q) -> p h s q", h=2, s=NS)
            for s in range(NS):
                mm = acc(past[:, :, s, :], past_kT[:, s, :], q_z[:, :, SEQ + SS * s:SEQ + SS * (s + 1)])
            mm.then_inc(z_ready, 1)

        def keep_sums(p):
            pe.wait_ge(sp_masked, 2 * p + 2)
            for b in range(6):
                acc(zb(b), ntri[:, :], ew_sp[:, 512 * b:512 * b + 512])
            for h in range(2):
                k1, k2, k3 = 1024 + 512 * h, 2048 + 256 * h, 1408 + 512 * h
                for dst, src, n in ((512 * h + 128, k1, 384), (512 * h + 256, k2, 256), (512 * h + 384, k3, 128),
                                    (k1 + 128, k2, 256), (k1 + 256, k3, 128), (k2 + 128, k3, 128)):
                    acc(z[:, dst:dst + n], nones[:, :], ew_sp[:, src:src + n])
            acc(zb(5, 256, 512), nones[:, :], ew_sp[:, 2560:2816], stop=True).then_inc(logw_ready, 1)

        def values(p):
            pe.wait_ge(w_masked, 2 * p + 2)
            pe.wait_ge(past_v_loaded, 16 * (p + 1))
            pe.wait_ge(fill_kept, (p + 1) * FILLS)
            for kb in range(NTP):
                for h in range(2):
                    src = (512 * h, 1024 + 512 * h, 2048 + 256 * h, 1408 + 512 * h)[kb]
                    n = SEQ - kb * P
                    acc(z[HD * h:HD * h + HD, kb * P:SEQ], v_tok[:, kb, HD * h:HD * h + HD],
                        ew_w[:, src:src + n], start=(kb == 0))
            for h in range(2):
                acc(z[HD * h:HD * h + HD, 512:640], v_tok[:, NTP, HD * h:HD * h + HD],
                    ew_w[:, 2560 + P * h:2688 + P * h], start=True)
            for s in range(NS):
                for h in range(2):
                    c = 2816 + P * h + SS * s
                    mm = acc(z[HD * h:HD * h + HD, 512 + SS * s:512 + SS * (s + 1)],
                             past_v[:, s, HD * h:HD * h + HD], ew_w[:, c:c + SS])
            mm.then_inc(o_ready, 1)

        def attend(p, more):
            scores(p)
            if more:
                for f in range(4):
                    project(p + 1, f)
            keep_sums(p)
            if more:
                for f in range(4, 8):
                    project(p + 1, f)
            values(p)
            if more:
                for f in range(8, 11):
                    project(p + 1, f)
            pe.wait_ge(ada_loaded[0], 16 * (p + 3))
            if more:
                pe.wait_ge(fill_kept, (p + 1) * FILLS + 10)
            else:
                pe.wait_ge(ada_kept, p + 4)
            ada_slice(ada_w[:, 0], fill_ps[:, 1, :]).then_inc(ada_mm, 1)

        pe.wait_ge(hT_ready, KD + 2 * KD)
        for f in range(11):
            project(0, f, first=True)
        with pe.Fori(0, NPAIR - 1) as p:
            attend(p, True)
        attend(NPAIR - 1, False)
        phase_b_pe(pe)


_INS = ["x_prompt", "x_sample", "cache_sb_k", "cache_sb_v", "c_prompt", "c_sample", "ada_w", "ada_b",
        "norm_mix_g", "norm_ffn_g", "final_norm_g", "sb_w_qkv", "sb_w_o", "router_w", "router_bias",
        "exp_w_gate", "exp_w_up", "exp_w_down"]
_OUTS = {"y_prompt": (1, SEQ, D), "y_sample": (NS, SS, D), "k_prompt": (1, SEQ, H, HD), "v_prompt": (1, SEQ, H, HD),
         "k_sample": (NS, SS, H, HD), "v_sample": (NS, SS, H, HD)}


def kernel(**inputs):
    import numpy as _np
    import concourse.bacc as _bacc
    from concourse.bass_utils import run_bass_kernel_spmd as _run

    nc = _bacc.Bacc("TRN2", target_bir_lowering=False, num_devices=1)
    arrays, io = {}, {}
    for name in _INS:
        a = _np.ascontiguousarray(inputs[name])
        arrays[f"in_{name}"] = a
        io[name] = nc.dram_tensor(f"in_{name}", a.shape, mybir.dt.from_np(a.dtype), kind="ExternalInput").ap()
    for name, shape in _OUTS.items():
        io[name] = nc.dram_tensor(f"out_{name}", shape, F32, kind="ExternalOutput").ap()
    stream_step(nc, io)
    r = _run(nc, [arrays], core_ids=[0])
    got = tuple(r.results[0][f"out_{name}"] for name in _OUTS)
    return got + (None, None, None, None)
```

```python
from contextlib import ExitStack

import concourse.bass as bass
from concourse import mybir

F32 = mybir.dt.float32
I32 = mybir.dt.int32
BF16 = mybir.dt.bfloat16
F32R = mybir.dt.float32r
ALU = mybir.AluOpType
ACT = mybir.ActivationFunctionType
AX_X = mybir.AxisListType.X

P = 128
D = 1024
KD = D // P
SEQ = 512
NS = 8
SS = 16
NSAM = NS * SS
TOK = SEQ + NSAM
NT = TOK // P
NTP = SEQ // P
NC = 1 + NS
H = 16
HD = 64
NPAIR = H // 2
CW = 32
NG4 = P // CW
ADW = 512
BIAS_ROW = CW - 1
NE = 16
NGRP = 4
EPG = NE // NGRP
FE = 512
KF = FE // P
EPS = 1e-6
SCALE = HD ** -0.5


def stream_step(nc, io):
    with ExitStack() as ctx:
        build(nc, io, ctx)


def build(nc, io, ctx):
    def sb(name, shape, dt=F32, c=ctx):
        return c.enter_context(nc.sbuf_tensor(name, shape, dt))

    def next_place():
        return -(-nc.sbuf_base // 32) * 32

    def sem(name):
        return ctx.enter_context(nc.semaphore(name))

    x_tok = sb("x_tok", [P, NT, D])
    h_T_at = next_place()
    h_T = sb("h_T", [P, KD, TOK])
    ident = sb("ident", [P, P])
    sum_sel = sb("sum_sel", [P, NC])
    sel_tok_at = next_place()
    sel_tok = sb("sel_tok", [P, 2, P])
    sel_tok_r = nc.alloc_sbuf_tensor_at("sel_tok_r", [P, 2, P], F32R, offset=sel_tok_at, align_bytes=32)
    mod_T = sb("mod_T", [P, 2 * KD, NC])
    ada_bT = sb("ada_bT", [P, 6 * KD])
    norm_gT = sb("norm_gT", [P, 2 * KD])
    scale_T = sb("scale_T", [P, KD, NC])
    rstd = sb("rstd", [P, NT])
    eps1 = sb("eps1", [P, 1])
    zero_f = sb("zero_f", [P, 1])
    zero_a = sb("zero_a", [P, 1])

    phase_a = ExitStack()
    o_T_at = next_place()
    o_T = sb("o_T", [P, NPAIR, TOK], c=phase_a)
    mod_rows_at = next_place()
    mod_rows = sb("mod_rows", [P, 8, ADW], c=phase_a)
    ada_w_at = next_place()
    ada_w = sb("ada_w", [P, 3, KD, ADW], c=phase_a)
    w_pair_at = next_place()
    w_pair = sb("w_pair", [P, 3, KD, P], c=phase_a)
    wp_lo = nc.alloc_sbuf_tensor_at("wp_lo", [P, 3, KD, P], F32R, offset=w_pair_at, align_bytes=32)
    wp_hi = nc.alloc_sbuf_tensor_at("wp_hi", [P, 3, KD, P], F32R, offset=ada_w_at + 4 * KD * ADW, align_bytes=32)
    o_lo = nc.alloc_sbuf_tensor_at("o_lo", [P, NPAIR, TOK], F32R, offset=o_T_at, align_bytes=32)
    o_hi = nc.alloc_sbuf_tensor_at("o_hi", [P, NPAIR, TOK], F32R, offset=w_pair_at, align_bytes=32)
    wo_lo = nc.alloc_sbuf_tensor_at("wo_lo", [P, NPAIR, D], F32R, offset=ada_w_at + 4 * KD * ADW, align_bytes=32)
    wo_hi = nc.alloc_sbuf_tensor_at("wo_hi", [P, NPAIR, D // 2], F32R, offset=ada_w_at, align_bytes=32)
    h_lo = nc.alloc_sbuf_tensor_at("h_lo", [P, KD, TOK], F32R, offset=h_T_at, align_bytes=32)
    h_hi = nc.alloc_sbuf_tensor_at("h_hi", [P, KD, TOK], F32R, offset=ada_w_at + 4 * KD * (ADW + 3 * P), align_bytes=32)
    past_k = sb("past_k", [P, NS, P], c=phase_a)
    past_v = sb("past_v", [P, NS, P], c=phase_a)
    past_kT_at = next_place()
    past_kT = sb("past_kT", [P, NS, P], c=phase_a)
    q_z = sb("q_z", [P, 2, TOK], c=phase_a)
    k_T = sb("k_T", [P, TOK], c=phase_a)
    v_T_at = next_place()
    v_T = sb("v_T", [P, SEQ], c=phase_a)
    qkv_s = sb("qkv_s", [P, 3, P], c=phase_a)
    sb("sums_end", [P, P], c=phase_a)
    k_tok = sb("k_tok", [P, NT, P], c=phase_a)
    v_tok = sb("v_tok", [P, NT, P], c=phase_a)
    ntri_at = next_place()
    ntri = sb("ntri", [P, P], c=phase_a)
    ntri_r = nc.alloc_sbuf_tensor_at("ntri_r", [P, P], F32R, offset=ntri_at, align_bytes=32)
    nones_at = next_place()
    nones = sb("nones", [P, P], c=phase_a)
    nones_r = nc.alloc_sbuf_tensor_at("nones_r", [P, P], F32R, offset=nones_at, align_bytes=32)
    zeros = sb("zeros", [P, D // 2], c=phase_a)
    c_T = sb("c_T", [P, KD, CW], c=phase_a)
    ZC = 6 * 512
    ZH = ZC // 2
    ew_at = next_place()
    ew_t = sb("ew_t", [P, ZC], c=phase_a)
    ew_sp = sb("ew_sp", [P, ZC], c=phase_a)
    ew_w = sb("ew_w", [P, ZC], c=phase_a)
    sp_hi = nc.alloc_sbuf_tensor_at("sp_hi", [P, ZC], F32R, offset=ew_at, align_bytes=32)
    sp_lo = nc.alloc_sbuf_tensor_at("sp_lo", [P, ZC], F32R, offset=ew_at + 8 * ZC, align_bytes=32)
    rows_lo = nc.alloc_sbuf_tensor_at("rows_lo", [P, 6, ADW], F32R, offset=mod_rows_at, align_bytes=32)
    rows_hi = nc.alloc_sbuf_tensor_at("rows_hi", [P, 6, ADW], F32R, offset=ew_at, align_bytes=32)
    sp_sums = nc.alloc_sbuf_tensor_at("sp_sums", [P, 2, 4 * P], F32, offset=v_T_at, align_bytes=32)
    sums_lo = nc.alloc_sbuf_tensor_at("sums_lo", [P, 2, 4 * P], F32R, offset=v_T_at, align_bytes=32)
    sums_hi = nc.alloc_sbuf_tensor_at("sums_hi", [P, 2, 4 * P], F32R, offset=past_kT_at, align_bytes=32)
    ada_w3 = nc.alloc_sbuf_tensor_at("ada_w3", [P, KD, ADW], F32, offset=ew_at + 4 * (ZC + 2 * D), align_bytes=32)
    c_rows = mod_rows[:, 6:8, :].rearrange("p a n -> p (a n)")
    c_tmp = mod_rows[:, 4:6, :].rearrange("p a n -> p (a n)")
    in_rows = v_T[0:64, 0:P]
    xs = [ew_t[:, 0:1024], ew_t[:, 1024:2048], ew_t[:, 2048:3072], ew_sp[:, 0:1024], ew_sp[:, 1024:2048]]
    x_sq = o_T[:, :, :].rearrange("p k n -> p (k n)")[:, 0:D]
    w_o = ada_w[:, 1:3, :, :].rearrange("p a k n -> p (a k n)").rearrange("p (k n) -> p k n", n=D)

    phase_a.close()

    MAX_SLOTS = NE + 2 * TOK // P - 1
    exp_w = sb("exp_w", [P, 2, 3 * 4096])
    gate2 = sb("gate2", [P, 2, D])
    std2 = sb("std2", [P, NT])
    ones_b = sb("ones_b", [P, P], BF16)
    before_b = sb("before_b", [P, P], BF16)
    chosen_b = sb("chosen_b", [P, NT, NE], BF16)
    router_w = sb("router_w", [P, KD, CW])
    expert_sel = sb("expert_sel", [P, NE])
    logits_T = sb("logits_T", [P, P])
    router_b = sb("router_b", [P, NE])
    s_e = sb("s_e", [P, NT, NE])
    sel = sb("sel", [P, NT, NE])
    in_top = sb("in_top", [P, NT, NE])
    r_tmp = sb("r_tmp", [P, NT, NE])
    rows = sb("rows", [P, NT, NE])
    cmp4 = sb("cmp4", [P, NT * NGRP, EPG, EPG])
    g_score = sb("g_score", [P, NT, NGRP])
    g_rank = sb("g_rank", [P, NT, NGRP])
    tok1 = sb("tok1", [P, NT])
    row_f = sb("row_f", [P, NT, 2])
    row_i = sb("row_i", [P, NT, 2], I32)
    gates12 = sb("gates12", [P, NT, 2])
    slot_iota = sb("slot_iota", [P, MAX_SLOTS + 1], I32)
    iota_f = sb("iota_f", [P, MAX_SLOTS + 1])
    limits = sb("limits", [P, NT])
    count = sb("count", [P, NE])
    over = sb("over", [P, NE, NT])
    n_slots = sb("n_slots", [P, NE])
    ones_e = sb("ones_e", [P, NE])
    slot_end = sb("slot_end", [P, NE])
    base = sb("base", [P, NE])
    ended = sb("ended", [P, MAX_SLOTS + 1, NE])
    TAB_E, TAB_N = 0, MAX_SLOTS + 1
    TAB_F = TAB_N + 1
    TAB_G = TAB_F + MAX_SLOTS + 1
    TAB_W = TAB_G + MAX_SLOTS + 1
    TAB_L = TAB_W + MAX_SLOTS + 1
    TAB = TAB_L + 1
    slot_f = sb("slot_f", [P, TAB])
    slot_tab = sb("slot_tab", [P, TAB], I32)
    fetch_w = sb("fetch_w", [P, NE - 1])
    sq_tmp = sb("sq_tmp", [P, D])
    tmp = sb("tmp", [P, D])
    phase_r = ExitStack()
    h2_tok = sb("h2_tok", [P, NT, D], c=phase_r)
    gate1 = sb("gate1", [P, 2, D], c=phase_r)
    shift2 = sb("shift2", [P, 2, D], c=phase_r)
    scale2 = sb("scale2", [P, 2, D], c=phase_r)
    phase_r.close()
    x_slot = sb("x_slot", [P, D])
    x_slotT_hi = sb("x_slotT_hi", [P, KD, P], F32R)
    x_slotT_lo = sb("x_slotT_lo", [P, KD, P], F32R)
    sig = sb("sig", [P, FE])
    hid = sb("hid", [P, FE])
    hidT = sb("hidT", [P, KF, P])
    y_slot = sb("y_slot", [P, D])
    RING = 4
    UK = KD // RING
    w_lo = sb("w_lo", [P, RING, UK * FE], F32R)
    gate_diag = sb("gate_diag", [P, NT, 2, P])
    w_hi = nc.alloc_sbuf_tensor_at("w_hi", [P, RING, UK * FE], F32R, offset=h_T_at, align_bytes=32)
    y_rows = exp_w[:, 0, 0:NT * 2 * D].rearrange("p (t r n) -> p t r n", r=2, n=D)
    g_fin = exp_w[:, 1, 4096:4096 + D]
    g_ffn = tmp
    ZIN = -(-(MAX_SLOTS + 1) // (NPAIR - 1))
    ZOUT = -(-(MAX_SLOTS - NE - 1) // (NPAIR - 1))
    slots_in = nc.dram_tensor("slots_in", [ZIN * (NPAIR - 1) * P, D], F32, kind="Internal").ap()
    slots_out = nc.dram_tensor("slots_out", [(NE + 1 + ZOUT * (NPAIR - 1)) * P, D], F32, kind="Internal").ap()
    slots_in_z = slots_in.rearrange("(p n) (a c) -> p (n a) c", p=P, a=2)
    slots_out_z = slots_out[NE * P:, :].rearrange("(p n) (a c) -> p (n a) c", p=P, a=2)

    def zero_rows(n):
        return zeros[:, :].unsqueeze(1).to_broadcast([P, 2 * n, D // 2])

    z = ctx.enter_context(nc.psum_tensor("z", [P, ZC], F32))
    fill_ps = ctx.enter_context(nc.psum_tensor("fill_ps", [P, 2, 512], F32))

    def zb(b, a=0, e=512):
        return z[:, 512 * b + a:512 * b + e]

    def blocks_of(buf, first, step, n):
        lo = first - first % step
        return buf[:, lo:lo + step * n].rearrange("p (n c) -> p n c", c=step)[:, :, first % step:first % step + P]

    ada_v = io["ada_w"].rearrange("o (k p) n -> p (o k) n", p=P)
    qkv_v = io["sb_w_qkv"].rearrange("(k p) n -> p k n", p=P)
    ck_v = io["cache_sb_k"].rearrange("s k h d -> k s (h d)")
    cv_v = io["cache_sb_v"].rearrange("s k h d -> k s (h d)")
    wo_v = io["sb_w_o"].rearrange("(k p) n -> p k n", p=P)
    xp_v = io["x_prompt"].rearrange("b (t p) d -> p (b t) d", p=P)
    xs_v = io["x_sample"].rearrange("b s d -> (b s) d")
    kp_v = io["k_prompt"].rearrange("b (t p) h d -> p (b t) (h d)", p=P)
    vp_v = io["v_prompt"].rearrange("b (t p) h d -> p (b t) (h d)", p=P)
    ks_v = io["k_sample"].rearrange("b s h d -> (b s) (h d)")
    vs_v = io["v_sample"].rearrange("b s h d -> (b s) (h d)")
    yp_v = io["y_prompt"].rearrange("b (t p) d -> p (b t) d", p=P)
    ys_v = io["y_sample"].rearrange("b s d -> (b s) d")

    c_loaded = sem("c_loaded")
    x_loaded = sem("x_loaded")
    ada_loaded = [sem(f"ada_loaded{i}") for i in range(4)]
    wqkv_loaded = [sem(f"w{c}_loaded") for c in "qkv"]
    past_k_loaded = sem("past_k_loaded")
    past_v_loaded = sem("past_v_loaded")
    wo_loaded = sem("wo_loaded")
    kv_stored = sem("kv_stored")
    y_stored = sem("y_stored")
    consts_set = sem("consts_set")
    small_dve = sem("small_dve")
    silu_sig = sem("silu_sig")
    silu_ready = sem("silu_ready")
    setup_T = sem("setup_T")
    setup_T_used = sem("setup_T_used")
    sq_ready = sem("sq_ready")
    std_ready = sem("std_ready")
    rstd_ready = sem("rstd_ready")
    xs_ready = sem("xs_ready")
    xsT_ready = sem("xsT_ready")
    hT_ready = sem("hT_ready")
    h_hi_ready = sem("h_hi_ready")
    h_lo_ready = sem("h_lo_ready")
    wp_hi_ready = sem("wp_hi_ready")
    wp_lo_ready = sem("wp_lo_ready")
    modT_ready = sem("modT_ready")
    mod_T_mm = sem("mod_T_mm")
    ada_mm = sem("ada_mm")
    ada_kept = sem("ada_kept")
    z_ready = sem("z_ready")
    fill_ready = sem("fill_ready")
    fill_kept = sem("fill_kept")
    abs_ready = sem("abs_ready")
    exp_ready = sem("exp_ready")
    ln_ready = sem("ln_ready")
    sp_ready = sem("sp_ready")
    sp_masked = sem("sp_masked")
    sp_hi_ready = sem("sp_hi_ready")
    sp_lo_ready = sem("sp_lo_ready")
    sums_ready = sem("sums_ready")
    sums_hi_ready = sem("sums_hi_ready")
    sums_lo_ready = sem("sums_lo_ready")
    exact_ready = sem("exact_ready")
    sel_ready = sem("sel_ready")
    logw_ready = sem("logw_ready")
    w_ready = sem("w_ready")
    w_masked = sem("w_masked")
    o_ready = sem("o_ready")
    o_kept = sem("o_kept")
    rows_loaded = sem("rows_loaded")
    exp_loaded = [sem(f"{c}_loaded") for c in ("gate", "up", "down")]
    x_slot_loaded = sem("x_slot_loaded")
    y_slot_stored = sem("y_slot_stored")
    zeros_stored = sem("zeros_stored")
    consts_b = sem("consts_b")
    scattered = sem("scattered")
    gathered = [sem(f"gathered{t}") for t in range(NT)]
    bias_loaded = sem("bias_loaded")
    rows_mm = sem("rows_mm")
    rows_kept = sem("rows_kept")
    rows_kept_act = sem("rows_kept_act")
    rows_hi_ready = sem("rows_hi_ready")
    rows_lo_ready = sem("rows_lo_ready")
    o_hi_ready = sem("o_hi_ready")
    o_lo_ready = sem("o_lo_ready")
    wo_hi_ready = sem("wo_hi_ready")
    wo_lo_ready = sem("wo_lo_ready")
    wo_used = sem("wo_used")
    proj_ready = sem("proj_ready")
    proj_kept = sem("proj_kept")
    proj_added = sem("proj_added")
    std2_ready = sem("std2_ready")
    std3_ready = sem("std3_ready")
    h2_ready = sem("h2_ready")
    h2T_mm = sem("h2T_mm")
    h2T_kept = sem("h2T_kept")
    route_mm = sem("route_mm")
    route_kept = sem("route_kept")
    logits_ready = sem("logits_ready")
    sig_exp = sem("sig_exp")
    route_step = sem("route_step")
    chosen_ready = sem("chosen_ready")
    places_mm = sem("places_mm")
    rows_known = sem("rows_known")
    slots_known = sem("slots_known")
    hi_ready = sem("hi_ready")
    table_set = sem("table_set")
    lo_ready = sem("lo_ready")
    unit_used = sem("unit_used")
    x_hi_ready = sem("x_hi_ready")
    x_slotT_mm = sem("x_slotT_mm")
    x_slotT_kept = sem("x_slotT_kept")
    gate_sig = sem("gate_sig")
    sig_step = sem("sig_step")
    hid_ready = sem("hid_ready")
    hidT_mm = sem("hidT_mm")
    hidT_kept = sem("hidT_kept")
    down_ready = sem("down_ready")
    y_slot_kept = sem("y_slot_kept")
    first_gathered = sem("first_gathered")
    mixed = sem("mixed")
    mix_kept = sem("mix_kept")
    x2_ready = sem("x2_ready")
    x2_last_ready = sem("x2_last_ready")
    y_ready = sem("y_ready")

    def phase_b_sync(sp):
        sp.wait_ge(ada_kept, 4 + NPAIR)
        sp.dma_start(mod_rows[BIAS_ROW:BIAS_ROW + 1, :, :].rearrange("p a n -> p (a n)"),
                     io["ada_b"][0:1, 2 * D:6 * D]).then_inc(bias_loaded, 16)
        sp.wait_ge(o_ready, NPAIR)
        sp.wait_ge(kv_stored, 64 * NPAIR)
        sp.dma_start(g_ffn[:, :], io["norm_ffn_g"].to_broadcast([P, D])).then_inc(rows_loaded, 16)
        sp.wait_ge(consts_b, 12)
        sp.dma_start(router_w[:, :, 0:NE], io["router_w"].rearrange("(k p) e -> p k e", p=P)).then_inc(rows_loaded, 16)
        sp.dma_start(router_b[:, :], io["router_bias"].unsqueeze(0).to_broadcast([P, NE])).then_inc(rows_loaded, 16)
        sp.wait_ge(proj_ready, 2 * NT)
        sp.wait_ge(rows_mm, 8)
        for i in range(2):
            load_expert(sp, i, 0, 0, None)
        sp.wait_ge(scattered, 16 * 2 * NT)
        sp.dma_start(x_slot[:, :], slots_in[0:P, :]).then_inc(x_slot_loaded, 16)
        load_expert(sp, 2, 0, 0, None)
        for i in range(2):
            sp.wait_ge(exp_loaded[i], 16)
            load_expert(sp, i, 1, 1, None)
        sp.wait_ge(x_slotT_mm, 1)
        sp.dma_start(x_slot[:, :], slots_in[P:2 * P, :]).then_inc(x_slot_loaded, 16)
        sp.wait_ge(exp_loaded[2], 16)
        load_expert(sp, 2, 1, 1, None)
        sp.wait_ge(slots_known, 1)
        n = sp.value_load(slot_tab[0:1, TAB_N:TAB_N + 1], min_val=NE, max_val=MAX_SLOTS)
        with sp.Fori(0, n) as j:
            after = sp.value_load(slot_tab[0:1, bass.ds(j + TAB_F, 1)], min_val=2, max_val=NE)
            then = sp.value_load(slot_tab[0:1, bass.ds(j + TAB_F + 1, 1)], min_val=2, max_val=NE)
            fetch = sp.value_load(slot_tab[0:1, bass.ds(j + TAB_G, 1)], min_val=2, max_val=NE - 1)

            def fetch_over(i):
                sp.wait_ge(exp_loaded[i], 16 * (j + 2))
                sp.nop(nofuse=True)
                load_expert(sp, i, fetch, fetch % 2, then != after)

            sp.wait_ge(lo_ready, (2 * RING) * j + RING)
            fetch_over(0)
            sp.wait_ge(lo_ready, (2 * RING) * (j + 1))
            fetch_over(1)
            sp.wait_ge(x_slotT_mm, j + 2)
            sp.dma_start(x_slot[:, :], slots_in[bass.ds((j + 2) * P, P), :]).then_inc(x_slot_loaded, 16)
            sp.wait_ge(y_slot_kept, j + 2)
            sp.dma_start(slots_out[bass.ds(j * P, P), :], y_slot[:, :]).then_inc(y_slot_stored, 16)
            sp.wait_ge(down_ready, j + 2)
            fetch_over(2)
        sp.wait_ge(x_slot_loaded, 16 * (n + 2))
        for i in range(3):
            sp.wait_ge(exp_loaded[i], 16 * (n + 2))
        sp.nop(nofuse=True)
        sp.dma_start(g_fin, io["final_norm_g"].unsqueeze(0).to_broadcast([P, D])).then_inc(rows_loaded, 16)
        for t in range(NT):
            sp.wait_ge(y_ready, t + 1)
            dst = yp_v[:, t, :] if t < NTP else ys_v
            sp.dma_start(dst, y_rows[:, t, 0, :]).then_inc(y_stored, 16)
        sp.wait_ge(y_stored, 16 * NT)

    def load_expert(sp, i, e, b, cond):
        more = {} if cond is None else {"cond": cond}
        dst = exp_w[:, bass.ds(b, 1), i * 4096:(i + 1) * 4096].rearrange("p b (k f) -> p b k f", f=(FE, FE, D)[i])
        src = io[("exp_w_gate", "exp_w_up", "exp_w_down")[i]][0].rearrange("e (k p) f -> p e k f", p=P)
        sp.dma_start(dst, src[:, bass.ds(e, 1)], **more).then_inc(exp_loaded[i], 16)

    def raw_unit(b, u):
        return exp_w[:, bass.ds(b, 1), u * UK * FE:(u + 1) * UK * FE]

    def hi_unit(act, b, u):
        act.activation(w_hi[:, u % RING, :].unsqueeze(1), raw_unit(b, u), ACT.Copy).then_inc(hi_ready, 1)

    def lo_unit(dve, b, u):
        dve.tensor_tensor(w_lo[:, u % RING, :].unsqueeze(1), raw_unit(b, u), w_hi[:, u % RING, :].bitcast(F32).unsqueeze(1),
                          ALU.subtract).then_inc(lo_ready, 1)

    def slot_expert(eng, j):
        return eng.value_load(slot_tab[0:1, bass.ds(j, 1)], min_val=0, max_val=NE - 1)

    def slot_fetched(eng, j):
        return eng.value_load(slot_tab[0:1, bass.ds(j + TAB_W, 1)], min_val=16, max_val=16 * (MAX_SLOTS + 2))

    def phase_b_pool(pool):
        pool.wait_ge(o_ready, NPAIR)
        pool.memset(router_w[:, :, :], 0.0).then_inc(consts_b, 1)
        pool.memset(expert_sel[:, :], 0.0).then_inc(consts_b, 1)
        pool.memset(ones_b[:, :], 1.0).then_inc(consts_b, 1)
        pool.memset(before_b[:, :], 1.0).then_inc(consts_b, 1)
        pool.memset(ones_e[:, :], 1.0).then_inc(consts_b, 1)
        pool.memset(cmp4[:, :, :, :], 0.0).then_inc(consts_b, 1)
        pool.iota(slot_iota[:, :], pattern=[[1, MAX_SLOTS + 1]], base=0, channel_multiplier=0).then_inc(consts_b, 1)
        pool.wait_ge(consts_b, 7)
        pool.affine_select(out=before_b[:, :], in_=before_b[:, :], compare_op=ALU.is_gt, fill=0.0, base=0,
                           pattern=[[1, P]], channel_multiplier=-1).then_inc(consts_b, 1)
        for g in range(NG4):
            pool.wait_ge(consts_b, 8 + g)
            pool.affine_select(out=expert_sel[:, :], in_=expert_sel[:, :], compare_op=ALU.not_equal, fill=1.0,
                               base=-CW * g, pattern=[[-1, NE]], channel_multiplier=1).then_inc(consts_b, 1)
        pool.wait_ge(zeros_stored, 32 * (NPAIR - 1))
        pool.wait_ge(rows_known, 1)
        for t in range(NT):
            for r in range(2):
                pool.indirect_dma_start(out=slots_in[:, :], out_offset=bass.IndirectOffsetOnAxis(ap=row_i[:, t, r:r + 1], axis=0),
                                        in_=h2_tok[:, t, :], in_offset=None).then_inc(scattered, 16)
        pool.wait_ge(slots_known, 1)
        n = pool.value_load(slot_tab[0:1, TAB_N:TAB_N + 1], min_val=NE, max_val=MAX_SLOTS)
        before_last = pool.value_load(slot_tab[0:1, TAB_L:TAB], min_val=NE - 1, max_val=MAX_SLOTS - 1)
        for r, slots in ((0, before_last), (1, n)):
            pool.wait_ge(y_slot_stored, slots * 16 + 16)
            pool.nop(nofuse=True)
            for t in range(NT):
                pool.indirect_dma_start(out=y_rows[:, t, r, :], out_offset=None, in_=slots_out[:, :],
                                        in_offset=bass.IndirectOffsetOnAxis(ap=row_i[:, t, r:r + 1], axis=0)
                                        ).then_inc(gathered[t] if r else first_gathered, 16)
        for t in range(NT - 1):
            pool.wait_ge(mix_kept, t + 1)
            pool.tensor_tensor(x_tok[:, t, :], x_tok[:, t, :], y_rows[:, t, 0, :], ALU.add).then_inc(x2_ready, 1)

    def rms(act, src, dst, done, count):
        act.activation(sq_tmp[:, :], src, ACT.Square, accum_out=dst).then_inc(sq_ready, 1)
        act.wait_ge(sq_ready, count)
        act.activation(dst, dst, ACT.Sqrt, scale=1.0 / D, bias=eps1[:, 0:1]).then_inc(done, 1)

    def phase_b_act(act):
        for r, dst in ((1, gate1), (3, shift2)):
            act.wait_ge(rows_mm, r + 1)
            act.activation(dst[:, 1, :], pair_ps(r), ACT.Copy).then_inc(rows_kept_act, 1)
        for k in range(NPAIR):
            if k < NPAIR - 1:
                act.wait_ge(wo_used, k + 1)
            else:
                act.wait_ge(proj_ready, NT)
            act.activation(wo_hi[:, k, :], w_o[:, k, D // 2:D], ACT.Copy).then_inc(wo_hi_ready, 1)
        for t in range(NT + 3):
            if t < NT:
                act.wait_ge(proj_added, NT + t + 1)
                rms(act, x_tok[:, t, :], std2[:, t:t + 1], std2_ready, NT + t + 1)
            if t >= 3:
                u = t - 3
                act.wait_ge(route_mm, u + 1)
                if u:
                    act.wait_ge(logits_ready, u)
                act.activation(logits_T[:, :], fill_ps[:, 1, 0:P], ACT.Copy).then_inc(route_kept, 1)
        act.activation(zero_a[:, :], eps1[:, :], ACT.Exp).then_inc(table_set, 1)
        act.wait_ge(logits_ready, NT)
        act.activation(s_e[:, :, :], fill_ps[:, 0, 0:NT * NE].rearrange("p (t e) -> p t e", e=NE), ACT.Exp,
                       scale=-1.0).then_inc(sig_exp, 1)
        act.wait_ge(exp_loaded[0], 16)
        for u in range(RING):
            hi_unit(act, 0, u)
        act.wait_ge(slots_known, 1)
        n = act.value_load(slot_tab[0:1, TAB_N:TAB_N + 1], min_val=NE, max_val=MAX_SLOTS)
        act.wait_ge(table_set, 1)
        act.activation(zero_a[:, :], eps1[:, :], ACT.Sigmoid).then_inc(table_set, 1)
        act.wait_ge(table_set, 2)
        act.activation(zero_a[:, :], eps1[:, :], ACT.Copy).then_inc(y_slot_kept, 1)
        act.wait_ge(y_slot_kept, 1)
        with act.Fori(0, n) as j:
            act.wait_ge(table_set, j + 2)
            act.activation(zero_a[:, :], eps1[:, :], ACT.Sigmoid).then_inc(table_set, 1)
            b = slot_expert(act, j) % 2
            act.wait_ge(exp_loaded[1], slot_fetched(act, j))
            for u in range(RING):
                act.wait_ge(unit_used, (2 * RING) * j + u + 1)
                hi_unit(act, b, RING + u)
            act.wait_ge(unit_used, (2 * RING) * j + RING)
            act.activation(sig[:, :], zb(0), ACT.Sigmoid).then_inc(gate_sig, 1)
            b = slot_expert(act, j + 1) % 2
            act.wait_ge(exp_loaded[0], slot_fetched(act, j + 1))
            for u in range(RING):
                act.wait_ge(unit_used, (2 * RING) * j + RING + u + 1)
                hi_unit(act, b, u)
            act.wait_ge(down_ready, j + 2)
            act.wait_ge(y_slot_stored, 16 * (j + 1))
            act.activation(y_slot[:, :], z[:, 1024:2048], ACT.Copy).then_inc(y_slot_kept, 1)
        act.wait_ge(table_set, n + 2)
        act.activation(zero_a[:, :], eps1[:, :], ACT.Sqrt).then_inc(table_set, 1)
        for t in range(NT - 1):
            act.wait_ge(x2_ready, t + 1)
            rms(act, x_tok[:, t, :], std2[:, t:t + 1], std3_ready, 2 * NT + t + 1)
        act.wait_ge(x2_last_ready, 1)
        rms(act, x_tok[:, NT - 1, :], std2[:, NT - 1:NT], std3_ready, 3 * NT)

    def rest_of_wo(dve, c, k):
        cols = slice(c * D // 2, (c + 1) * D // 2)
        dve.wait_ge(wo_hi_ready, c * NPAIR + k + 1)
        dve.tensor_tensor(wo_lo[:, k, cols], w_o[:, k, cols], wo_hi[:, k, :].bitcast(F32),
                          ALU.subtract).then_inc(wo_lo_ready, 1)

    def keep_rows(dve, rs):
        for r in rs:
            kind, part = r // 2, r % 2
            dve.wait_ge(rows_mm, r + 1)
            if kind == 2:
                dve.wait_ge(rows_loaded, 48)
                dve.scalar_tensor_tensor(out=scale2[:, part, :], in0=pair_ps(r), scalar=1.0, in1=g_ffn[:, :],
                                         op0=ALU.add, op1=ALU.mult).then_inc(rows_kept, 1)
            else:
                dst = {0: gate1, 1: shift2, 3: gate2}[kind]
                dve.tensor_copy(dst[:, part, :], pair_ps(r)).then_inc(rows_kept, 1)

    def add_projected(dve, q):
        c, t = divmod(q, NT)
        cols = slice(c * D // 2, (c + 1) * D // 2)
        dve.wait_ge(proj_ready, q + 1)
        if q == 0:
            dve.wait_ge(rows_kept, 4)
            dve.wait_ge(rows_kept_act, 2)
        else:
            dve.wait_ge(proj_added, q)
        dve.tensor_tensor(tmp[:, cols], zb(q % 4), gate1[:, t // NTP, cols], ALU.mult).then_inc(proj_kept, 1)
        dve.wait_ge(proj_kept, q + 1)
        dve.tensor_tensor(x_tok[:, t, cols], x_tok[:, t, cols], tmp[:, cols], ALU.add).then_inc(proj_added, 1)

    def phase_b_dve(dve):
        n_step = [0]

        def step(ins):
            n_step[0] += 1
            ins.then_inc(route_step, 1)
            dve.wait_ge(route_step, n_step[0])

        dve.wait_ge(consts_b, 12)
        keep_rows(dve, (0, 2, 4, 5))
        for t in range(NT):
            if t == NT - 1:
                for k in range(NPAIR):
                    rest_of_wo(dve, 1, k)
            add_projected(dve, t)
        for t in range(NT + 2):
            if t < NT:
                add_projected(dve, NT + t)
            if 1 <= t <= NT:
                u = t - 1
                part = u // NTP
                dve.wait_ge(std2_ready, u + 1)
                step(dve.reciprocal(rstd[:, u:u + 1], std2[:, u:u + 1]))
                step(dve.scalar_tensor_tensor(out=h2_tok[:, u, :], in0=x_tok[:, u, :], scalar=rstd[:, u:u + 1],
                                              in1=scale2[:, part, :], op0=ALU.mult, op1=ALU.mult))
                dve.tensor_tensor(h2_tok[:, u, :], h2_tok[:, u, :], shift2[:, part, :], ALU.add).then_inc(h2_ready, 1)
            if t >= 2:
                u = t - 2
                dve.wait_ge(h2T_mm, u + 1)
                dve.tensor_copy(h_T[:, :, u * P:(u + 1) * P],
                                z[:, 2048:3072].rearrange("p (k c) -> p k c", c=P)).then_inc(h2T_kept, 1)
        dve.wait_ge(rows_loaded, 48)
        step(dve.tensor_copy(iota_f[:, :], slot_iota[:, :]))
        step(dve.tensor_scalar(limits[:, :], iota_f[:, 0:NT], float(P), None, ALU.mult))
        dve.wait_ge(sig_exp, 1)
        step(dve.tensor_scalar_add(s_e[:, :, :], s_e[:, :, :], 1.0))
        step(dve.reciprocal(s_e[:, :, :], s_e[:, :, :]))
        step(dve.tensor_tensor(sel[:, :, :], s_e[:, :, :], router_b[:, :].unsqueeze(1).to_broadcast([P, NT, NE]), ALU.add))

        def ranks(v, n, out):
            for j in range(EPG):
                for lo, hi, op in ((0, j, ALU.is_gt), (j + 1, EPG, ALU.is_ge)):
                    if hi > lo:
                        ins = dve.tensor_tensor(cmp4[:, 0:n, lo:hi, j], v[:, :, j:j + 1].to_broadcast([P, n, hi - lo]),
                                                v[:, :, lo:hi], op)
            step(ins)
            step(dve.tensor_reduce(out, cmp4[:, 0:n], AX_X, ALU.add))

        sel4 = sel[:, :, :].rearrange("p t (g i) -> p (t g) i", i=EPG)
        in_top4 = in_top[:, :, :].rearrange("p t (g i) -> p (t g) i", i=EPG)
        tmp4 = r_tmp[:, :, :].rearrange("p t (g i) -> p (t g) i", i=EPG)
        ranks(sel4, NT * NGRP, in_top4)
        step(dve.tensor_scalar(in_top[:, :, :], in_top[:, :, :], 2.0, None, ALU.is_lt))
        step(dve.tensor_tensor(r_tmp[:, :, :], sel[:, :, :], in_top[:, :, :], ALU.mult))
        step(dve.tensor_reduce(g_score[:, :, :].rearrange("p t g -> p (t g)"), tmp4, AX_X, ALU.add))
        ranks(g_score[:, :, :], NT, g_rank[:, :, :])
        step(dve.tensor_scalar(g_rank[:, :, :], g_rank[:, :, :], 1.0, None, ALU.is_lt))
        step(dve.tensor_tensor(in_top4, in_top4,
                               g_rank[:, :, :].rearrange("p t g -> p (t g)").unsqueeze(2).to_broadcast([P, NT * NGRP, EPG]),
                               ALU.mult))
        dve.tensor_copy(chosen_b[:, :, :], in_top[:, :, :]).then_inc(chosen_ready, 1)
        step(dve.tensor_tensor(s_e[:, :, :], s_e[:, :, :], in_top[:, :, :], ALU.mult))
        step(dve.tensor_reduce(tok1[:, :], s_e[:, :, :], AX_X, ALU.add))
        step(dve.reciprocal(tok1[:, :], tok1[:, :]))
        step(dve.tensor_tensor(s_e[:, :, :], s_e[:, :, :], tok1[:, :].unsqueeze(2).to_broadcast([P, NT, NE]), ALU.mult))
        dve.wait_ge(places_mm, 1)
        step(dve.tensor_copy(count[:, :], fill_ps[:, 1, NT * NE:(NT + 1) * NE]))
        step(dve.tensor_tensor(over[:, :, :], count[:, :].unsqueeze(2).to_broadcast([P, NE, NT]),
                               limits[:, :].unsqueeze(1).to_broadcast([P, NE, NT]), ALU.is_gt))
        step(dve.tensor_reduce(n_slots[:, :], over[:, :, :], AX_X, ALU.add))
        step(dve.tensor_scalar(n_slots[:, :], n_slots[:, :], 1.0, None, ALU.max))
        step(dve.tensor_tensor_scan(slot_end[:, :], ones_e[:, :], n_slots[:, :], 0.0, ALU.mult, ALU.add))
        step(dve.tensor_tensor(base[:, :], slot_end[:, :], n_slots[:, :], ALU.subtract))
        step(dve.tensor_scalar(base[:, :], base[:, :], float(P), None, ALU.mult))
        step(dve.tensor_tensor(rows[:, :, :], fill_ps[:, 1, 0:NT * NE].rearrange("p (t e) -> p t e", e=NE),
                               base[:, :].unsqueeze(1).to_broadcast([P, NT, NE]), ALU.add))
        step(dve.tensor_tensor(rows[:, :, :], rows[:, :, :], in_top[:, :, :], ALU.mult))
        step(dve.tensor_reduce(row_f[:, :, 1], rows[:, :, :], AX_X, ALU.max))
        step(dve.tensor_scalar(r_tmp[:, :, :], in_top[:, :, :], -8192.0, 8192.0, ALU.mult, ALU.add))
        step(dve.tensor_tensor(sel[:, :, :], rows[:, :, :], r_tmp[:, :, :], ALU.add))
        step(dve.tensor_reduce(row_f[:, :, 0], sel[:, :, :], AX_X, ALU.min))
        dve.tensor_copy(row_i[:, :, :], row_f[:, :, :]).then_inc(rows_known, 1)
        step(dve.memset(fetch_w[:, 0:1], 16.0))
        step(dve.tensor_tensor(ended[:, :, :], iota_f[:, :].unsqueeze(2).to_broadcast([P, MAX_SLOTS + 1, NE]),
                               slot_end[:, :].unsqueeze(1).to_broadcast([P, MAX_SLOTS + 1, NE]), ALU.is_ge))
        step(dve.tensor_reduce(slot_f[:, 0:MAX_SLOTS + 1], ended[:, :, :], AX_X, ALU.add))
        step(dve.tensor_scalar(slot_f[:, TAB_F:TAB_F + MAX_SLOTS + 1], slot_f[:, 0:MAX_SLOTS + 1], 2.0, float(NE),
                               ALU.add, ALU.min))
        step(dve.tensor_scalar(slot_f[:, TAB_G:TAB_G + MAX_SLOTS + 1], slot_f[:, TAB_F:TAB_F + MAX_SLOTS + 1],
                               float(NE - 1), None, ALU.min))
        step(dve.tensor_scalar(slot_f[:, 0:MAX_SLOTS + 1], slot_f[:, 0:MAX_SLOTS + 1], float(NE - 1), None, ALU.min))
        step(dve.tensor_copy(slot_f[:, TAB_N:TAB_N + 1], slot_end[:, NE - 1:NE]))
        step(dve.tensor_scalar(fetch_w[:, 1:NE - 1], n_slots[:, 0:NE - 2], 16.0, None, ALU.mult))
        step(dve.tensor_tensor(ended[:, :, 0:NE - 1], ended[:, :, 0:NE - 1],
                               fetch_w[:, :].unsqueeze(1).to_broadcast([P, MAX_SLOTS + 1, NE - 1]), ALU.mult))
        step(dve.tensor_copy(slot_f[:, TAB_L:TAB], slot_end[:, NE - 2:NE - 1]))
        step(dve.tensor_reduce(slot_f[:, TAB_W:TAB_L], ended[:, :, 0:NE - 1], AX_X, ALU.add))
        step(dve.tensor_scalar(slot_f[:, TAB_W:TAB_L], slot_f[:, TAB_W:TAB_L], 16.0, None, ALU.add))
        dve.tensor_copy(slot_tab[:, :], slot_f[:, :]).then_inc(slots_known, 1)
        for r, src in ((0, sel), (1, rows)):
            step(dve.tensor_tensor(r_tmp[:, :, :], src[:, :, :], row_f[:, :, r:r + 1].to_broadcast([P, NT, NE]), ALU.is_equal))
            step(dve.tensor_tensor(r_tmp[:, :, :], r_tmp[:, :, :], s_e[:, :, :], ALU.mult))
            step(dve.tensor_reduce(gates12[:, :, r], r_tmp[:, :, :], AX_X, ALU.add))

        dve.wait_ge(slots_known, 1)
        n = dve.value_load(slot_tab[0:1, TAB_N:TAB_N + 1], min_val=NE, max_val=MAX_SLOTS)

        def keep_slotT(j):
            dve.wait_ge(x_slotT_mm, j + 1)
            rows_T = z[:, 2048:3072].rearrange("p (k c) -> p k c", c=P)
            dve.tensor_copy(x_slotT_hi[:, :, :], rows_T).then_inc(x_hi_ready, 1)
            dve.wait_ge(x_hi_ready, j + 1)
            dve.tensor_tensor(x_slotT_lo[:, :, :], rows_T, x_slotT_hi[:, :, :].bitcast(F32),
                              ALU.subtract).then_inc(x_slotT_kept, 1)

        for t in range(NT):
            for r in range(2):
                step(dve.tensor_scalar(gate_diag[:, t, r, :], ident[:, :], gates12[:, t, r:r + 1], None, ALU.mult))
        keep_rows(dve, (6, 7))
        for u in range(RING):
            dve.wait_ge(hi_ready, u + 1)
            lo_unit(dve, 0, u)
        dve.wait_ge(scattered, 16 * 2 * NT)
        dve.tensor_copy(zero_f[:, :], eps1[:, :]).then_inc(hid_ready, 1)
        keep_slotT(0)
        with dve.Fori(0, n) as j:
            b = slot_expert(dve, j) % 2
            for u in range(RING):
                dve.wait_ge(hi_ready, (2 * RING) * j + RING + u + 1)
                lo_unit(dve, b, RING + u)
            dve.wait_ge(gate_sig, j + 1)
            dve.tensor_tensor(sig[:, :], sig[:, :], zb(0), ALU.mult).then_inc(sig_step, 1)
            dve.wait_ge(sig_step, j + 1)
            dve.wait_ge(unit_used, (2 * RING) * (j + 1))
            for a in range(2):
                cols = slice(a * FE // 2, (a + 1) * FE // 2)
                dve.tensor_tensor(hid[:, cols], sig[:, cols], zb(1)[:, cols], ALU.mult).then_inc(hid_ready, 1)
            for a in range(2):
                dve.wait_ge(hidT_mm, 2 * j + a + 1)
                dve.tensor_copy(hidT[:, 2 * a:2 * a + 2, :],
                                fill_ps[:, a, 0:2 * P].rearrange("p (k c) -> p k c", c=P)).then_inc(hidT_kept, 1)
            keep_slotT(j + 1)
            b = slot_expert(dve, j + 1) % 2
            for u in range(RING):
                dve.wait_ge(hi_ready, (2 * RING) * (j + 1) + u + 1)
                lo_unit(dve, b, u)

        dve.wait_ge(rows_loaded, 64)
        for t in range(NT + 2):
            if t < NT:
                dve.wait_ge(mixed, t + 1)
                dve.tensor_tensor(y_rows[:, t, 0, :], mix_ps(t), gate2[:, t // NTP, :], ALU.mult).then_inc(mix_kept, 1)
            if t == NT - 1:
                dve.wait_ge(mix_kept, NT)
                dve.tensor_tensor(x_tok[:, t, :], x_tok[:, t, :], y_rows[:, t, 0, :], ALU.add).then_inc(x2_last_ready, 1)
            if t >= 2:
                u = t - 2
                dve.wait_ge(std3_ready, u + 1)
                step(dve.reciprocal(rstd[:, u:u + 1], std2[:, u:u + 1]))
                dve.scalar_tensor_tensor(out=y_rows[:, u, 0, :], in0=x_tok[:, u, :], scalar=rstd[:, u:u + 1],
                                         in1=g_fin, op0=ALU.mult, op1=ALU.mult).then_inc(y_ready, 1)

    def pair_ps(r):
        b = 2 * (r % 3) if r < 6 else 2 * (7 - r)
        return z[:, 512 * b:512 * b + 1024]

    def mix_ps(t):
        if t == 3:
            return fill_ps[:, :, :].rearrange("p a n -> p (a n)")
        return z[:, 1024 * (t % 4):1024 * (t % 4) + 1024]

    def phase_b_pe(pe):
        def acc(out, lhsT, rhs, start=False, stop=False):
            return pe.matmul(out, lhsT, rhs, start=start, stop=stop, skip_group_check=True)

        def spread(r):
            kind, part = r // 2, r % 2
            for c in range(2):
                j, out = 2 * kind + c, pair_ps(r)[:, 512 * c:512 * c + 512]
                if kind < 3:
                    pe.wait_ge(rows_lo_ready, j + 1)
                    acc(out, sel_tok_r[:, part, :], rows_hi[:, j, :], start=True)
                    mm = acc(out, sel_tok_r[:, part, :], rows_lo[:, j, :], stop=True)
                else:
                    mm = acc(out, sel_tok_r[:, part, :].bitcast(F32), mod_rows[:, j, :], start=True, stop=True)
            mm.then_inc(rows_mm, 1)

        pe.wait_ge(ada_kept, 4 + NPAIR)
        pe.wait_ge(bias_loaded, 16)
        pe.wait_ge(o_kept, 1 + NPAIR)
        pe.wait_ge(sel_ready, 1)
        for r in range(6):
            if r == 4:
                pe.wait_ge(rows_kept_act, 1)
            elif r >= 3:
                pe.wait_ge(rows_kept, r // 2)
            spread(r)

        def project_out(q):
            c, t = divmod(q, NT)
            if q == 0:
                pe.wait_ge(rows_kept, 3)
                pe.wait_ge(rows_kept_act, 2)
                pe.wait_ge(o_lo_ready, NPAIR)
            elif q >= 4:
                pe.wait_ge(proj_kept, q - 3)
            toks = slice(t * P, (t + 1) * P)
            for k in range(NPAIR):
                if t == 0:
                    pe.wait_ge(wo_lo_ready, c * NPAIR + k + 1)
                acc(zb(q % 4), o_hi[:, k, toks], wo_hi[:, k, :], start=(k == 0))
                acc(zb(q % 4), o_hi[:, k, toks], wo_lo[:, k, 512 * c:512 * c + 512])
                mm = acc(zb(q % 4), o_lo[:, k, toks], wo_hi[:, k, :], stop=(k == NPAIR - 1))
                if q == NT - 1 and k < NPAIR - 1:
                    mm.then_inc(wo_used, 1)
            mm.then_inc(proj_ready, 1)

        def turn_h2(u):
            pe.wait_ge(h2_ready, u + 1)
            if u:
                pe.wait_ge(h2T_kept, u)
            else:
                pe.wait_ge(rows_kept, 4)
            for k in range(KD):
                mm = pe.transpose(z[:, 2048 + k * P:2048 + (k + 1) * P], h2_tok[:, u, k * P:(k + 1) * P], ident[:, :])
            mm.then_inc(h2T_mm, 1)

        def route(u):
            pe.wait_ge(h2T_kept, u + 1)
            if u:
                pe.wait_ge(route_kept, u)
            for k in range(KD):
                g = k % NG4
                mm = acc(fill_ps[CW * g:CW * g + CW, 1, 0:P], router_w[:, k, :],
                         h_T[:, k, u * P:(u + 1) * P], start=(k < NG4), stop=(k >= NG4))
            mm.then_inc(route_mm, 1)

        def sum_route(u):
            pe.wait_ge(route_kept, u + 1)
            acc(fill_ps[:, 0, NE * u:NE * (u + 1)], logits_T[:, :], expert_sel[:, :],
                start=(u == 0), stop=True).then_inc(logits_ready, 1)

        for q in range(NT):
            project_out(q)
        for t in range(NT + 4):
            if t < NT:
                project_out(NT + t)
            if t == NT:
                spread(6)
            if t == NT + 1:
                pe.wait_ge(proj_kept, 2 * NT)
                spread(7)
            if 2 <= t < NT + 2:
                turn_h2(t - 2)
            if 3 <= t < NT + 3:
                route(t - 3)
            if t >= 4:
                sum_route(t - 4)
        pe.wait_ge(chosen_ready, 1)
        for t in range(NT + 1):
            for u in range(min(t, NT - 1) + 1):
                mm = acc(fill_ps[:, 1, NE * t:NE * (t + 1)], before_b[:, :] if u == t else ones_b[:, :],
                         chosen_b[:, u, :], start=(t == 0), stop=(u == min(t, NT - 1)))
        mm.then_inc(places_mm, 1)

        def turn_slot(ks):
            for k in ks:
                mm = pe.transpose(z[:, 2048 + k * P:2048 + (k + 1) * P], x_slot[:, k * P:(k + 1) * P], ident[:, :])
            return mm

        pe.wait_ge(x_slot_loaded, 16)
        turn_slot(range(KD)).then_inc(x_slotT_mm, 1)
        pe.transpose(fill_ps[:, 0, 0:P], ident[:, :], ident[:, :]).then_inc(down_ready, 1)
        pe.wait_ge(slots_known, 1)
        n = pe.value_load(slot_tab[0:1, TAB_N:TAB_N + 1], min_val=NE, max_val=MAX_SLOTS)
        with pe.Fori(0, n) as j:
            b = slot_expert(pe, j) % 2
            fetched = slot_fetched(pe, j)
            pe.wait_ge(x_slotT_kept, j + 1)
            pe.wait_ge(hid_ready, 2 * j + 1)
            for i in range(2):
                for u in range(RING):
                    pe.wait_ge(lo_ready, (2 * RING) * j + i * RING + u + 1)
                    for k in range(UK * u, UK * (u + 1)):
                        cols = slice((k - UK * u) * FE, (k - UK * u + 1) * FE)
                        acc(zb(i), x_slotT_hi[:, k, :], w_hi[:, u, cols], start=(k == 0))
                        acc(zb(i), x_slotT_hi[:, k, :], w_lo[:, u, cols])
                        mm = acc(zb(i), x_slotT_lo[:, k, :], w_hi[:, u, cols], stop=(k == KD - 1))
                    mm.then_inc(unit_used, 1)
            pe.wait_ge(x_slot_loaded, 16 * (j + 2))
            turn_slot(range(KD // 2))
            for a in range(2):
                pe.wait_ge(hid_ready, 2 * j + a + 2)
                for k in range(2):
                    mm = pe.transpose(fill_ps[:, a, k * P:(k + 1) * P], hid[:, (2 * a + k) * P:(2 * a + k + 1) * P], ident[:, :])
                mm.then_inc(hidT_mm, 1)
                mm = turn_slot(range(4 + 2 * a, 6 + 2 * a))
            mm.then_inc(x_slotT_mm, 1)
            pe.wait_ge(exp_loaded[2], fetched)
            pe.wait_ge(y_slot_kept, j + 1)
            for c in range(2):
                for k in range(KF):
                    if c == 0 and k % 2 == 0:
                        pe.wait_ge(hidT_kept, 2 * j + k // 2 + 1)
                    mm = acc(zb(2 + c), hidT[:, k, :],
                             exp_w[:, bass.ds(b, 1), 8192 + k * D + c * 512:8192 + k * D + (c + 1) * 512],
                             start=(k == 0), stop=(k == KF - 1))
            mm.then_inc(down_ready, 1)
        pe.wait_ge(hid_ready, 2 * n + 1)
        pe.wait_ge(y_slot_kept, n + 1)
        pe.wait_ge(x_slotT_kept, n + 1)
        pe.wait_ge(first_gathered, 16 * NT)

        def mix(t, r):
            for c in range(2):
                cols = slice(512 * c, 512 * c + 512)
                mm = acc(mix_ps(t)[:, cols], gate_diag[:, t, r, :], y_rows[:, t, r, cols], start=(r == 0), stop=(r == 1))
            return mm

        for t in range(4):
            mix(t, 0)
        for t in range(NT):
            if t == 2:
                pe.wait_ge(mix_kept, 1)
                mix(4, 0)
            pe.wait_ge(gathered[t], 16)
            mix(t, 1).then_inc(mixed, 1)

    FILLS = 9

    block = ctx.enter_context(nc.Block())

    @block.sync
    def _(sp):
        sp.dma_start(c_rows[0:1, :], io["c_prompt"]).then_inc(c_loaded, 16)
        sp.dma_start(c_rows[1:NC, :], io["c_sample"]).then_inc(c_loaded, 16)
        sp.dma_start(in_rows[0:6 * KD, :], io["ada_b"].rearrange("o (k p) -> (o k) p", p=P)).then_inc(c_loaded, 16)
        sp.dma_start(in_rows[6 * KD:7 * KD, :], io["norm_mix_g"].rearrange("o (k p) -> (o k) p", p=P)).then_inc(c_loaded, 16)
        sp.dma_start(in_rows[7 * KD:8 * KD, :], io["norm_ffn_g"].rearrange("o (k p) -> (o k) p", p=P)).then_inc(c_loaded, 16)
        sp.dma_start(x_tok[:, 0:NTP, :], xp_v).then_inc(x_loaded, 16)
        sp.dma_start(x_tok[:, NTP, :], xs_v).then_inc(x_loaded, 16)
        for j in range(4):
            sp.dma_start(ada_w[:, j] if j < 3 else ada_w3[:, :, :], ada_v[:, :, j * ADW:(j + 1) * ADW]).then_inc(ada_loaded[j], 16)

        def load_pair(p, first):
            if not first:
                sp.wait_ge(fill_ready, (p - 1) * FILLS + 4)
            for c in range(3):
                sp.dma_start(w_pair[:, c], qkv_v[:, :, bass.ds(p * P + c * D, P)]).then_inc(wqkv_loaded[c], 16)
            if not first:
                sp.wait_ge(fill_ready, (p - 1) * FILLS + 6)
            sp.dma_start(past_k[:, :, :], ck_v[:, :, bass.ds(p * P, P)]).then_inc(past_k_loaded, 16)

        def store_pair(p):
            sp.wait_ge(fill_kept, (p + 1) * FILLS)
            c = bass.ds(p * P, P)
            sp.dma_start(kp_v[:, :, c], k_tok[:, 0:NTP, :]).then_inc(kv_stored, 16)
            sp.dma_start(vp_v[:, :, c], v_tok[:, 0:NTP, :]).then_inc(kv_stored, 16)
            sp.dma_start(ks_v[:, c], k_tok[:, NTP, :]).then_inc(kv_stored, 16)
            sp.dma_start(vs_v[:, c], v_tok[:, NTP, :]).then_inc(kv_stored, 16)

        load_pair(0, True)
        sp.dma_start(past_v[:, :, :], cv_v[:, :, 0:P]).then_inc(past_v_loaded, 16)
        sp.wait_ge(ada_mm, 1)
        sp.dma_start(ada_w[:, 0], ada_v[:, :, 4 * ADW:5 * ADW]).then_inc(ada_loaded[0], 16)
        sp.dma_start(slots_out_z[:, 0:2, :], zero_rows(1)).then_inc(y_slot_stored, 16)
        load_pair(1, False)

        def serve_pair(p, more):
            sp.dma_start(slots_in_z[:, bass.ds(p * 2 * ZIN, 2 * ZIN), :], zero_rows(ZIN)).then_inc(zeros_stored, 16)
            sp.dma_start(slots_out_z[:, bass.ds(p * 2 * ZOUT + 2, 2 * ZOUT), :], zero_rows(ZOUT)).then_inc(zeros_stored, 16)
            store_pair(p)
            if more:
                load_pair(p + 2, False)
            sp.wait_ge(o_ready, p + 1)
            sp.dma_start(past_v[:, :, :], cv_v[:, :, bass.ds((p + 1) * P, P)]).then_inc(past_v_loaded, 16)
            sp.wait_ge(ada_mm, p + 5)
            sp.dma_start(ada_w[:, 0], ada_v[:, :, bass.ds((p + 5) * ADW, ADW)]).then_inc(ada_loaded[0], 16)

        with sp.Fori(0, NPAIR - 2) as p:
            serve_pair(p, True)
        serve_pair(NPAIR - 2, False)
        sp.wait_ge(fill_ready, NPAIR * FILLS)
        sp.dma_start(w_o, wo_v).then_inc(wo_loaded, 16)
        store_pair(NPAIR - 1)
        phase_b_sync(sp)

    @block.gpsimd
    def _(pool):
        pool.memset(ident[:, :], 0.0).then_inc(consts_set, 1)
        pool.memset(sum_sel[:, :], 0.0).then_inc(consts_set, 1)
        pool.memset(sel_tok[:, :, :], 0.0).then_inc(consts_set, 1)
        pool.memset(ntri[:, :], -1.0).then_inc(consts_set, 1)
        pool.memset(nones[:, :], -1.0).then_inc(consts_set, 1)
        pool.memset(eps1[:, :], EPS).then_inc(consts_set, 1)
        pool.memset(zeros[:, :], 0.0).then_inc(consts_set, 1)
        pool.memset(q_z[:, :, :], 0.0).then_inc(consts_set, 1)
        pool.memset(c_T[:, :, :], 0.0).then_inc(consts_set, 1)
        pool.wait_ge(consts_set, 9)
        pool.affine_select(out=ident[:, :], in_=ident[:, :], compare_op=ALU.not_equal, fill=1.0, base=0,
                           pattern=[[-1, P]], channel_multiplier=1).then_inc(consts_set, 1)
        pool.affine_select(out=ntri[:, :], in_=ntri[:, :], compare_op=ALU.is_ge, fill=0.0, base=0,
                           pattern=[[-1, P]], channel_multiplier=1).then_inc(consts_set, 1)
        for g in range(NG4):
            pool.wait_ge(consts_set, 11 + 3 * g)
            pool.affine_select(out=sum_sel[:, :], in_=sum_sel[:, :], compare_op=ALU.not_equal, fill=1.0,
                               base=-CW * g, pattern=[[-1, NC]], channel_multiplier=1).then_inc(consts_set, 1)
            pool.affine_select(out=sel_tok[:, 0, :], in_=sel_tok[:, 0, :], compare_op=ALU.not_equal, fill=1.0,
                               base=-CW * g, pattern=[[0, P]], channel_multiplier=1).then_inc(consts_set, 1)
            pool.affine_select(out=sel_tok[:, 1, :], in_=sel_tok[:, 1, :], compare_op=ALU.not_equal, fill=1.0,
                               base=-CW * g - 1, pattern=[[-1, NS], [0, SS]],
                               channel_multiplier=1).then_inc(consts_set, 1)
        pool.wait_ge(consts_set, 11 + 3 * NG4)
        pool.affine_select(out=sel_tok[:, :, :], in_=sel_tok[:, :, :], compare_op=ALU.not_equal, fill=1.0,
                           base=-BIAS_ROW, pattern=[[0, 2], [0, P]], channel_multiplier=1).then_inc(consts_set, 1)

        def causal(buf, half):
            for first, step, n in (((0, 512, 3), (1408, 512, 1)), ((1536, 384, 2), (2048, 256, 2), (2560, 128, 2)))[half]:
                v = buf[:, first:first + P] if n == 1 else blocks_of(buf, first, step, n)
                last = pool.affine_select(out=v, in_=v, compare_op=ALU.is_gt, fill=0.0, base=0,
                                          pattern=[[0, n], [1, P]] if n > 1 else [[1, P]], channel_multiplier=-1)
            return last

        def mask(buf, ready, done, p):
            pool.wait_ge(ready, 2 * p + 1)
            pool.nop(nofuse=True)
            causal(buf, 0).then_inc(done, 1)
            pool.wait_ge(ready, 2 * p + 2)
            pool.nop(nofuse=True)
            causal(buf, 1).then_inc(done, 1)
            pool.wait_ge(done, 3 * p + 2)
            pool.nop(nofuse=True)
            v = buf[:, 2560:2816].rearrange("p (a s q) -> p a s q", a=2, s=NS)
            pool.affine_select(out=v, in_=v, compare_op=ALU.is_ge, fill=0.0, base=0,
                               pattern=[[0, 2], [-SS, NS], [0, SS]], channel_multiplier=1).then_inc(done, 1)

        with pool.Fori(0, NPAIR) as p:
            mask(ew_sp, sp_ready, sp_masked, p)
            mask(ew_w, w_ready, w_masked, p)
        phase_b_pool(pool)

    @block.scalar
    def _(act):
        act.wait_ge(c_loaded, 80)
        act.activation(c_tmp[0:NC, :], c_rows[0:NC, :], ACT.Sigmoid).then_inc(silu_sig, 1)
        act.wait_ge(x_loaded, 32)
        for t in range(NT):
            act.activation(x_sq, x_tok[:, t, :], ACT.Square, accum_out=rstd[:, t:t + 1]).then_inc(sq_ready, 1)
            act.wait_ge(sq_ready, t + 1)
        act.wait_ge(consts_set, 9)
        act.activation(rstd[:, :], rstd[:, :], ACT.Sqrt, scale=1.0 / D, bias=eps1[:, 0:1]).then_inc(std_ready, 1)
        for t in range(NT):
            act.wait_ge(rstd_ready, 1)
            act.activation(xs[t], x_tok[:, t, :], ACT.Copy, scale=rstd[:, t:t + 1]).then_inc(xs_ready, 1)

        def split_w(p, cs=range(3)):
            for c in cs:
                act.wait_ge(wqkv_loaded[c], 16 * (p + 1))
                act.activation(wp_hi[:, c], w_pair[:, c], ACT.Copy).then_inc(wp_hi_ready, 1)

        act.wait_ge(ada_mm, 3)
        split_w(0, [0])
        for k in range(KD):
            act.wait_ge(hT_ready, k + 1)
            act.activation(h_hi[:, k, 0:SEQ], h_T[:, k, 0:SEQ], ACT.Copy).then_inc(h_hi_ready, 1)
        split_w(0, [1, 2])
        act.wait_ge(hT_ready, KD + 2 * KD)
        act.activation(h_hi[:, :, SEQ:TOK], h_T[:, :, SEQ:TOK], ACT.Copy).then_inc(h_hi_ready, 1)
        split_w(1)

        def attend(p, split, last=False):
            halves = (slice(0, ZH), slice(ZH, ZC))
            for i, a in enumerate(halves):
                act.wait_ge(abs_ready, 2 * p + i + 1)
                act.activation(ew_t[:, a], ew_t[:, a], ACT.Exp, scale=-1.0).then_inc(exp_ready, 1)
            for i, a in enumerate(halves):
                act.wait_ge(exp_ready, 2 * p + i + 1)
                act.activation(ew_t[:, a], ew_t[:, a], ACT.Ln, bias=1.0).then_inc(ln_ready, 1)
            for i, a in enumerate(halves):
                act.wait_ge(sp_masked, 3 * p + (1, 3)[i])
                act.activation(sp_hi[:, a], ew_sp[:, a], ACT.Copy).then_inc(sp_hi_ready, 1)
            act.activation(sums_hi[:, :, 0:P], blocks_of(ew_sp, 2048, 256, 2), ACT.Copy).then_inc(sums_hi_ready, 1)
            act.wait_ge(sums_ready, 3 * p + 3)
            act.activation(sums_hi[:, :, P:4 * P], sp_sums[:, :, P:4 * P], ACT.Copy).then_inc(sums_hi_ready, 1)
            if last:
                act.wait_ge(fill_ready, NPAIR * FILLS)
                act.wait_ge(o_kept, NPAIR - 1)
                for k in range(NPAIR - 2):
                    act.activation(o_hi[:, k, :], o_T[:, k, :], ACT.Copy).then_inc(o_hi_ready, 1)
            act.wait_ge(logw_ready, p + 1)
            for a in halves:
                act.activation(ew_w[:, a], z[:, a], ACT.Exp).then_inc(w_ready, 1)
            if last:
                act.wait_ge(wo_loaded, 16)
                act.wait_ge(ada_mm, 4 + NPAIR)
                for k in range(NPAIR):
                    act.activation(wo_hi[:, k, :], w_o[:, k, 0:D // 2], ACT.Copy).then_inc(wo_hi_ready, 1)
                act.wait_ge(bias_loaded, 16)
                for j in range(6):
                    act.activation(rows_hi[:, j, :], mod_rows[:, j, :], ACT.Copy).then_inc(rows_hi_ready, 1)
            act.wait_ge(o_ready, p + 1)
            act.activation(o_T[:, bass.ds(p, 1), 0:SEQ], zb(0).unsqueeze(1), ACT.Copy)
            act.activation(o_T[:, bass.ds(p, 1), SEQ:TOK], zb(1, 0, P).unsqueeze(1), ACT.Copy).then_inc(o_kept, 1)
            if split:
                split_w(p + 2)
            if last:
                for k in (NPAIR - 2, NPAIR - 1):
                    act.wait_ge(o_kept, k + 2)
                    act.activation(o_hi[:, k, :], o_T[:, k, :], ACT.Copy).then_inc(o_hi_ready, 1)

        with act.Fori(0, NPAIR - 2) as p:
            attend(p, True)
        attend(NPAIR - 2, False)
        attend(NPAIR - 1, False, last=True)
        phase_b_act(act)

    @block.vector
    def _(dve):
        dve.wait_ge(silu_sig, 1)
        dve.tensor_tensor(c_rows[0:NC, :], c_rows[0:NC, :], c_tmp[0:NC, :], ALU.mult).then_inc(silu_ready, 1)
        dve.wait_ge(setup_T, 1)
        dve.wait_ge(consts_set, 9)
        dve.tensor_copy(c_T[:, :, 0:NC], fill_ps[:, 0, 0:KD * NC].rearrange("p (k c) -> p k c", c=NC)).then_inc(setup_T_used, 1)
        dve.tensor_copy(ada_bT[:, :], fill_ps[:, 0, 128:128 + 6 * KD]).then_inc(setup_T_used, 1)
        dve.tensor_copy(norm_gT[:, :], fill_ps[:, 0, 128 + 6 * KD:128 + 8 * KD]).then_inc(setup_T_used, 1)
        dve.wait_ge(consts_set, 11)
        dve.tensor_copy(ntri_r[:, :], ntri[:, :]).then_inc(exact_ready, 1)
        dve.tensor_copy(nones_r[:, :], nones[:, :]).then_inc(exact_ready, 1)
        dve.wait_ge(std_ready, 1)
        dve.reciprocal(rstd[:, :], rstd[:, :]).then_inc(rstd_ready, 1)
        for j in range(4):
            dve.wait_ge(ada_mm, j + 1)
            dve.tensor_copy(mod_rows[:, j, :], fill_ps[:, 1, :]).then_inc(ada_kept, 1)
        dve.wait_ge(mod_T_mm, 1)
        dve.tensor_tensor(mod_T[:, :, :], fill_ps[:, 0, 0:2 * KD * NC].rearrange("p (k c) -> p k c", c=NC),
                          ada_bT[:, 0:2 * KD].unsqueeze(2).to_broadcast([P, 2 * KD, NC]), ALU.add).then_inc(small_dve, 1)
        dve.wait_ge(small_dve, 1)
        dve.scalar_tensor_tensor(out=scale_T[:, :, :], in0=mod_T[:, KD:2 * KD, :], scalar=1.0,
                                 in1=norm_gT[:, 0:KD].unsqueeze(2).to_broadcast([P, KD, NC]),
                                 op0=ALU.add, op1=ALU.mult).then_inc(modT_ready, 1)
        dve.wait_ge(modT_ready, 1)

        def split_w(p, cs=range(3)):
            for c in cs:
                dve.wait_ge(wp_hi_ready, 3 * p + c + 1)
                dve.tensor_tensor(wp_lo[:, c], w_pair[:, c], wp_hi[:, c].bitcast(F32), ALU.subtract).then_inc(wp_lo_ready, 1)

        for k in range(KD + 1):
            if k < KD:
                dve.wait_ge(xsT_ready, k + 1)
                dve.tensor_scalar(h_T[:, k, 0:SEQ], zb(k % 6), scale_T[:, k, 0:1], mod_T[:, k, 0:1],
                                  ALU.mult, ALU.add).then_inc(hT_ready, 1)
            if k == 1:
                split_w(0, [0])
            if k >= 1:
                dve.wait_ge(h_hi_ready, k)
                dve.tensor_tensor(h_lo[:, k - 1, 0:SEQ], h_T[:, k - 1, 0:SEQ], h_hi[:, k - 1, 0:SEQ].bitcast(F32),
                                  ALU.subtract).then_inc(h_lo_ready, 1)
        split_w(0, [1, 2])
        def keep(p, f):
            dve.wait_ge(fill_ready, p * FILLS + f + 1)
            src = fill_ps[:, f % 2, :]
            blocks = src.rearrange("p (s k) -> p s k", k=P)
            if f == 0:
                dve.tensor_scalar(q_z[0:HD, 0, 0:SEQ], src[0:HD, :], SCALE, None, ALU.mult)
                ins = dve.tensor_scalar(q_z[HD:P, 1, 0:SEQ], src[HD:P, :], SCALE, None, ALU.mult)
            elif f == 1:
                ins = dve.tensor_copy(k_T[:, 0:SEQ], src)
            elif f == 2:
                ins = dve.tensor_copy(v_T[:, :], src)
            elif f == 3:
                ins = dve.tensor_copy(qkv_s[:, :, :], blocks[:, 0:3])
            elif f < 6:
                ins = dve.tensor_copy(past_kT[:, 4 * (f - 4):4 * (f - 4) + 4, :], blocks)
            elif f == 6:
                ins = dve.tensor_copy(k_tok[:, 0:NTP, :], blocks)
            elif f == 7:
                ins = dve.tensor_copy(v_tok[:, 0:NTP, :], blocks)
            elif f == 8:
                dve.tensor_copy(k_tok[:, NTP, :], qkv_s[:, 1, :])
                dve.tensor_copy(v_tok[:, NTP, :], qkv_s[:, 2, :])
                dve.tensor_scalar(q_z[0:HD, 0, SEQ:TOK], src[0:HD, 0:P], SCALE, None, ALU.mult)
                dve.tensor_scalar(q_z[HD:P, 1, SEQ:TOK], src[HD:P, 0:P], SCALE, None, ALU.mult)
                ins = dve.tensor_copy(k_T[:, SEQ:TOK], src[:, P:2 * P])
            ins.then_inc(fill_kept, 1)

        keep(0, 0)
        for a in range(2):
            ks = slice(4 * a, 4 * a + 4)
            hs = h_T[:, ks, SEQ:TOK]
            dve.wait_ge(xsT_ready, KD + 1 + a)
            for k in range(4 * a, 4 * a + 4):
                hv = h_T[:, k, SEQ:TOK].rearrange("p (s q) -> p s q", q=SS)
                src = zb(2 + a, 128 * (k % 4), 128 * (k % 4) + 128).rearrange("p (s q) -> p s q", q=SS)
                dve.tensor_tensor(hv, src, scale_T[:, k, 1:NC].unsqueeze(2).to_broadcast([P, NS, SS]),
                                  ALU.mult).then_inc(hT_ready, 1)
        for k in range(KD):
            hv = h_T[:, k, SEQ:TOK].rearrange("p (s q) -> p s q", q=SS)
            dve.wait_ge(hT_ready, KD + k + 1)
            dve.tensor_tensor(hv, hv, mod_T[:, k, 1:NC].unsqueeze(2).to_broadcast([P, NS, SS]),
                              ALU.add).then_inc(hT_ready, 1)

        dve.wait_ge(h_hi_ready, KD + 1)
        dve.tensor_tensor(h_lo[:, :, SEQ:TOK], h_T[:, :, SEQ:TOK], h_hi[:, :, SEQ:TOK].bitcast(F32),
                          ALU.subtract).then_inc(h_lo_ready, 1)

        def keep_slice(p):
            dve.wait_ge(ada_mm, p + 5)
            dve.tensor_copy(mod_rows[:, bass.ds(p, 1), :], fill_ps[:, 1, :].unsqueeze(1)).then_inc(ada_kept, 1)

        def rest_of_o(k):
            dve.wait_ge(o_hi_ready, k + 1)
            dve.tensor_tensor(o_lo[:, k, :], o_T[:, k, :], o_hi[:, k, :].bitcast(F32), ALU.subtract).then_inc(o_lo_ready, 1)

        last_q = sp_sums[:, :, P:2 * P]
        two_q = sp_sums[:, :, 2 * P:4 * P]

        def attend(p, more, split):
            halves = (slice(0, ZH), slice(ZH, ZC))
            for i, a in enumerate(halves):
                dve.wait_ge(z_ready, 2 * p + i + 1)
                dve.tensor_scalar(ew_t[:, a].bitcast(I32), z[:, a].bitcast(I32), 0x7FFFFFFF, None,
                                  ALU.bitwise_and).then_inc(abs_ready, 1)
            if more:
                keep(p + 1, 0)
            else:
                keep_slice(p)
            for i, a in enumerate(halves):
                dve.wait_ge(ln_ready, 2 * p + i + 1)
                dve.scalar_tensor_tensor(out=ew_sp[:, a], in0=z[:, a], scalar=0.0, in1=ew_t[:, a],
                                         op0=ALU.max, op1=ALU.add).then_inc(sp_ready, 1)
            if more:
                keep(p + 1, 1)
            dve.wait_ge(sp_hi_ready, 2 * p + 1)
            dve.tensor_tensor(sp_lo[:, halves[0]], ew_sp[:, halves[0]], sp_hi[:, halves[0]].bitcast(F32),
                              ALU.subtract).then_inc(sp_lo_ready, 1)
            dve.wait_ge(sp_masked, 3 * p + 3)
            dve.tensor_tensor(last_q, blocks_of(ew_sp, 2048 + P, 256, 2), blocks_of(ew_sp, 1408, 512, 2),
                              ALU.add).then_inc(sums_ready, 1)
            dve.tensor_tensor(two_q[:, :, 0:P], blocks_of(ew_sp, 1024 + P, 512, 2), blocks_of(ew_sp, 2048, 256, 2),
                              ALU.add).then_inc(sums_ready, 1)
            dve.wait_ge(sums_ready, 3 * p + 1)
            dve.tensor_tensor(two_q[:, :, P:2 * P], blocks_of(ew_sp, 1024 + 2 * P, 512, 2), last_q,
                              ALU.add).then_inc(sums_ready, 1)
            dve.wait_ge(sp_hi_ready, 2 * p + 2)
            dve.tensor_tensor(sp_lo[:, halves[1]], ew_sp[:, halves[1]], sp_hi[:, halves[1]].bitcast(F32),
                              ALU.subtract).then_inc(sp_lo_ready, 1)
            dve.wait_ge(sums_hi_ready, 2 * p + 1)
            dve.tensor_tensor(sums_lo[:, :, 0:P], blocks_of(ew_sp, 2048, 256, 2), sums_hi[:, :, 0:P].bitcast(F32),
                              ALU.subtract).then_inc(sums_lo_ready, 1)
            dve.wait_ge(sums_hi_ready, 2 * p + 2)
            dve.tensor_tensor(sums_lo[:, :, P:4 * P], sp_sums[:, :, P:4 * P], sums_hi[:, :, P:4 * P].bitcast(F32),
                              ALU.subtract).then_inc(sums_lo_ready, 1)
            if more:
                dve.wait_ge(logw_ready, p + 1)
                for f in range(2, 6):
                    keep(p + 1, f)
            if not more:
                for k in range(NPAIR - 2):
                    rest_of_o(k)
                for k in range(NPAIR):
                    rest_of_wo(dve, 0, k)
                for j in range(6):
                    dve.wait_ge(rows_hi_ready, j + 1)
                    dve.tensor_tensor(rows_lo[:, j, :], mod_rows[:, j, :], rows_hi[:, j, :].bitcast(F32),
                                      ALU.subtract).then_inc(rows_lo_ready, 1)
            if more:
                dve.wait_ge(kv_stored, 64 * (p + 1))
                dve.wait_ge(o_ready, p + 1)
                for f in range(6, 9):
                    keep(p + 1, f)
                keep_slice(p)
            else:
                for k in (NPAIR - 2, NPAIR - 1):
                    rest_of_o(k)
            if split:
                split_w(p + 2)

        for f in range(1, FILLS):
            keep(0, f)
        dve.tensor_copy(zero_f[:, :], eps1[:, :]).then_inc(o_kept, 1)
        split_w(1)
        dve.wait_ge(consts_set, 12 + 3 * NG4)
        dve.tensor_copy(sel_tok_r[:, :, :], sel_tok[:, :, :]).then_inc(sel_ready, 1)
        with dve.Fori(0, NPAIR - 2) as p:
            attend(p, True, True)
        attend(NPAIR - 2, True, False)
        attend(NPAIR - 1, False, False)
        phase_b_dve(dve)

    @block.tensor
    def _(pe):
        def ada_slice(src, out):
            for k in range(KD):
                g = k % NG4
                mm = pe.matmul(out[CW * g:CW * g + CW, :], c_T[:, k, :], src[:, k, :],
                               start=(k < NG4), stop=(k >= NG4), skip_group_check=True)
            return mm

        def transposes(srcs, out):
            for i, s in enumerate(srcs):
                mm = pe.transpose(out[:, i * P:(i + 1) * P], s, ident[:, :])
            return mm

        pe.wait_ge(consts_set, 12 + 3 * NG4)
        pe.wait_ge(c_loaded, 80)
        pe.wait_ge(silu_ready, 1)
        for k in range(KD):
            pe.transpose(fill_ps[:, 0, k * NC:(k + 1) * NC], c_rows[0:NC, k * P:(k + 1) * P], ident[0:NC, 0:NC])
        pe.transpose(fill_ps[:, 0, 128:128 + 64], in_rows, ident[0:64, 0:64]).then_inc(setup_T, 1)

        def slice_by_channel(j):
            pe.wait_ge(ada_kept, j + 1)
            for k in range(4 * j, 4 * j + 4):
                mm = pe.matmul(fill_ps[:, 0, k * NC:(k + 1) * NC], mod_rows[:, j, (k % 4) * P:(k % 4 + 1) * P],
                               sum_sel[:, :], start=(k == 0), stop=True, skip_group_check=True)
            return mm

        pe.wait_ge(setup_T_used, 3)
        for j in range(4):
            pe.wait_ge(ada_loaded[j], 16)
            if j >= 1:
                pe.wait_ge(ada_kept, j)
            ada_slice(ada_w[:, j] if j < 3 else ada_w3, fill_ps[:, 1, :]).then_inc(ada_mm, 1)
            if j >= 1:
                slice_by_channel(j - 1)
            if j in (1, 2):
                pe.wait_ge(xs_ready, NT)
                for k in range(3 * j - 3, 3 * j):
                    transposes([xs[t][:, k * P:(k + 1) * P] for t in range(NTP)], zb(k)).then_inc(xsT_ready, 1)
        slice_by_channel(3).then_inc(mod_T_mm, 1)
        for k in (6, 7):
            pe.wait_ge(hT_ready, k - 5)
            transposes([xs[t][:, k * P:(k + 1) * P] for t in range(NTP)], zb(k % 6)).then_inc(xsT_ready, 1)

        def project(p, f, first=False):
            out = fill_ps[:, f % 2, :]
            if f == 0 and not first:
                pe.wait_ge(fill_kept, p * FILLS)
            elif f == 1 and not first:
                pe.wait_ge(ada_kept, p + 3)
            elif f >= 2:
                pe.wait_ge(fill_kept, p * FILLS + f - 1)
            if f < 3:
                pe.wait_ge(wp_lo_ready, 3 * p + f + 1)
                for k in range(KD):
                    if first and f == 0:
                        pe.wait_ge(h_lo_ready, k + 1)
                    h = (h_hi[:, k, 0:SEQ], h_lo[:, k, 0:SEQ])
                    acc(out, wp_hi[:, f, k, :], h[0], start=(k == 0))
                    acc(out, wp_hi[:, f, k, :], h[1])
                    mm = acc(out, wp_lo[:, f, k, :], h[0], stop=(k == KD - 1))
            elif f == 3:
                if first:
                    pe.wait_ge(h_lo_ready, KD + 1)
                rows = out[:, 0:3 * P].rearrange("p (c n) -> p c n", n=P)
                for k in range(KD):
                    acc(rows, h_hi[:, k, SEQ:TOK], wp_hi[:, :, k, :], start=(k == 0))
                    acc(rows, h_hi[:, k, SEQ:TOK], wp_lo[:, :, k, :])
                    mm = acc(rows, h_lo[:, k, SEQ:TOK], wp_hi[:, :, k, :], stop=(k == KD - 1))
            elif f < 6:
                pe.wait_ge(past_k_loaded, 16 * (p + 1))
                mm = transposes([past_k[:, s, :] for s in range(4 * (f - 4), 4 * (f - 4) + 4)], out)
            elif f < 8:
                src = (k_T, v_T)[f - 6]
                mm = transposes([src[:, t * P:(t + 1) * P] for t in range(NTP)], out)
            else:
                mm = transposes([qkv_s[:, 0, :], qkv_s[:, 1, :]], out)
            mm.then_inc(fill_ready, 1)

        def acc(out, lhsT, rhs, start=False, stop=False):
            return pe.matmul(out, lhsT, rhs, start=start, stop=stop, skip_group_check=True)

        def scores(p):
            pe.wait_ge(fill_kept, (p + 1) * FILLS)
            pe.wait_ge(o_kept, p + 1)
            def late(h):
                acc(zb(2 + h, 0, 384), k_T[:, P:2 * P], q_z[:, h, P:SEQ], start=True)
                return acc(zb(2 + h, 384, 512), k_T[:, 3 * P:4 * P], q_z[:, h, 3 * P:SEQ])
            for h in range(2):
                acc(zb(h), k_T[:, 0:P], q_z[:, h, 0:SEQ], start=True)
            late(0).then_inc(z_ready, 1)
            late(1)
            acc(zb(4), k_T[:, 2 * P:3 * P], q_z[:, :, 2 * P:SEQ], start=True)
            acc(zb(5, 0, 256), k_T[:, SEQ:TOK], q_z[:, :, SEQ:TOK], start=True)
            past = zb(5, 256, 512).rearrange("p (h s q) -> p h s q", h=2, s=NS)
            for s in range(NS):
                mm = acc(past[:, :, s, :], past_kT[:, s, :], q_z[:, :, SEQ + SS * s:SEQ + SS * (s + 1)])
            mm.then_inc(z_ready, 1)

        def keep_sums(p):
            pe.wait_ge(exact_ready, 2)
            for b in range(6):
                if b % 3 == 0:
                    pe.wait_ge(sp_lo_ready, 2 * p + 1 + b // 3)
                acc(zb(b), ntri_r[:, :], sp_hi[:, 512 * b:512 * b + 512])
                acc(zb(b), ntri_r[:, :], sp_lo[:, 512 * b:512 * b + 512])
            for sp in (sp_hi, sp_lo):
                acc(blocks_of(z, 2048 + P, 256, 2), nones_r[:, :], blocks_of(sp, 1408, 512, 2))
                acc(zb(5, 256, 512), nones_r[:, :], sp[:, 2560:2816])
            for h in range(2):
                acc(zb(h, P, 2 * P), nones_r[:, :].bitcast(F32), ew_sp[:, 1024 + 512 * h:1024 + 512 * h + P])
            pe.wait_ge(sums_lo_ready, 2 * p + 2)
            for h in range(2):
                for sums in (sums_hi, sums_lo):
                    acc(zb(h, 2 * P, 4 * P), nones_r[:, :], sums[:, h, 2 * P:4 * P])
                    mm = acc(zb(2 + h, P, 3 * P), nones_r[:, :], sums[:, h, 0:2 * P], stop=(h == 1))
            mm.then_inc(logw_ready, 1)

        def values(p):
            pe.wait_ge(w_masked, 3 * p + 3)
            pe.wait_ge(past_v_loaded, 16 * (p + 1))
            for kb in range(NTP):
                for h in range(2):
                    src = (512 * h, 1024 + 512 * h, 2048 + 256 * h, 1408 + 512 * h)[kb]
                    n = SEQ - kb * P
                    acc(z[HD * h:HD * h + HD, kb * P:SEQ], v_tok[:, kb, HD * h:HD * h + HD],
                        ew_w[:, src:src + n], start=(kb == 0))
            for h in range(2):
                acc(z[HD * h:HD * h + HD, 512:640], v_tok[:, NTP, HD * h:HD * h + HD],
                    ew_w[:, 2560 + P * h:2688 + P * h], start=True)
            for s in range(NS):
                for h in range(2):
                    c = 2816 + P * h + SS * s
                    mm = acc(z[HD * h:HD * h + HD, 512 + SS * s:512 + SS * (s + 1)],
                             past_v[:, s, HD * h:HD * h + HD], ew_w[:, c:c + SS])
            mm.then_inc(o_ready, 1)

        def attend(p, more):
            def modulate():
                pe.wait_ge(ada_loaded[0], 16 * (p + 2))
                ada_slice(ada_w[:, 0], fill_ps[:, 1, :]).then_inc(ada_mm, 1)

            scores(p)
            if more:
                for f in range(3):
                    project(p + 1, f)
            else:
                pe.wait_ge(ada_kept, p + 4)
                modulate()
            keep_sums(p)
            if more:
                for f in range(3, 6):
                    project(p + 1, f)
            values(p)
            if more:
                for f in range(6, 9):
                    project(p + 1, f)
            if more:
                pe.wait_ge(fill_kept, (p + 1) * FILLS + 8)
                modulate()

        project(0, 0, first=True)
        for a in range(2):
            pe.wait_ge(hT_ready, 3 + a)
            transposes([xs[NTP][:, k * P:(k + 1) * P] for k in range(4 * a, 4 * a + 4)],
                       zb(2 + a)).then_inc(xsT_ready, 1)
        for f in range(1, FILLS):
            project(0, f, first=True)
        with pe.Fori(0, NPAIR - 1) as p:
            attend(p, True)
        attend(NPAIR - 1, False)
        phase_b_pe(pe)


_INS = ["x_prompt", "x_sample", "cache_sb_k", "cache_sb_v", "c_prompt", "c_sample", "ada_w", "ada_b",
        "norm_mix_g", "norm_ffn_g", "final_norm_g", "sb_w_qkv", "sb_w_o", "router_w", "router_bias",
        "exp_w_gate", "exp_w_up", "exp_w_down"]
_OUTS = {"y_prompt": (1, SEQ, D), "y_sample": (NS, SS, D), "k_prompt": (1, SEQ, H, HD), "v_prompt": (1, SEQ, H, HD),
         "k_sample": (NS, SS, H, HD), "v_sample": (NS, SS, H, HD)}


def kernel(**inputs):
    import numpy as _np
    import concourse.bacc as _bacc
    from concourse.bass_utils import run_bass_kernel_spmd as _run

    nc = _bacc.Bacc("TRN2", target_bir_lowering=False, num_devices=1)
    arrays, io = {}, {}
    for name in _INS:
        a = _np.ascontiguousarray(inputs[name])
        arrays[f"in_{name}"] = a
        io[name] = nc.dram_tensor(f"in_{name}", a.shape, mybir.dt.from_np(a.dtype), kind="ExternalInput").ap()
    for name, shape in _OUTS.items():
        io[name] = nc.dram_tensor(f"out_{name}", shape, F32, kind="ExternalOutput").ap()
    stream_step(nc, io)
    r = _run(nc, [arrays], core_ids=[0])
    got = tuple(r.results[0][f"out_{name}"] for name in _OUTS)
    return got + (None, None, None, None)
```
